# Optimizing a Trainium2 kernel written in Bass

```python
import jax, jax.numpy as jnp
from jax import lax
import numpy as np

D_MODEL = 2048
BATCH = 1
SEQ = 256
DEPTH = 2

RWKV_HEADS = 16
RWKV_HEAD_DIM = 64
RWKV_WIDTH = RWKV_HEADS * RWKV_HEAD_DIM
DECAY_LORA = 96
ICLR_LORA = 96
VRES_LORA = 64
GN_EPS = 64e-5
L2_EPS = 1e-12
SHIFT_WIDTH = 3 * RWKV_WIDTH + DECAY_LORA + ICLR_LORA

NSA_HEADS = 16
NSA_KV_GROUPS = 4
NSA_HEAD_DIM = 64
NSA_WIDTH = NSA_HEADS * NSA_HEAD_DIM
NSA_KV_WIDTH = NSA_KV_GROUPS * NSA_HEAD_DIM
CMP_LEN = 32
CMP_STRIDE = 16
CMP_HIDDEN = 256
SEL_LEN = 64
SEL_TOPK = 16
N_LOCAL_SEL = 2
WINDOW = 512
Q_BLOCK = 64
ROPE_THETA = 500000.0
ROT_DIM = NSA_HEAD_DIM // 4
FORCE_BONUS = 1e3
MASK_VALUE = -1e30
MAX_POS_OFFSET = 1024

NORM_EPS = 1e-6
IN_SPLITS = (SHIFT_WIDTH, RWKV_WIDTH, NSA_WIDTH, 6 * NSA_KV_WIDTH, 3 * NSA_HEADS, NSA_WIDTH, 2 * D_MODEL)
IN_WIDTH = SHIFT_WIDTH + RWKV_WIDTH + NSA_WIDTH + 6 * NSA_KV_WIDTH + 3 * NSA_HEADS + NSA_WIDTH + 2 * D_MODEL

kernel_name = 'hybrid_rwkv7_nsa_block'

def rms_norm(x, gain):
    xf = x.astype(jnp.float32)
    y = xf * lax.rsqrt(jnp.mean(xf * xf, axis=-1, keepdims=True) + NORM_EPS)
    return y * gain.astype(jnp.float32)

def partial_rotary(t, pos):
    half = ROT_DIM // 2
    inv_freq = ROPE_THETA ** (-jnp.arange(half, dtype=jnp.float32) * (2.0 / ROT_DIM))
    ang = pos.astype(jnp.float32)[..., None] * inv_freq
    ang = ang.reshape(pos.shape + (1,) * (t.ndim - pos.ndim - 1) + (half,))
    cos, sin = jnp.cos(ang), jnp.sin(ang)
    t1, t2 = t[..., :half], t[..., half:ROT_DIM]
    return jnp.concatenate([t1 * cos - t2 * sin, t1 * sin + t2 * cos, t[..., ROT_DIM:]], axis=-1)

def wkv7_scan(r, decay, k, v, kk, a):
    B, S, H, N = r.shape

    def step(state, inp):
        r_t, w_t, k_t, v_t, kk_t, a_t = inp
        s_kk = jnp.einsum('bhvk,bhk->bhv', state, kk_t)
        state = (state * w_t[:, :, None, :]
                 - s_kk[..., None] * (kk_t * a_t)[:, :, None, :]
                 + v_t[..., None] * k_t[:, :, None, :])
        return state, jnp.einsum('bhvk,bhk->bhv', state, r_t)

    xs = tuple(jnp.moveaxis(t, 1, 0) for t in (r, decay, k, v, kk, a))
    state0 = jnp.zeros((B, H, N, N), jnp.float32)
    _, y = lax.scan(step, state0, xs)
    return jnp.moveaxis(y, 0, 1)

def rwkv7_time_mix(u, mu, w0, w_up, a0, a_up, k_k, k_a, r_k, gn_w, gn_b, v_first, vres):
    f32 = jnp.float32
    u = u.astype(f32)
    B, S, _ = u.shape
    H, N, C = RWKV_HEADS, RWKV_HEAD_DIM, RWKV_WIDTH
    prev = jnp.pad(u[:, :-1], ((0, 0), (1, 0), (0, 0)))
    m = u + (prev - u) * mu
    r, k, v = m[..., :C], m[..., C:2 * C], m[..., 2 * C:3 * C]
    w_lo = m[..., 3 * C:3 * C + DECAY_LORA]
    a_lo = m[..., 3 * C + DECAY_LORA:]
    w = -jax.nn.softplus(-(w0 + jnp.tanh(w_lo) @ w_up)) - 0.5
    decay = jnp.exp(-jnp.exp(w))
    a = jax.nn.sigmoid(a0 + a_lo @ a_up)
    if vres is None:
        v_first = v
    else:
        v0, v_dn, v_upm = vres
        v = v + (v_first - v) * jax.nn.sigmoid(v0 + (v @ v_dn) @ v_upm)
    heads = lambda t: t.reshape(B, S, H, N)
    kk = heads(k * k_k)
    kk = kk / jnp.maximum(jnp.sqrt(jnp.sum(kk * kk, axis=-1, keepdims=True)), L2_EPS)
    k = k * (1.0 + (a - 1.0) * k_a)
    r, k, v, decay, a = heads(r), heads(k), heads(v), heads(decay), heads(a)
    y = wkv7_scan(r, decay, k, v, kk, a)
    mean = jnp.mean(y, axis=-1, keepdims=True)
    var = jnp.mean(jnp.square(y - mean), axis=-1, keepdims=True)
    y = ((y - mean) * lax.rsqrt(var + GN_EPS)).reshape(B, S, C) * gn_w + gn_b
    bonus = (jnp.sum(r * k * r_k, axis=-1, keepdims=True) * v).reshape(B, S, C)
    return y + bonus, v_first

def compress_blocks(t, pe, w1, w2):
    B, S, G, dh = t.shape
    n_cmp = (S - CMP_LEN) // CMP_STRIDE + 1
    c = t.reshape(B, S // CMP_STRIDE, CMP_STRIDE, G, dh)
    blocks = jnp.concatenate([c[:, m:m + n_cmp] for m in range(CMP_LEN // CMP_STRIDE)], axis=2)
    blocks = blocks + pe[None, None, :, None, :]
    flat = blocks.transpose(0, 1, 3, 2, 4).reshape(B, n_cmp, G, CMP_LEN * dh)
    return jax.nn.gelu(flat @ w1) @ w2

def nsa_attention(q, kv, gate_logits, positions, pe_k, pe_v, ck_w1, ck_w2, cv_w1, cv_w2):
    f32 = jnp.float32
    B, S, _ = q.shape
    G, HG, DH = NSA_KV_GROUPS, NSA_HEADS // NSA_KV_GROUPS, NSA_HEAD_DIM
    scale = DH ** -0.5
    n_cmp = (S - CMP_LEN) // CMP_STRIDE + 1
    n_sel = S // SEL_LEN
    sel_k = min(SEL_TOPK, n_sel)
    q = partial_rotary(q.astype(f32).reshape(B, S, G, HG, DH), positions)
    k_cmp, v_cmp, k_slc, v_slc, k_win, v_win = [t.astype(f32).reshape(B, S, G, DH) for t in jnp.split(kv, 6, axis=-1)]
    cmp_end = jnp.arange(n_cmp) * CMP_STRIDE + CMP_LEN - 1
    kc = partial_rotary(compress_blocks(k_cmp, pe_k, ck_w1, ck_w2), positions[:, cmp_end])
    vc = compress_blocks(v_cmp, pe_v, cv_w1, cv_w2)
    ksel = partial_rotary(k_slc, positions).reshape(B, n_sel, SEL_LEN, G, DH).transpose(0, 3, 1, 2, 4)
    vsel = v_slc.reshape(B, n_sel, SEL_LEN, G, DH).transpose(0, 3, 1, 2, 4)
    kwin = jnp.pad(partial_rotary(k_win, positions), ((0, 0), (WINDOW, 0), (0, 0), (0, 0)))
    vwin = jnp.pad(v_win, ((0, 0), (WINDOW, 0), (0, 0), (0, 0)))
    ci = jnp.arange(n_cmp)[:, None] * CMP_STRIDE
    sj = jnp.arange(n_sel)[None, :] * SEL_LEN
    overlap = ((ci < sj + SEL_LEN) & (ci + CMP_LEN > sj)).astype(f32)
    blk = jnp.arange(n_sel)
    bi = jnp.arange(B)[:, None, None, None]
    gi = jnp.arange(G)[None, :, None, None]

    def block_fn(c):
        t0 = c * Q_BLOCK
        qb = lax.dynamic_slice_in_dim(q, t0, Q_BLOCK, axis=1)
        tq = t0 + jnp.arange(Q_BLOCK)
        cmp_ok = cmp_end[None, :] <= tq[:, None]
        s_cmp = jnp.einsum('bqghd,bngd->bghqn', qb, kc) * scale
        p_cmp = jax.nn.softmax(jnp.where(cmp_ok, s_cmp, MASK_VALUE), axis=-1) * cmp_ok
        o_cmp = jnp.einsum('bghqn,bngd->bqghd', p_cmp, vc)
        imp = jnp.einsum('bghqn,nj->bgqj', p_cmp, overlap)
        cur = tq // SEL_LEN
        dist = cur[:, None] - blk[None, :]
        forced = (blk[None, :] == 0) | ((dist >= 0) & (dist < N_LOCAL_SEL))
        causal_blk = blk[None, :] * SEL_LEN <= tq[:, None]
        imp = jnp.where(causal_blk, imp + jnp.where(forced, FORCE_BONUS, 0.0), MASK_VALUE)
        _, idx = lax.top_k(imp, sel_k)
        ks = ksel[bi, gi, idx]
        vs = vsel[bi, gi, idx]
        kpos = idx[..., None] * SEL_LEN + jnp.arange(SEL_LEN)
        sel_ok = kpos <= tq[None, None, :, None, None]
        s_slc = jnp.einsum('bqghd,bgqksd->bghqks', qb, ks) * scale
        s_slc = jnp.where(sel_ok[:, :, None], s_slc, MASK_VALUE)
        p_slc = jax.nn.softmax(s_slc.reshape(B, G, HG, Q_BLOCK, sel_k * SEL_LEN), axis=-1)
        o_slc = jnp.einsum('bghqks,bgqksd->bqghd', p_slc.reshape(s_slc.shape), vs)
        kw = lax.dynamic_slice_in_dim(kwin, t0, Q_BLOCK + WINDOW, axis=1)
        vw = lax.dynamic_slice_in_dim(vwin, t0, Q_BLOCK + WINDOW, axis=1)
        kwpos = t0 - WINDOW + jnp.arange(Q_BLOCK + WINDOW)
        diff = tq[:, None] - kwpos[None, :]
        win_ok = (diff >= 0) & (diff < WINDOW) & (kwpos[None, :] >= 0)
        s_win = jnp.einsum('bqghd,bkgd->bghqk', qb, kw) * scale
        p_win = jax.nn.softmax(jnp.where(win_ok, s_win, MASK_VALUE), axis=-1)
        o_win = jnp.einsum('bghqk,bkgd->bqghd', p_win, vw)
        return o_cmp, o_slc, o_win

    o_cmp, o_slc, o_win = lax.map(block_fn, jnp.arange(S // Q_BLOCK))
    unblock = lambda o: jnp.moveaxis(o, 0, 1).reshape(B, S, NSA_HEADS, DH)
    g = jax.nn.sigmoid(gate_logits.astype(f32)).reshape(B, S, 3, NSA_HEADS, 1)
    o = g[:, :, 0] * unblock(o_cmp) + g[:, :, 1] * unblock(o_slc) + g[:, :, 2] * unblock(o_win)
    return o.reshape(B, S, NSA_WIDTH)

def setup_inputs(seed: int = 0) -> dict:
    key = jax.random.key(seed)
    ks = jax.random.split(key, 32)
    L = DEPTH
    f32 = jnp.float32

    def nrm(k, shape, scale):
        return scale * jax.random.normal(k, shape, f32)

    x = jax.random.normal(ks[0], (BATCH, SEQ, D_MODEL), f32)
    positions = (jnp.arange(SEQ, dtype=jnp.int32)[None, :]
                 + jax.random.randint(ks[1], (BATCH, 1), 0, MAX_POS_OFFSET, dtype=jnp.int32))
    return {
        'x': x,
        'positions': positions,
        'norm_pre': 1.0 + nrm(ks[2], (L, D_MODEL), 0.05),
        'norm_post': 1.0 + nrm(ks[3], (L, D_MODEL), 0.05),
        'w_in': nrm(ks[4], (L, D_MODEL, IN_WIDTH), D_MODEL ** -0.5),
        'rwkv_mu': jax.random.uniform(ks[5], (L, SHIFT_WIDTH), f32),
        'rwkv_w0': jax.random.uniform(ks[6], (L, RWKV_WIDTH), f32, -6.5, -1.5),
        'rwkv_w_up': nrm(ks[7], (L, DECAY_LORA, RWKV_WIDTH), 0.1 * DECAY_LORA ** -0.5),
        'rwkv_a0': nrm(ks[8], (L, RWKV_WIDTH), 0.1),
        'rwkv_a_up': nrm(ks[9], (L, ICLR_LORA, RWKV_WIDTH), ICLR_LORA ** -0.5),
        'rwkv_k_k': 0.85 + nrm(ks[10], (L, RWKV_WIDTH), 0.05),
        'rwkv_k_a': 1.0 + nrm(ks[11], (L, RWKV_WIDTH), 0.05),
        'rwkv_r_k': nrm(ks[12], (L, RWKV_HEADS, RWKV_HEAD_DIM), 0.1),
        'rwkv_gn_w': 1.0 + nrm(ks[13], (L, RWKV_WIDTH), 0.05),
        'rwkv_gn_b': nrm(ks[14], (L, RWKV_WIDTH), 0.02),
        'rwkv_v0': 1.0 + nrm(ks[15], (L - 1, RWKV_WIDTH), 0.1),
        'rwkv_v_down': nrm(ks[16], (L - 1, RWKV_WIDTH, VRES_LORA), RWKV_WIDTH ** -0.5),
        'rwkv_v_up': nrm(ks[17], (L - 1, VRES_LORA, RWKV_WIDTH), VRES_LORA ** -0.5),
        'nsa_pe_k': nrm(ks[18], (L, CMP_LEN, NSA_HEAD_DIM), 0.1),
        'nsa_pe_v': nrm(ks[19], (L, CMP_LEN, NSA_HEAD_DIM), 0.1),
        'nsa_ck_w1': nrm(ks[20], (L, CMP_LEN * NSA_HEAD_DIM, CMP_HIDDEN), (CMP_LEN * NSA_HEAD_DIM) ** -0.5),
        'nsa_ck_w2': nrm(ks[21], (L, CMP_HIDDEN, NSA_HEAD_DIM), CMP_HIDDEN ** -0.5),
        'nsa_cv_w1': nrm(ks[22], (L, CMP_LEN * NSA_HEAD_DIM, CMP_HIDDEN), (CMP_LEN * NSA_HEAD_DIM) ** -0.5),
        'nsa_cv_w2': nrm(ks[23], (L, CMP_HIDDEN, NSA_HEAD_DIM), CMP_HIDDEN ** -0.5),
        'w_proj_a': nrm(ks[24], (L, RWKV_WIDTH, D_MODEL), RWKV_WIDTH ** -0.5),
        'w_proj_b': nrm(ks[25], (L, NSA_WIDTH, D_MODEL), NSA_WIDTH ** -0.5),
        'w_out': nrm(ks[26], (L, D_MODEL, D_MODEL), D_MODEL ** -0.5),
    }

def reference(x, positions, norm_pre, norm_post, w_in, rwkv_mu, rwkv_w0, rwkv_w_up, rwkv_a0, rwkv_a_up,
              rwkv_k_k, rwkv_k_a, rwkv_r_k, rwkv_gn_w, rwkv_gn_b, rwkv_v0, rwkv_v_down, rwkv_v_up,
              nsa_pe_k, nsa_pe_v, nsa_ck_w1, nsa_ck_w2, nsa_cv_w1, nsa_cv_w2, w_proj_a, w_proj_b, w_out):
    f32 = jnp.float32
    split_points = np.cumsum(IN_SPLITS)[:-1].tolist()
    v_first = None
    for l in range(DEPTH):
        h = rms_norm(x, norm_pre[l]).astype(x.dtype)
        proj = h @ w_in[l]
        u_shift, z_a, q, kv, nsa_gate, z_b, merge_gate = jnp.split(proj, split_points, axis=-1)
        vres = None if l == 0 else (rwkv_v0[l - 1], rwkv_v_down[l - 1], rwkv_v_up[l - 1])
        y_a, v_first = rwkv7_time_mix(u_shift, rwkv_mu[l], rwkv_w0[l], rwkv_w_up[l], rwkv_a0[l], rwkv_a_up[l],
                                      rwkv_k_k[l], rwkv_k_a[l], rwkv_r_k[l], rwkv_gn_w[l], rwkv_gn_b[l],
                                      v_first, vres)
        y_b = nsa_attention(q, kv, nsa_gate, positions, nsa_pe_k[l], nsa_pe_v[l],
                            nsa_ck_w1[l], nsa_ck_w2[l], nsa_cv_w1[l], nsa_cv_w2[l])
        y_a = y_a * jax.nn.silu(z_a.astype(f32))
        y_b = y_b * jax.nn.silu(z_b.astype(f32))
        g_a, g_b = jnp.split(jax.nn.sigmoid(merge_gate.astype(f32)), 2, axis=-1)
        merged = g_a * (y_a @ w_proj_a[l]) + g_b * (y_b @ w_proj_b[l])
        out = merged @ w_out[l]
        x = x + rms_norm(out, norm_post[l]).astype(x.dtype)
    return x


_drawn_inputs = setup_inputs


def setup_inputs(seed=0):
    import zlib

    import numpy as np

    out = dict(_drawn_inputs(seed))
    spreads = {}
    factors = {'rwkv_w_up': 8.0, 'rwkv_v0': 76.128, 'nsa_pe_k': 8.0, 'rwkv_v_down': 8.0, 'rwkv_v_up': 8.0}
    for name, (base, spread) in spreads.items():
        noise = np.random.default_rng([zlib.crc32(name.encode()), seed]).standard_normal(out[name].shape)
        drawn = base * np.exp(spread * noise) if base else spread * noise
        out[name] = __import__('jax').numpy.asarray(drawn.astype(out[name].dtype))
    for name, factor in factors.items():
        out[name] = (out[name] * factor).astype(out[name].dtype)
    return out
```

```python
from contextlib import ExitStack

import numpy as np
import concourse.bass as bass
from concourse import mybir

F32 = mybir.dt.float32
I32 = mybir.dt.int32
ALU = mybir.AluOpType
ACT = mybir.ActivationFunctionType
AX = mybir.AxisListType

P = 128
LAYERS, D, S = 2, 2048, 256
KC = D // P
RW = 1024
HP = RW // P
HEADS = 16
HD = 64
CH = 64
NCH = S // CH
LORA_W = 96
LORA_V = 64
CMP = 32
CSTR = 16
NCMP = (S - CMP) // CSTR + 1
NG = 4
NCG = NCMP * NG
SCALE = HD ** -0.5
DECAY = float(np.exp(-0.5))
GN_EPS, L2_EPS, NORM_EPS = 64e-5, 1e-12, 1e-6

B_LOG, B_KC, B_VC, B_KS, B_KW, B_VT, B_Q, B_CK, B_CV = 0, 1, 2, 3, 4, 5, 7, 11, 12
B_ZB, B_K, B_V, B_R, B_ZA, B_MGB, B_PB, B_A, B_WO = 13, 17, 21, 25, 29, 33, 41, 45, 57
NB = 65
BLK = 4096
SLOTS = 2
USES = [len(range(s, NB, SLOTS)) for s in range(SLOTS)]
U_LO, U_GATE, U_KC, U_VC, U_KS, U_KW, U_VT, U_Q, U_ZB = 0, 1, 2, 3, 4, 5, 6, 8, 12
U_K, U_ZA, U_MGB, U_PB, U_A, U_WO, UNITS = 16, 28, 32, 40, 48, 64, 72

PAR = {}
_at = 0
for _n, _w in (("w_up", RW), ("a_up", RW), ("v_up", RW), ("v_down", HP * LORA_V), ("w2k", 128), ("w2v", 128),
               ("mu", 26), ("w0", 8), ("a0", 8), ("v0", 8), ("k_k", 8), ("k_a", 8), ("r_k", 8), ("gn_w", 8),
               ("gn_b", 8), ("norm_pre", 16), ("pe_k", 16), ("pe_v", 16), ("first", 1)):
    PAR[_n] = (_at, _at + _w)
    _at += _w
NPAR = _at
CON = {}
_at = 0
for _n, _w in (("ident", 128), ("q_blk", 128), ("qt_blk", 128), ("qt_32", 128), ("qt_64", 128), ("incl", 128),
               ("strict_x", 128), ("incl_x", 128), ("ones", 128), ("ident2", 64), ("rot", 128), ("dup", 4 * 128),
               ("caus0", 128), ("caus1", 256), ("cmpmask", 30), ("rowok", 1), ("invf", 1), ("inchunk", 256)):
    CON[_n] = (_at, _at + _w)
    _at += _w
NCON = _at

RW_STEPS = 27
PRE_STEPS = 2


def rw_at(p, k):
    return PRE_STEPS + p * RW_STEPS + k + 1


def lora_at(p):
    return 1 if p == 0 else rw_at(p - 1, 9)


def norms_at(p):
    return 2 if p == 0 else rw_at(p - 1, 11)


class Signal:

    def __init__(self, sem, per_layer, ahead=0):
        self.sem, self.per_layer, self.ahead = sem, per_layer, ahead

    def at(self, l, n):
        return l * self.per_layer + (n + self.ahead)


class Chain:

    def __init__(self, eng, sem):
        self.eng, self.sem, self.n = eng, sem, 0

    def step(self, ins):
        self.n += 1
        ins.then_inc(self.sem, 1)
        return ins

    def settle(self):
        self.eng.wait_ge(self.sem, self.n)

    def restart(self):
        self.settle()
        self.eng.sem_clear(self.sem)
        self.n = 0


def build(nc, x, pos, stream, params, consts, norm_post, out):
    ctx = ExitStack()
    with ctx:
        def sb(name, cols, dt=F32):
            return ctx.enter_context(nc.sbuf_tensor(name, [P, cols], dt))

        def sem(name):
            return ctx.enter_context(nc.semaphore(name))

        def signal(name, per_layer, ahead=0):
            return Signal(sem(name), per_layer, ahead)

        hT_t = sb("hT", KC * S)
        hT = hT_t[:, :].rearrange("p (c n) -> p c n", c=KC)
        OUT = hT_t[:, :].rearrange("p (t n) -> p t n", t=2)
        slots = [sb(f"weights{s}", BLK) for s in range(SLOTS)]
        ZA = sb("za", HP * S)[:, :].rearrange("p (t n) -> p t n", t=HP)
        ZB = sb("zb", HP * S)[:, :].rearrange("p (t n) -> p t n", t=HP)
        MB = sb("merged", KC * S)[:, :].rearrange("p (t n) -> p t n", t=KC)
        KVR = [sb(n, HP * S)[:, :].rearrange("p (t n) -> p t n", t=HP) for n in ("rk", "rv", "rr")]
        K, V, R = KVR
        VF = sb("v_first", HP * S)[:, :].rearrange("p (t n) -> p t n", t=HP)
        par = sb("par", NPAR)
        con = sb("con", NCON)
        cs = sb("cos_sin", 2 * S)
        derived = sb("derived", 26 + 24)
        w2kd = sb("w2kd", 256)
        gates = sb("gates", HEADS * 6)[:, :].rearrange("p (h i) -> p h i", i=6)
        VC = sb("v_cmp", NG * HD)[:, :].rearrange("p (g d) -> p g d", g=NG)
        PC = sb("p_cmp", 2 * 2 * P)[:, :].rearrange("p (b q k) -> p b q k", b=2, q=2)
        LO = sb("lora_in", 2 * S)
        small = sb("small", 64)
        halves = sb("halves", 4)
        half8 = sb("half8", 8)
        VD = sb("v_down_out", S)
        ZT = sb("z_tanh", 512)
        WORK = sb("work", 14464)

        def pv(name, a=0, b=None):
            lo, hi = PAR[name]
            return par[:, lo + a:(hi if b is None else lo + b)]

        def cv(name, a=0, b=None):
            lo, hi = CON[name]
            return con[:, lo + a:(hi if b is None else lo + b)]

        def spread(ap, n, w):
            return ap.rearrange("p (o w) -> p o w", o=1).to_broadcast([P, n, w])

        omu = derived[:, 0:26]
        nw0, ha0, hv0 = (derived[:, 26 + 8 * i:34 + 8 * i] for i in range(3))
        cosT, sinT = cs[:, 0:S], cs[:, S:2 * S]

        def views(*sizes):
            at, res = 0, []
            for w in sizes:
                res.append(WORK[:, at:at + w])
                at += w
            assert at <= 14464, at
            return res

        (QR, KD, KRAW, QRAW, X2, XW, VTM, RT, SC0, SC1, PT, HIDK, HIDV, HT, GS, KCR, KCd) = views(
            2048, 2048, 1024, 1024, 1024, 1920, 1024, 1024, 512, 1024, 1024, 120, 120, 240, 96, 120, 60)
        QR = QR.rearrange("p (t n) -> p t n", t=HP)
        KD = KD.rearrange("p (t n) -> p t n", t=8)
        X2 = X2.rearrange("p (b g n) -> p b g n", b=2, g=NG)
        XW = XW.rearrange("p (b m j) -> p b m j", b=2, m=CMP // 2)
        VTM = VTM.rearrange("p (t n) -> p t n", t=2)
        SC0 = SC0.rearrange("p (b r k) -> p b r k", b=2, r=2)
        SC1 = SC1.rearrange("p (b r k) -> p b r k", b=2, r=2)
        GS = GS.rearrange("p (t n) -> p t n", t=2)

        (KR, BB, KA, Ybd, BBt, KAt, Qd, QdT, QT32, QT64, Mrb, Mak, Mrk, Q2, Q2T, Q4T, X, VDUP, Vst, SG, LPW, LIW,
         Wd, TA, NK, K2, KSQ, TV, VX, WC, Z, Zt, RHS, Uc, GNS) = views(
            2048, 512, 512, 512, 512, 512, 512, 512, 512, 512, 512, 512, 512, 512, 512, 512, 512, 512, 256,
            256, 256, 256, 256, 256, 256, 256, 256, 256, 256, 8, 64, 64, 64, 64, 24)
        KR = KR.rearrange("p (b c n) -> p b c n", b=2, c=NCH)
        BB, KA, Ybd, BBt, KAt, Qd, QdT, QT32, QT64, Mrb, Mak, Mrk, Q2, Q2T, Q4T, X, VDUP = (
            a.rearrange("p (c n) -> p c n", c=NCH)
            for a in (BB, KA, Ybd, BBt, KAt, Qd, QdT, QT32, QT64, Mrb, Mak, Mrk, Q2, Q2T, Q4T, X, VDUP))
        Vst = Vst.rearrange("p (c n) -> p c n", c=NCH)
        TT, XT, WX = Qd, Q2T, Q2
        RKK, BKK = SG, TA
        (XR, XN, GPOST) = views(4096, 4096, 2048)
        XR = XR.rearrange("p (t n) -> p t n", t=2)
        XN = XN.rearrange("p (t n) -> p t n", t=2)
        GAB = WORK[:, 10240:12288].rearrange("p (b n) -> p b n", b=2)
        SQJ = WORK[:, 12288:12800]

        bank = [ctx.enter_context(nc.psum_tensor(f"bank{b}", [P, 512], F32)) for b in range(8)]
        PB, A = bank[0:2], bank[2:8]

        def quad(b):
            return b[:, :].rearrange("p (c n) -> p c n", c=4)

        loaded = [signal(f"block_loaded{s}", 16 * USES[s]) for s in range(SLOTS)]
        par_loaded = signal("params_loaded", 16)
        con_loaded = sem("constants_loaded")
        pos_loaded = sem("positions_loaded")
        x_loaded = sem("x_loaded")
        x_copied = sem("x_copied")
        xr_loaded = signal("residual_loaded", 32)
        x_stored = signal("x_stored", 32)
        unit_done = [signal(f"unit_done{b}", UNITS // 2, 1) for b in range(2)]
        half_used = signal("half_block_used", 5, 1)
        hT_turned = signal("hT_turned", 8)
        hidden_done = signal("hidden_done", 2)
        cmp_done = signal("cmp_done", 3)
        krope_done = signal("krope_done", 8)
        qrope_done = signal("qrope_done", 4)
        scores_done = signal("scores_done", HEADS)
        probs_turned = signal("probs_turned", HEADS)
        pv_done = signal("pv_done", HEADS)
        vd_done = signal("vd_done", 1)
        rwkv_step = signal("rwkv_step", PRE_STEPS + HP * RW_STEPS + 1)
        unit_free = [signal(f"unit_free{b}", UNITS // 2, 1) for b in range(2)]
        act_chain = sem("act_chain")
        x_squared = signal("x_squared", 1)
        hT_act = signal("hT_act", 4)
        lo_act = signal("lora_inputs_scaled", 1)
        lo_ready = signal("lora_inputs_ready", 1)
        x2_act = signal("x2_act", 2)
        z_tanh = signal("z_tanh", 8)
        kvr_act = signal("kvr_scaled", 12)
        wo_sq = signal("wo_squared", 8)
        hid_sq = signal("hidden_squared", 2)
        hid_tanh = signal("hidden_tanh", 2)
        kcraw_ready = signal("kcraw_ready", 1)
        vc_ready = signal("vc_ready", 1)
        exps_done = signal("exps_done", HEADS)
        pt_act = signal("pt_act", HEADS)
        vd_ready = signal("vd_ready", 1)
        q2_ready = signal("q2_ready", HP)
        tok_ready = signal("bet_kha_tokenmajor", HP)
        q4_ready = signal("q4_ready", HP)
        v1_ready = signal("v1_ready", HP)
        xt_ready = signal("xt_ready", 2 * HP)
        wx_ready = signal("wx_ready", 2 * HP)
        rhs_ready = signal("rhs_ready", NCH * HP)
        u_ready = signal("u_ready", NCH * HP)
        ksq_ready = signal("ksq_ready", HP)
        lora_read = signal("lora_read", HP)
        tv_ready = signal("tv_ready", HP)
        decays_ready = signal("decays_ready", HP)
        sqrt_ready = signal("sqrt_ready", HP)
        ysq_ready = signal("ysq_ready", HP)
        yt_ready = signal("yt_ready", HP)
        dve_chain = sem("dve_chain")
        sin_arg = sem("sin_arg")
        table_ready = sem("table_ready")
        ms_ready = signal("ms_ready", 1)
        xn_ready = signal("xn_ready", 1)
        hT_dve = signal("hT_dve", 4)
        xw_ready = signal("xw_ready", 2)
        kd_ready = signal("kd_ready", 8)
        qr_ready = signal("qr_ready", 4)
        hid_arg = signal("hidden_arg", 2)
        hid_ready = signal("hid_ready", 2)
        kc_ready = signal("kc_ready", 1)
        sc_ready = signal("scores_masked", HEADS)
        cf_ready = signal("coef_ready", HEADS)
        pt_dve = signal("pt_dve", HEADS)
        yb_ready = signal("yb_ready", HP)
        q_masked = signal("q_masked", HP)
        m_masked = signal("m_masked", HP)
        v_ready = signal("v_stack_ready", HP)
        x_step = signal("x_step", 4 * HP)
        t_ready = signal("t_ready", HP)
        bonus_ready = signal("bonus_ready", HP)
        z_ready = signal("z_ready", (NCH - 1) * HP)
        scan_done = signal("scan_done", HP)
        n_ready = signal("n_ready", HP)
        mid_ready = signal("mid_ready", HP)
        ew_dve = signal("ew_dve", HP)
        yc_ready = signal("yc_ready", HP)
        var_ready = signal("var_ready", HP)
        ybd_ready = signal("ybd_ready", HP)
        ya_ready = signal("ya_ready", HP)
        merged_ready = signal("merged_ready", 8)
        ms2_ready = signal("ms2_ready", 1)
        x_new = signal("x_new", 1, 1)
        zeroed = sem("zeroed")
        pads_zero = signal("pads_zero", 1)
        derived_ready = signal("derived_ready", 1)
        rstd_ready = signal("rstd_ready", 1)
        probs_ready = signal("probs_ready", HEADS)
        x1_ready = signal("x1_ready", HP)
        lp_ready = signal("lp_ready", HP)
        ew_pool = signal("ew_pool", HP)
        grstd_ready = signal("grstd_ready", HP)
        rstd2_ready = signal("rstd2_ready", 1)

        def taken(l, u):
            return unit_free[u % 2].sem, unit_free[u % 2].at(l, u // 2 + 1)

        def done(l, u):
            return unit_done[u % 2].sem, unit_done[u % 2].at(l, u // 2 + 1)

        block = ctx.enter_context(nc.Block())
        out2 = out.rearrange("a (t p) n -> p (a t) n", p=P)
        x2 = x.rearrange("a (t p) n -> p (a t) n", p=P)

        @block.sync
        def _(sp):
            sp.dma_start(con[:, :], consts).then_inc(con_loaded, 16)
            sp.dma_start(WORK[:, 14208:14208 + S].bitcast(I32), pos.to_broadcast([P, S])).then_inc(pos_loaded, 16)
            sp.dma_start(XR, x2).then_inc(x_loaded, 16)
            sp.dma_start(par[:, :], params[0, :, :]).then_inc(par_loaded.sem, 16)
            sp.dma_start(out, x).then_inc(x_copied, 16)


            def used_up(b):
                if b in (B_VT,) or (b >= B_WO and (b - B_WO) % 2 == 0):
                    return half_used, 1 if b == B_VT else 2 + (b - B_WO) // 2
                if b in (B_CK, B_CV):
                    return hidden_done, b - B_CK + 1
                if b == B_LOG:
                    u = U_GATE
                elif b < B_VT:
                    u = U_KC + b - B_KC
                elif b == B_VT + 1:
                    u = U_VT + 1
                elif b < B_CK:
                    u = U_Q + b - B_Q
                elif b < B_PB:
                    u = U_ZB + b - B_ZB
                elif b < B_A:
                    u = U_PB + 2 * (b - B_PB) + 1
                elif b < B_WO:
                    u = U_A + 4 * ((b - B_A) // 3) + (0, 1, 3)[(b - B_A) % 3]
                else:
                    u = U_WO + 2 * ((b - B_WO) // 2) + 1
                return unit_done[u % 2], u // 2 + 1

            with sp.Fori(0, LAYERS) as l:
                def load(b):
                    s = b % SLOTS
                    before = used_up(b - SLOTS) if b >= SLOTS else (half_used, 0) if b == 1 else (unit_done[1], 0)
                    sp.wait_ge(before[0].sem, before[0].at(l, before[1]))
                    sp.dma_start(slots[s][:, :], stream[bass.ds(l * NB + b, 1), :, :].rearrange("a p n -> (a p) n")
                                 ).then_inc(loaded[s].sem, 16)

                for b in range(B_WO - 2):
                    load(b)
                sp.wait_ge(ya_ready.sem, ya_ready.at(l, HP))
                sp.wait_ge(x_copied, 16)
                sp.wait_ge(x_stored.sem, x_stored.at(l, 0) + 1)
                sp.dma_start(XR, out2).then_inc(xr_loaded.sem, 16)
                sp.dma_start(GPOST, norm_post[bass.ds(l, 1), :].to_broadcast([P, D])).then_inc(xr_loaded.sem, 16)
                sp.dma_start(par[:, :], params[bass.ds(l + 1, 1), :, :].rearrange("a p n -> (a p) n")
                             ).then_inc(par_loaded.sem, 16)
                for b in range(B_WO - 2, NB):
                    load(b)
                sp.wait_ge(x_new.sem, x_new.at(l, 1))
                for t in range(2):
                    sp.dma_start(out2[:, t, :], XR[:, t, :]).then_inc(x_stored.sem, 16)
            sp.wait_ge(x_stored.sem, LAYERS * 32 + 1)
            sp.wait_ge(par_loaded.sem, (LAYERS + 1) * 16)

        def pe_layer(pe, l):
            mm = pe.matmul

            def take(b):
                s = b % SLOTS
                pe.wait_ge(loaded[s].sem, loaded[s].at(l, 16 * (b // SLOTS + 1)))
                return slots[s]

            def start_unit(u):
                pe.wait_ge(unit_free[u % 2].sem, unit_free[u % 2].at(l, u // 2))
                return PB[u % 2]

            def end_unit(ins, u):
                ins.then_inc(unit_done[u % 2].sem, 1)

            def point(kind, i):
                if kind == "att":
                    attention(i)
                if kind == "rwkv":
                    rwkv(i)

            def product(b, u, rhs, kind=None, first=0, every=16, chunks=KC, wide=2 * P, tiles=(0, 1)):
                w, o = take(b), start_unit(u)
                n = 0
                for j, tile in enumerate(tiles):
                    for c in range(chunks):
                        ins = mm(o[:, j * S:(j + 1) * S], w[:, c * wide + tile * P:c * wide + (tile + 1) * P], rhs[:, c, :],
                                 start=(c == 0), stop=(c == chunks - 1))
                        n += 1
                        if n == chunks * len(tiles):
                            end_unit(ins, u)
                        if kind and n % every == 0:
                            point(kind, first + n // every - 1)

            pe.wait_ge(xn_ready.sem, xn_ready.at(l, 1))
            for j in range(8):
                if j >= 4:
                    read = hT_dve if j % 2 else hT_act
                    pe.wait_ge(read.sem, read.at(l, j // 2 - 1))
                for c in (2 * j, 2 * j + 1):
                    for t in range(2):
                        at = (c % 2) * S + t * P
                        ins = pe.transpose(A[j % 4][:, at:at + P], XN[:, t, c * P:(c + 1) * P], cv("ident"))
                ins.then_inc(hT_turned.sem, 1)
            pe.wait_ge(hT_act.sem, hT_act.at(l, 4))
            pe.wait_ge(hT_dve.sem, hT_dve.at(l, 4))

            w, o = take(B_LOG), start_unit(U_LO)
            for j in range(2):
                for c in range(KC):
                    ins = mm(o[0:LORA_W, j * S:(j + 1) * S], w[:, c * 256 + j * LORA_W:c * 256 + (j + 1) * LORA_W],
                             hT[:, c, :], start=(c == 0), stop=(c == KC - 1))
            end_unit(ins, U_LO)
            o = start_unit(U_GATE)
            for t in range(2):
                for c in range(KC):
                    ins = mm(o[:, t * 64:t * 64 + 48], hT[:, c, t * P:(t + 1) * P], w[:, c * 256 + 192:c * 256 + 240],
                             start=(c == 0), stop=(c == KC - 1))
            end_unit(ins, U_GATE)

            for b, u in ((B_KC, U_KC), (B_VC, U_VC), (B_KS, U_KS), (B_KW, U_KW)):
                product(b, u, hT)
            for kh in range(2):
                w = take(B_VT + kh)
                for t in range(2):
                    if kh == 0:
                        start_unit(U_VT + t)
                    for c in range(8):
                        ins = mm(PB[t][:, :], hT[:, 8 * kh + c, t * P:(t + 1) * P], w[:, c * 512:(c + 1) * 512],
                                 start=(kh == 0 and c == 0), stop=(kh == 1 and c == 7))
                    if kh == 1:
                        end_unit(ins, U_VT + t)
                if kh == 0:
                    ins.then_inc(half_used.sem, 1)

            def k_rope(n):
                src, tile, gg = n // 4, (n % 4) // 2, n % 2
                if n % 4 == 0:
                    pe.wait_ge(*taken(l, U_KS + src))
                if n >= 4:
                    pe.wait_ge(kd_ready.sem, kd_ready.at(l, n - 3))
                raw = KRAW[:, src * 512 + tile * S:src * 512 + (tile + 1) * S]
                for r in range(2):
                    ins = mm(A[n % 4][:, r * S:(r + 1) * S], cv("dup", (2 * gg + r) * P, (2 * gg + r + 1) * P), raw,
                             start=True, stop=True)
                ins.then_inc(krope_done.sem, 1)

            def q_rope(j):
                pe.wait_ge(*taken(l, U_Q + j))
                if j >= 2:
                    pe.wait_ge(qr_ready.sem, qr_ready.at(l, j - 1))
                mm(A[4 + j % 2][:, :], cv("rot"), QRAW[:, (j % 2) * 512:(j % 2 + 1) * 512], start=True, stop=True
                   ).then_inc(qrope_done.sem, 1)

            for j in range(4):
                product(B_Q + j, U_Q + j, hT)
                k_rope(2 * j)
                k_rope(2 * j + 1)
                if j >= 1:
                    q_rope(j - 1)
            for i in range(2):
                w = take(B_CK + i)
                pe.wait_ge(xw_ready.sem, xw_ready.at(l, i + 1))
                if i == 0:
                    pe.wait_ge(kd_ready.sem, kd_ready.at(l, 8))
                for hh in range(2):
                    for m in range(CMP // 2):
                        ins = mm(A[i][:, hh * 64:hh * 64 + NCG], w[:, m * 256 + hh * P:m * 256 + (hh + 1) * P],
                                 XW[:, i, m, :], start=(m == 0), stop=(m == CMP // 2 - 1))
                ins.then_inc(hidden_done.sem, 1)
            q_rope(3)
            product(B_ZB, U_ZB, hT)
            pe.wait_ge(hid_ready.sem, hid_ready.at(l, 1))
            pe.wait_ge(derived_ready.sem, derived_ready.at(l, 1))
            for hh in range(2):
                ins = mm(A[2][:, 0:NCG], w2kd[:, hh * P:(hh + 1) * P], HIDK[:, hh * NCG:(hh + 1) * NCG],
                         start=(hh == 0), stop=(hh == 1))
            ins.then_inc(cmp_done.sem, 1)
            product(B_ZB + 1, U_ZB + 1, hT)
            pe.wait_ge(kcraw_ready.sem, kcraw_ready.at(l, 1))
            mm(A[2][:, 64:64 + NCG], cv("rot"), KCR[:, 0:NCG], start=True, stop=True).then_inc(cmp_done.sem, 1)
            pe.wait_ge(hid_ready.sem, hid_ready.at(l, 2))
            for g in range(NG):
                for hh in range(2):
                    ins = mm(A[3][0:NCMP, g * HD:(g + 1) * HD],
                             HIDV[:, hh * NCG + g * NCMP:hh * NCG + (g + 1) * NCMP],
                             pv("w2v", hh * HD, (hh + 1) * HD), start=(hh == 0), stop=(hh == 1))
            ins.then_inc(cmp_done.sem, 1)
            product(B_ZB + 2, U_ZB + 2, hT)
            product(B_ZB + 3, U_ZB + 3, hT)
            pe.wait_ge(qr_ready.sem, qr_ready.at(l, 4))
            pe.wait_ge(kc_ready.sem, kc_ready.at(l, 1))
            pe.wait_ge(vc_ready.sem, vc_ready.at(l, 1))
            pe.wait_ge(*taken(l, U_VT))
            pe.wait_ge(*taken(l, U_VT + 1))

            def scores(h):
                g, tile, a = h // 4, h // 2, (h % 2) * HD
                if h >= 1:
                    pe.wait_ge(sc_ready.sem, sc_ready.at(l, h))
                for qt in range(2):
                    q = QR[a:a + HD, tile, qt * P:(qt + 1) * P]
                    n = P * (qt + 1)
                    for r in range(2):
                        mm(A[qt][:, r * n:(r + 1) * n], q, KD[a:a + HD, 4 * r + g, 0:n], start=True, stop=True)
                for qt in range(2):
                    q = QR[a:a + HD, tile, qt * P:(qt + 1) * P]
                    ins = mm(A[0][:, 256 + 16 * qt:256 + 16 * qt + NCMP], q, KCd[a:a + HD, g * NCMP:(g + 1) * NCMP],
                             start=True, stop=True)
                ins.then_inc(scores_done.sem, 1)

            def turn_probs(h):
                pe.wait_ge(probs_ready.sem, probs_ready.at(l, h + 1))
                if h >= 1:
                    pe.wait_ge(pt_act.sem, pt_act.at(l, h))
                    pe.wait_ge(pt_dve.sem, pt_dve.at(l, h))
                b = h % 2
                for r in range(2):
                    pe.transpose(A[2 + r][:, 0:128], SC0[:, b, r, :], cv("ident"))
                    pe.transpose(A[2 + r][:, 128:256], SC1[:, b, r, 0:128], cv("ident"))
                    pe.transpose(A[2 + r][:, 256:384], SC1[:, b, r, 128:256], cv("ident"))
                    ins = pe.transpose(A[2 + r][:, 384:512], PC[:, b, r, :], cv("ident"))
                ins.then_inc(probs_turned.sem, 1)

            def weigh_values(h):
                g, a = h // 4, (h % 2) * HD
                pe.wait_ge(pt_act.sem, pt_act.at(l, h + 1))
                pe.wait_ge(pt_dve.sem, pt_dve.at(l, h + 1))
                if h >= 4 and h % 2 == 0:
                    pe.wait_ge(yb_ready.sem, yb_ready.at(l, h // 2 - 1))
                full, lo, hi = (A[4 + (h // 2) % 2][a:a + HD, s:e] for s, e in ((0, S), (0, P), (P, S)))
                mm(full, VTM[:, 0, g * HD:(g + 1) * HD], PT[:, 0:256], start=True, stop=False)
                mm(hi, VTM[:, 1, g * HD:(g + 1) * HD], PT[:, 256:384], start=False, stop=False)
                mm(lo, VC[:, g, :], PT[:, 384:512], start=False, stop=False)
                mm(full, VTM[:, 0, 256 + g * HD:256 + (g + 1) * HD], PT[:, 512:768], start=False, stop=False)
                mm(hi, VTM[:, 1, 256 + g * HD:256 + (g + 1) * HD], PT[:, 768:896], start=False, stop=False)
                mm(hi, VC[:, g, :], PT[:, 896:1024], start=False, stop=True).then_inc(pv_done.sem, 1)

            def attention(i):
                if 2 <= i < HEADS + 2:
                    weigh_values(i - 2)
                if 1 <= i < HEADS + 1:
                    turn_probs(i - 1)
                if i < HEADS:
                    scores(i)
                if i == 20:
                    pe.wait_ge(yb_ready.sem, yb_ready.at(l, HP))
                    pe.wait_ge(*taken(l, U_K + 6))
                    pe.wait_ge(*taken(l, U_K + 7))
                    for c in range(HP):
                        ins = mm(A[5][0:LORA_V, 0:S], pv("v_down", c * LORA_V, (c + 1) * LORA_V), V[:, c, :],
                                 start=(c == 0), stop=(c == HP - 1))
                    ins.then_inc(vd_done.sem, 1)

            for u in range(12):
                product(B_K + u, U_K + u, hT, "att", 2 * u)

            def lora(p):
                cols = slice(p * P, (p + 1) * P)
                mm(A[3][:, 0:S], par[0:LORA_W, PAR["w_up"][0] + p * P:PAR["w_up"][0] + (p + 1) * P], LO[0:LORA_W, 0:S],
                   start=True, stop=True)
                return mm(A[3][:, S:2 * S], par[0:LORA_W, PAR["a_up"][0] + p * P:PAR["a_up"][0] + (p + 1) * P],
                          LO[0:LORA_W, S:2 * S], start=True, stop=True)

            def norms(p):
                mm(A[1][:, 0:S], par[0:LORA_V, PAR["v_up"][0] + p * P:PAR["v_up"][0] + (p + 1) * P], VD[0:LORA_V, :],
                   start=True, stop=True)
                pe.wait_ge(ksq_ready.sem, ksq_ready.at(l, p + 1))
                return mm(A[1][:, S:2 * S], cv("ones"), KSQ, start=True, stop=True)

            def four(o, lhs, rhs, turn=False):
                for c in range(NCH):
                    if turn:
                        ins = pe.transpose(quad(o)[:, c, :], lhs[:, c, :], cv("ident"))
                    else:
                        ins = mm(quad(o)[:, c, :], lhs[:, c, :], rhs[:, c, :], start=True, stop=True)
                return ins

            def turn_y(p):
                pe.wait_ge(ybd_ready.sem, ybd_ready.at(l, p + 1))
                for c in range(NCH):
                    ins = mm(A[2][:, c * CH:(c + 1) * CH], Ybd[:, c, :], cv("ident2"), start=True, stop=True)
                return ins

            def rwkv_pair(p, k):
                kap, rho = KR[:, p % 2, :, 0:P], KR[:, p % 2, :, P:2 * P]
                wait = pe.wait_ge
                if k == 0:
                    wait(ew_dve.sem, ew_dve.at(l, p + 1))
                    wait(ew_pool.sem, ew_pool.at(l, p + 1))
                    if p:
                        wait(z_ready.sem, z_ready.at(l, 3 * p))
                    four(A[0], BB, kap)
                    ins = four(A[1], kap, BB)
                elif k == 1:
                    if p:
                        wait(yc_ready.sem, yc_ready.at(l, p))
                    four(A[2], BB, rho)
                    four(A[3], KA, kap)
                    ins = four(A[4], KA, rho)
                elif k == 2:
                    ins = four(A[5], VDUP, None, True)
                elif k == 3:
                    wait(q_masked.sem, q_masked.at(l, p + 1))
                    four(A[0], QdT, Qd)
                    ins = four(A[1], Qd, QdT)
                elif k == 4:
                    wait(m_masked.sem, m_masked.at(l, p + 1))
                    four(A[2], BB, None, True)
                    ins = four(A[3], KA, None, True)
                elif k == 5:
                    wait(q2_ready.sem, q2_ready.at(l, p + 1))
                    wait(x1_ready.sem, x1_ready.at(l, p + 1))
                    four(A[4], Q2T, X)
                    ins = four(A[0], Q2, Q2T)
                elif k == 6:
                    ins = mm(A[1][:, 0:S], cv("ones"), RKK, start=True, stop=True)
                elif k == 7:
                    wait(q4_ready.sem, q4_ready.at(l, p + 1))
                    wait(x_step.sem, x_step.at(l, 4 * p + 1))
                    ins = four(A[4], Q4T, X)
                    if p:
                        wait(tok_ready.sem, tok_ready.at(l, p + 1))
                        ins = turn_y(p - 1)
                elif k == 8:
                    wait(x_step.sem, x_step.at(l, 4 * p + 2))
                    wait(v_ready.sem, v_ready.at(l, p + 1))
                    ins = four(A[5], Q4T, X)
                elif k == 9:
                    wait(v1_ready.sem, v1_ready.at(l, p + 1))
                    ins = four(A[4], Q4T, WX)
                    if p + 1 < HP:
                        wait(tok_ready.sem, tok_ready.at(l, p + 1))
                        ins = lora(p + 1)
                elif k == 10 or k == 13:
                    wait(x_step.sem, x_step.at(l, 4 * p + (3 if k == 10 else 4)))
                    ins = four(A[5], X, None, True)
                elif k == 11:
                    ins = four(A[0], QT32, X)
                    if p + 1 < HP:
                        wait(bonus_ready.sem, bonus_ready.at(l, p + 1))
                        ins = norms(p + 1)
                elif k == 12:
                    wait(xt_ready.sem, xt_ready.at(l, 2 * p + 1))
                    wait(wx_ready.sem, wx_ready.at(l, 2 * p + 1))
                    ins = four(A[4], XT, WX)
                elif k == 14:
                    four(A[0], QT64, X)
                    if p + 1 < HP:
                        wait(lora_read.sem, lora_read.at(l, p + 2))
                    else:
                        wait(tok_ready.sem, tok_ready.at(l, p + 1))
                    ins = mm(A[3][:, 0:CH], Mak[:, 0, :], Vst[:, 0, :], start=True, stop=True)
                elif k == 15:
                    wait(xt_ready.sem, xt_ready.at(l, 2 * p + 2))
                    wait(wx_ready.sem, wx_ready.at(l, 2 * p + 2))
                    ins = four(A[4], XT, WX)
                elif k % 3 == 0:
                    c = (k - 15) // 3
                    wait(z_ready.sem, z_ready.at(l, 3 * p + c))
                    mm(A[3][:, c * CH:(c + 1) * CH], kap[:, c, :], Z, start=True, stop=False)
                    ins = mm(A[3][:, c * CH:(c + 1) * CH], Mak[:, c, :], Vst[:, c, :], start=False, stop=True)
                elif k % 3 == 1:
                    c = (k - 16) // 3
                    if c == 0:
                        wait(t_ready.sem, t_ready.at(l, p + 1))
                    wait(rhs_ready.sem, rhs_ready.at(l, NCH * p + c + 1))
                    ins = mm(A[3][:, 256 + c * CH:256 + (c + 1) * CH], TT[:, c, :], RHS, start=True, stop=True)
                else:
                    c = (k - 17) // 3
                    y, z = A[2][:, c * CH:(c + 1) * CH], A[1][:, 256 + c * CH:256 + (c + 1) * CH]
                    wait(u_ready.sem, u_ready.at(l, NCH * p + c + 1))
                    if c == 0:
                        wait(tok_ready.sem, tok_ready.at(l, p + 1))
                        if p:
                            wait(yt_ready.sem, yt_ready.at(l, p))
                        if p + 1 < HP:
                            wait(tv_ready.sem, tv_ready.at(l, p + 2))
                            wait(n_ready.sem, n_ready.at(l, p + 2))
                    else:
                        mm(y, rho[:, c, :], Z, start=True, stop=False)
                    mm(y, Mrb[:, c, :], Uc, start=(c == 0), stop=False)
                    ins = mm(y, Mrk[:, c, :], Vst[:, c, :], start=False, stop=True)
                    if c + 1 < NCH:
                        mm(z, BBt[:, c, :], Uc, start=True, stop=False)
                        ins = mm(z, KAt[:, c, :], Vst[:, c, :], start=False, stop=True)
                ins.then_inc(rwkv_step.sem, 1)

            def rwkv(i):
                if i < HP * RW_STEPS:
                    rwkv_pair(i // RW_STEPS, i % RW_STEPS)

            pe.wait_ge(lo_ready.sem, lo_ready.at(l, 1))
            pe.wait_ge(yb_ready.sem, yb_ready.at(l, HP))
            lora(0).then_inc(rwkv_step.sem, 1)
            pe.wait_ge(vd_ready.sem, vd_ready.at(l, 1))
            norms(0).then_inc(rwkv_step.sem, 1)
            for u in range(4):
                product(B_ZA + u, U_ZA + u, hT, "rwkv", 16 * u, 2)
            for u in range(8):
                product(B_MGB + u, U_MGB + u, hT, "rwkv", 64 + 16 * u, 2)
            for u in range(8):
                product(B_PB + u // 2, U_PB + u, ZB, "rwkv", 192 + 8 * u, 2, HP, 512,
                        (2 * (u % 2), 2 * (u % 2) + 1))
            turn_y(HP - 1).then_inc(rwkv_step.sem, 1)

            for j in range(4):
                product(B_A + 3 * j, U_A + 4 * j, hT)
                product(B_A + 3 * j + 1, U_A + 4 * j + 1, hT)
                if j == 0:
                    pe.wait_ge(ya_ready.sem, ya_ready.at(l, HP))
                for i in range(2):
                    product(B_A + 3 * j + 2, U_A + 4 * j + 2 + i, ZA, None, 0, 16, HP, 512, (2 * i, 2 * i + 1))
            pe.wait_ge(merged_ready.sem, merged_ready.at(l, 8))
            for n in range(4):
                for kh in range(2):
                    w = take(B_WO + 2 * n + kh)
                    for t in range(2):
                        u = U_WO + 2 * n + t
                        if kh == 0:
                            start_unit(u)
                        for c in range(8):
                            ins = mm(PB[t][:, :], MB[:, 8 * kh + c, t * P:(t + 1) * P], w[:, c * 512:(c + 1) * 512],
                                     start=(kh == 0 and c == 0), stop=(kh == 1 and c == 7))
                        if kh == 1:
                            end_unit(ins, u)
                    if kh == 0:
                        ins.then_inc(half_used.sem, 1)

        @block.tensor
        def _(pe):
            for s in unit_done + unit_free + [half_used]:
                pe.sem_inc(s.sem, 1)
            pe.sem_inc(x_stored.sem, 1)
            pe.sem_inc(x_new.sem, 1)
            pe.wait_ge(con_loaded, 16)
            pe.wait_ge(zeroed, 1)
            with pe.Fori(0, LAYERS) as l:
                pe_layer(pe, l)

        def act_layer(act, l, chain):
            wait = act.wait_ge

            def copy(o, i, scale=1.0):
                return act.activation(o, i, ACT.Copy, scale=scale)

            def flat(a):
                return a.rearrange("p a b -> p (a b)")

            wait(x_new.sem, x_new.at(l, 0))
            for t in range(2):
                chain.step(act.activation(XN[:, t, :], XR[:, t, :], ACT.Square, accum_out=small[:, t:t + 1]))
            chain.settle()
            act.activation(small[:, 60:61], small[:, 0:1], ACT.Copy).then_inc(x_squared.sem, 1)
            wait(par_loaded.sem, par_loaded.at(l, 16))
            for j in range(0, 8, 2):
                wait(hT_turned.sem, hT_turned.at(l, j + 1))
                for c in range(2):
                    ins = copy(hT[:, 2 * j + c, :], A[j % 4][:, c * S:(c + 1) * S],
                               pv("norm_pre", 2 * j + c, 2 * j + c + 1))
                ins.then_inc(hT_act.sem, 1)
            wait(derived_ready.sem, derived_ready.at(l, 1))
            wait(*done(l, U_LO))
            for j in range(2):
                ins = copy(LO[0:LORA_W, j * S:(j + 1) * S], PB[0][0:LORA_W, j * S:(j + 1) * S],
                           omu[0:LORA_W, 24 + j:25 + j])
            ins.then_inc(lo_act.sem, 1)
            wait(*done(l, U_GATE))
            act.activation(GS, PB[1][:, 0:128].rearrange("p (t n) -> p t n", t=2)[:, :, 0:48], ACT.Tanh, scale=0.5
                           ).then_inc(unit_free[1].sem, 1)
            wait(*taken(l, U_LO))
            act.activation(LO[0:LORA_W, 0:S], LO[0:LORA_W, 0:S], ACT.Tanh).then_inc(lo_ready.sem, 1)

            for i in range(2):
                u = U_KC + i
                wait(*done(l, u))
                src = PB[u % 2][:, :].rearrange("p (t n r) -> p t n r", t=2, r=2)
                for gg in range(2):
                    ins = copy(X2[0:HD, i, gg::2, :], src[gg * HD:(gg + 1) * HD, :, :, 0])
                ins.then_inc(x2_act.sem, 1)
            for i in range(2):
                u = U_KS + i
                wait(*done(l, u))
                copy(KRAW[:, i * 512:(i + 1) * 512], PB[u % 2][:, :]).then_inc(unit_free[u % 2].sem, 1)
            for t in range(2):
                u = U_VT + t
                wait(*done(l, u))
                copy(VTM[:, t, :], PB[u % 2][:, :]).then_inc(unit_free[u % 2].sem, 1)
            for j in range(4):
                u = U_Q + j
                wait(*done(l, u))
                if j >= 2:
                    wait(qr_ready.sem, qr_ready.at(l, j - 1))
                copy(QRAW[:, (j % 2) * 512:(j % 2 + 1) * 512], PB[u % 2][:, :]).then_inc(unit_free[u % 2].sem, 1)
            for i in range(2):
                wait(hidden_done.sem, hidden_done.at(l, i + 1))
                if i:
                    wait(hid_ready.sem, hid_ready.at(l, 1))
                x = A[i][:, 0:128].rearrange("p (h n) -> p h n", h=2)[:, :, 0:NCG]
                act.activation(HT[:, 0:120].rearrange("p (h n) -> p h n", h=2), x, ACT.Square
                               ).then_inc(hid_sq.sem, 1)
                wait(hid_arg.sem, hid_arg.at(l, i + 1))
                act.activation(HT[:, 120:240], HT[:, 0:120], ACT.Tanh, scale=float(np.sqrt(2 / np.pi))
                               ).then_inc(hid_tanh.sem, 1)

            def z_pass(i, u):
                wait(*done(l, u))
                if i >= 1:
                    wait(*taken(l, u - 1))
                act.activation(ZT[:, :], PB[u % 2][:, :], ACT.Tanh, scale=0.5).then_inc(z_tanh.sem, 1)

            z_pass(0, U_ZB)
            wait(cmp_done.sem, cmp_done.at(l, 1))
            copy(KCR[:, 0:NCG], A[2][:, 0:NCG], 0.5).then_inc(kcraw_ready.sem, 1)
            z_pass(1, U_ZB + 1)
            wait(cmp_done.sem, cmp_done.at(l, 3))
            wait(zeroed, 1)
            copy(flat(VC)[0:NCMP, :], A[3][0:NCMP, 0:256], 0.5).then_inc(vc_ready.sem, 1)
            z_pass(2, U_ZB + 2)
            z_pass(3, U_ZB + 3)

            def attention(i):
                if 1 <= i < HEADS + 1:
                    wait(probs_turned.sem, probs_turned.at(l, i))
                    copy(PT[:, 0:512], A[2][:, :]).then_inc(pt_act.sem, 1)
                if i < HEADS:
                    b = i % 2
                    wait(sc_ready.sem, sc_ready.at(l, i + 1))
                    for n, s in enumerate((SC0[:, b, 0, :], SC0[:, b, 1, :], SC1[:, b, 0, :], SC1[:, b, 1, :],
                                           PC[:, b, 0, 0:NCMP], PC[:, b, 1, 0:NCMP])):
                        ins = act.activation(s, s, ACT.Exp, bias=small[:, 12 + 6 * b + n:13 + 6 * b + n],
                                             accum_out=small[:, 24 + 6 * b + n:25 + 6 * b + n])
                        chain.step(ins)
                    chain.settle()
                    act.activation(small[:, 61:62], small[:, 24:25], ACT.Copy).then_inc(exps_done.sem, 1)
                if i == 21:
                    wait(vd_done.sem, vd_done.at(l, 1))
                    copy(VD[0:LORA_V, :], A[5][0:LORA_V, 0:S]).then_inc(vd_ready.sem, 1)

            for u in range(12):
                attention(2 * u)
                wait(*done(l, U_K + u))
                for t in range(2):
                    n = 2 * u + t
                    ins = copy(KVR[n // 8][:, n % 8, :], PB[u % 2][:, t * S:(t + 1) * S], omu[:, n:n + 1])
                ins.then_inc(kvr_act.sem, 1)
                attention(2 * u + 1)

            def kk_square(p):
                act.activation(KSQ, K[:, p, :], ACT.Square, scale=pv("k_k", p, p + 1)).then_inc(ksq_ready.sem, 1)

            def lora_pass(p):
                wait(rwkv_step.sem, rwkv_step.at(l, lora_at(p)))
                act.activation(SG, A[3][:, 0:S], ACT.Exp, bias=nw0[:, p:p + 1], scale=-1.0)
                act.activation(TA, A[3][:, S:2 * S], ACT.Tanh, bias=ha0[:, p:p + 1], scale=0.5
                               ).then_inc(lora_read.sem, 1)

            def tv_pass(p):
                wait(rwkv_step.sem, rwkv_step.at(l, norms_at(p)))
                act.activation(TV, A[1][:, 0:S], ACT.Tanh, bias=hv0[:, p:p + 1], scale=0.5).then_inc(tv_ready.sem, 1)

            def decays(p):
                wait(lp_ready.sem, lp_ready.at(l, p + 1))
                chain.step(act.activation(Wd, LIW, ACT.Exp, scale=-DECAY))
                act.activation(LPW, LPW, ACT.Exp, scale=-DECAY)
                chain.settle()
                act.activation(LIW, LIW, ACT.Exp, scale=DECAY).then_inc(decays_ready.sem, 1)

            def kk_norm(p):
                wait(n_ready.sem, n_ready.at(l, p + 1))
                act.activation(NK, NK, ACT.Sqrt).then_inc(sqrt_ready.sem, 1)

            def y_pass(p):
                act.activation(V[:, p, :], A[2][:, 0:S], ACT.Identity, bias=pv("gn_b", p, p + 1),
                               scale=pv("gn_w", p, p + 1)).then_inc(yt_ready.sem, 1)

            def rwkv_pair(p, k):
                if k in (3, 4, 5, 7, 8, 9, 10, 11, 13, 14) or k >= 16:
                    wait(rwkv_step.sem, rwkv_step.at(l, rw_at(p, k)))
                nxt = p + 1 < HP
                if k == 3:
                    copy(flat(Q2), A[0][:, :])
                    copy(flat(Q2T), A[1][:, :]).then_inc(q2_ready.sem, 1)
                elif k == 4:
                    copy(flat(BBt), A[2][:, :])
                    copy(flat(KAt), A[3][:, :]).then_inc(tok_ready.sem, 1)
                elif k == 5:
                    copy(flat(Q4T), A[0][:, :]).then_inc(q4_ready.sem, 1)
                elif k == 7 and p:
                    y_pass(p - 1)
                elif k == 8:
                    copy(flat(WX), A[5][:, :]).then_inc(v1_ready.sem, 1)
                    if nxt:
                        kk_square(p + 1)
                elif k == 9 and nxt:
                    lora_pass(p + 1)
                elif k == 10 or k == 13:
                    copy(flat(XT), A[5][:, :]).then_inc(xt_ready.sem, 1)
                elif k == 11:
                    copy(flat(WX), A[0][:, :]).then_inc(wx_ready.sem, 1)
                    if nxt:
                        tv_pass(p + 1)
                elif k == 12 and nxt:
                    decays(p + 1)
                elif k == 14:
                    copy(flat(WX), A[0][:, :]).then_inc(wx_ready.sem, 1)
                    copy(RHS, A[3][:, 0:CH]).then_inc(rhs_ready.sem, 1)
                    if nxt:
                        kk_norm(p + 1)
                elif k >= 16 and k % 3 == 1:
                    c = (k - 16) // 3
                    copy(Uc, A[3][:, 256 + c * CH:256 + (c + 1) * CH]).then_inc(u_ready.sem, 1)
                elif k >= 16 and k % 3 == 0:
                    c = (k - 15) // 3
                    copy(RHS, A[3][:, c * CH:(c + 1) * CH]).then_inc(rhs_ready.sem, 1)
                elif k == 26:
                    wait(yc_ready.sem, yc_ready.at(l, p + 1))
                    act.activation(V[:, p, :], K[:, p, :], ACT.Square).then_inc(ysq_ready.sem, 1)

            def rwkv(i):
                if i < HP * RW_STEPS:
                    rwkv_pair(i // RW_STEPS, i % RW_STEPS)

            wait(yb_ready.sem, yb_ready.at(l, HP))
            wait(*taken(l, U_K + 10))
            wait(*taken(l, U_K + 11))
            kk_square(0)
            lora_pass(0)
            tv_pass(0)
            decays(0)
            kk_norm(0)
            for u in range(4):
                for i in range(16):
                    rwkv(16 * u + i)
                z_pass(4 + u, U_ZA + u)
            for u in range(8):
                for i in range(16):
                    rwkv(64 + 16 * u + i)
                wait(*done(l, U_MGB + u))
                act.activation(flat(MB[:, 2 * u:2 * u + 2, :]), PB[u % 2][:, :], ACT.Tanh, scale=0.5
                               ).then_inc(unit_free[u % 2].sem, 1)
            for i in range(192, HP * RW_STEPS):
                rwkv(i)
            wait(rwkv_step.sem, rwkv_step.at(l, rw_at(HP, 0)))
            y_pass(HP - 1)

            wait(ya_ready.sem, ya_ready.at(l, HP))
            for j in range(4):
                if j >= 2:
                    wait(merged_ready.sem, merged_ready.at(l, 2 * j - 2))
                for i in range(2):
                    u = U_A + 4 * j + i
                    wait(*done(l, u))
                    act.activation(GAB[:, j % 2, i * 512:(i + 1) * 512], PB[u % 2][:, :], ACT.Tanh, scale=0.5
                                   ).then_inc(unit_free[u % 2].sem, 1)
            for n in range(4):
                for t in range(2):
                    u = U_WO + 2 * n + t
                    wait(*done(l, u))
                    chain.step(act.activation(SQJ, PB[t][:, :], ACT.Square,
                                              accum_out=small[:, 40 + 4 * t + n:41 + 4 * t + n]))
                    chain.settle()
                    act.activation(small[:, 62:63], small[:, 0:1], ACT.Copy).then_inc(wo_sq.sem, 1)

        @block.scalar
        def _(act):
            chain = Chain(act, act_chain)
            act.wait_ge(sin_arg, 1)
            act.activation(cs[:, :], cs[:, :], ACT.Sin).then_inc(table_ready, 1)
            act.wait_ge(x_loaded, 16)
            act.wait_ge(zeroed, 1)
            with act.Fori(0, LAYERS) as l:
                act_layer(act, l, chain)
                chain.restart()

        def dve_layer(dve, l, chain):
            wait = dve.wait_ge
            stt, tt, ts = dve.scalar_tensor_tensor, dve.tensor_tensor, dve.tensor_scalar

            def op(ins):
                chain.step(ins)
                chain.settle()

            def flat(a):
                return a.rearrange("p a b -> p (a b)")

            def view2(ap, n):
                return ap.rearrange("p (t n) -> p t n", t=n)

            wait(x_squared.sem, x_squared.at(l, 1))
            ts(small[:, 2:4], small[:, 0:2], 1.0 / D, NORM_EPS, ALU.mult, ALU.add).then_inc(ms_ready.sem, 1)
            wait(rstd_ready.sem, rstd_ready.at(l, 1))
            for t in range(2):
                ins = ts(XN[:, t, :], XR[:, t, :], small[:, 4 + t:5 + t], None, ALU.mult)
            ins.then_inc(xn_ready.sem, 1)
            wait(par_loaded.sem, par_loaded.at(l, 16))
            for j in range(1, 8, 2):
                wait(hT_turned.sem, hT_turned.at(l, j + 1))
                for c in range(2):
                    ins = ts(hT[:, 2 * j + c, :], A[j % 4][:, c * S:(c + 1) * S],
                             pv("norm_pre", 2 * j + c, 2 * j + c + 1), None, ALU.mult)
                ins.then_inc(hT_dve.sem, 1)
            wait(lo_act.sem, lo_act.at(l, 1))
            for j in range(2):
                ins = stt(LO[0:LORA_W, j * S + 1:(j + 1) * S], PB[0][0:LORA_W, j * S:(j + 1) * S - 1],
                          pv("mu", 24 + j, 25 + j)[0:LORA_W, :], LO[0:LORA_W, j * S + 1:(j + 1) * S], ALU.mult, ALU.add)
            ins.then_inc(unit_free[0].sem, 1)
            wait(*taken(l, U_GATE))
            for i, (qt, br) in enumerate(((0, 1), (0, 2), (1, 1), (1, 2), (0, 0), (1, 0))):
                chain.step(ts(gates[:, :, i], GS[:, qt, br * HEADS:(br + 1) * HEADS], 0.5, 0.5, ALU.mult, ALU.add))
            chain.settle()
            chain.step(ts(gates[:, :, 4], gates[:, :, 4], cv("rowok"), None, ALU.mult))

            for i in range(2):
                u = U_KC + i
                wait(x2_act.sem, x2_act.at(l, i + 1))
                src = PB[u % 2][:, :].rearrange("p (t n r) -> p t n r", t=2, r=2)
                for gg in range(2):
                    ins = dve.tensor_copy(X2[HD:P, i, gg::2, :], src[gg * HD:(gg + 1) * HD, :, :, 1])
                ins.then_inc(unit_free[u % 2].sem, 1)
                wait(*taken(l, u))
                for m in range(CMP // 2):
                    ins = ts(view2(XW[:, i, m, :], NG), X2[:, i, :, m:m + 8 * (NCMP - 1) + 1:8],
                             pv("pe_k" if i == 0 else "pe_v", m, m + 1), None, ALU.add)
                ins.then_inc(xw_ready.sem, 1)

            wait(x_stored.sem, x_stored.at(l, 0) + 1)
            for j in range(5):
                if j < 4:
                    for n in (2 * j, 2 * j + 1):
                        wait(krope_done.sem, krope_done.at(l, n + 1))
                        chain.step(tt(RT[:, 0:S], A[n % 4][:, 0:S], cosT, ALU.mult))
                        chain.step(tt(RT[:, S:2 * S], A[n % 4][:, S:2 * S], sinT, ALU.mult))
                        chain.settle()
                        tt(KD[:, n, :], RT[:, 0:S], RT[:, S:2 * S], ALU.add).then_inc(kd_ready.sem, 1)
                        wait(kd_ready.sem, kd_ready.at(l, n + 1))
                if j >= 1:
                    q = j - 1
                    wait(qrope_done.sem, qrope_done.at(l, q + 1))
                    chain.step(tt(view2(RT[:, 0:512], 2), view2(QRAW[:, (q % 2) * 512:(q % 2 + 1) * 512], 2),
                                  spread(cosT, 2, S), ALU.mult))
                    chain.step(tt(view2(RT[:, 512:1024], 2), view2(A[4 + q % 2][:, :], 2), spread(sinT, 2, S),
                                  ALU.mult))
                    chain.settle()
                    tt(flat(QR[:, 2 * q:2 * q + 2, :]), RT[:, 0:512], RT[:, 512:1024], ALU.add
                       ).then_inc(qr_ready.sem, 1)
                    wait(qr_ready.sem, qr_ready.at(l, q + 1))
            for i in range(2):
                x = A[i][:, 0:128].rearrange("p (h n) -> p h n", h=2)[:, :, 0:NCG]
                poly, th = view2(HT[:, 0:120], 2), view2(HT[:, 120:240], 2)
                wait(hid_sq.sem, hid_sq.at(l, i + 1))
                op(ts(poly, poly, 0.044715, 1.0, ALU.mult, ALU.add))
                tt(poly, poly, x, ALU.mult).then_inc(hid_arg.sem, 1)
                wait(hid_tanh.sem, hid_tanh.at(l, i + 1))
                stt(view2(HIDV if i else HIDK, 2), th, 1.0, x, ALU.add, ALU.mult).then_inc(hid_ready.sem, 1)

            def silu(i, u, z, tile):
                wait(z_tanh.sem, z_tanh.at(l, i + 1))
                stt(flat(z[:, tile:tile + 2, :]), ZT[:, :], 1.0, PB[u % 2][:, :], ALU.add, ALU.mult
                    ).then_inc(unit_free[u % 2].sem, 1)

            silu(0, U_ZB, ZB, 0)
            silu(1, U_ZB + 1, ZB, 2)
            wait(cmp_done.sem, cmp_done.at(l, 2))
            wait(kcraw_ready.sem, kcraw_ready.at(l, 1))
            ends = slice(CMP - 1, CMP - 1 + CSTR * (NCMP - 1) + 1, CSTR)
            chain.step(tt(view2(RT[:, 0:NCG], NG), view2(KCR[:, 0:NCG], NG), spread(cosT[:, ends], NG, NCMP), ALU.mult))
            chain.step(tt(view2(RT[:, 64:64 + NCG], NG), view2(A[2][:, 64:64 + NCG], NG),
                          spread(sinT[:, ends], NG, NCMP), ALU.mult))
            chain.settle()
            tt(KCd, RT[:, 0:NCG], RT[:, 64:64 + NCG], ALU.add).then_inc(kc_ready.sem, 1)
            silu(2, U_ZB + 2, ZB, 4)
            silu(3, U_ZB + 3, ZB, 6)

            def attention(i):
                if 3 <= i < HEADS + 2 and i % 2 == 1:
                    tile = (i - 3) // 2
                    wait(pv_done.sem, pv_done.at(l, i - 1))
                    stt(ZB[:, tile, :], A[4 + tile % 2][:, 0:S], 0.5, ZB[:, tile, :],
                        ALU.mult, ALU.mult).then_inc(yb_ready.sem, 1)
                if 1 <= i < HEADS + 1:
                    wait(probs_turned.sem, probs_turned.at(l, i))
                    dve.tensor_copy(PT[:, 512:1024], A[3][:, :]).then_inc(pt_dve.sem, 1)
                if i < HEADS:
                    b = i % 2
                    mx, rs, cf = (small[:, o + 6 * b:o + 6 * b + 6] for o in (12, 24, 48))
                    wait(scores_done.sem, scores_done.at(l, i + 1))
                    chain.step(stt(SC0[:, b, :, :], view2(A[0][:, 0:256], 2), SCALE, spread(cv("caus0"), 2, P),
                                   ALU.mult, ALU.add))
                    chain.step(stt(SC1[:, b, :, :], view2(A[1][:, :], 2), SCALE, spread(cv("caus1"), 2, S),
                                   ALU.mult, ALU.add))
                    chain.step(stt(PC[:, b, :, 0:NCMP], view2(A[0][:, 256:288], 2)[:, :, 0:NCMP], SCALE,
                                   view2(cv("cmpmask"), 2), ALU.mult, ALU.add))
                    chain.settle()
                    for n, s in enumerate((SC0[:, b, :, :], SC1[:, b, :, :], PC[:, b, :, 0:NCMP])):
                        chain.step(dve.tensor_reduce(mx[:, 2 * n:2 * n + 2], s, AX.X, ALU.max))
                    chain.settle()
                    ts(mx, mx, -1.0, None, ALU.mult).then_inc(sc_ready.sem, 1)
                    wait(exps_done.sem, exps_done.at(l, i + 1))
                    op(dve.reciprocal(rs, rs))
                    tt(cf, rs, gates[:, i, :], ALU.mult).then_inc(cf_ready.sem, 1)

            for u in range(12):
                attention(2 * u)
                wait(kvr_act.sem, kvr_act.at(l, u + 1))
                for t in range(2):
                    n = 2 * u + t
                    o = KVR[n // 8][:, n % 8, 1:S]
                    ins = stt(o, PB[u % 2][:, t * S:(t + 1) * S - 1], pv("mu", n, n + 1), o, ALU.mult, ALU.add)
                ins.then_inc(unit_free[u % 2].sem, 1)
                attention(2 * u + 1)

            def scan(p):
                wait(lora_read.sem, lora_read.at(l, p + 1))
                op(ts(SG, SG, 1.0, None, ALU.add))
                op(dve.reciprocal(SG, SG))
                dve.tensor_tensor_scan(LIW, cv("inchunk"), SG, 0.0, ALU.mult, ALU.add).then_inc(scan_done.sem, 1)

            def norm_floor(p):
                wait(tv_ready.sem, tv_ready.at(l, p + 1))
                ts(NK, A[1][:, S:2 * S], L2_EPS * L2_EPS, None, ALU.max).then_inc(n_ready.sem, 1)

            def values(p):
                wait(tv_ready.sem, tv_ready.at(l, p + 1))
                op(tt(VX, V[:, p, :], VF[:, p, :], ALU.subtract))
                op(stt(VF[:, p, :], VX, pv("first"), VF[:, p, :], ALU.mult, ALU.add))
                op(tt(VX, VF[:, p, :], V[:, p, :], ALU.subtract))
                op(stt(VX, TV, 1.0, VX, ALU.add, ALU.mult))
                for r in range(2):
                    chain.step(stt(VDUP[:, :, r * CH:(r + 1) * CH], view2(VX, NCH), 0.5, view2(V[:, p, :], NCH),
                                   ALU.mult, ALU.add))

            def keys(p):
                wait(sqrt_ready.sem, sqrt_ready.at(l, p + 1))
                chain.step(dve.reciprocal(NK, NK))
                op(ts(TA, TA, 0.5, -0.5, ALU.mult, ALU.add))
                chain.step(stt(NK, K[:, p, :], pv("k_k", p, p + 1), NK, ALU.mult, ALU.mult))
                op(ts(K2, TA, pv("k_a", p, p + 1), None, ALU.mult))
                chain.step(stt(K2, K2, 1.0, K[:, p, :], ALU.add, ALU.mult))
                chain.settle()
                stt(BKK, TA, 1.0, NK, ALU.add, ALU.mult).then_inc(mid_ready.sem, 1)

            def queries(p):
                wait(decays_ready.sem, decays_ready.at(l, p + 1))
                wait(mid_ready.sem, mid_ready.at(l, p + 1))
                if isinstance(p, int) and p == 0:
                    wait(pads_zero.sem, pads_zero.at(l, 1))
                chain.step(stt(RKK, R[:, p, :], pv("r_k", p, p + 1), K2, ALU.mult, ALU.mult))
                chain.step(dve.tensor_copy(WC[:, (p % 2) * 4:(p % 2) * 4 + 4], Wd[:, CH - 1:S:CH]))
                for h in range(2):
                    a, b = h * HD, (h + 1) * HD
                    chain.step(tt(KR[a:b, p % 2, :, a:b], view2(NK[a:b, :], NCH), view2(LPW[a:b, :], NCH), ALU.mult))
                    chain.step(tt(KR[a:b, p % 2, :, P + a:P + b], view2(R[a:b, p, :], NCH), view2(Wd[a:b, :], NCH),
                                  ALU.mult))
                chain.settle()
                dve.tensor_copy(GNS[:, 20:21], GNS[:, 20:21]).then_inc(ew_dve.sem, 1)

            def group_norm(p):
                wait(ysq_ready.sem, ysq_ready.at(l, p + 1))
                op(dve.tensor_reduce(GNS[:, 4:8], view2(V[:, p, :], NCH), AX.X, ALU.add))
                ts(GNS[:, 8:12], GNS[:, 4:8], 1.0 / HD, GN_EPS, ALU.mult, ALU.add).then_inc(var_ready.sem, 1)
                wait(grstd_ready.sem, grstd_ready.at(l, p + 1))
                for h in range(2):
                    a, b = h * HD, (h + 1) * HD
                    ins = tt(Ybd[a:b, :, a:b], view2(K[a:b, p, :], NCH),
                             GNS[a:b, 12:16].rearrange("p (c o) -> p c o", o=1).to_broadcast([HD, NCH, HD]), ALU.mult)
                ins.then_inc(ybd_ready.sem, 1)

            def y_end(p):
                wait(yt_ready.sem, yt_ready.at(l, p + 1))
                op(tt(V[:, p, :], V[:, p, :], R[:, p, :], ALU.add))
                stt(ZA[:, p, :], V[:, p, :], 0.5, ZA[:, p, :], ALU.mult, ALU.mult).then_inc(ya_ready.sem, 1)

            def masked(o, b, mask):
                return tt(o, quad(b), spread(cv(mask), NCH, P), ALU.mult)

            def grow(p, n):
                tt(flat(X), A[4][:, :], flat(X), ALU.add).then_inc(x_step.sem, 1)

            def rwkv_pair(p, k):
                if k in (0, 1, 2, 5, 6, 7, 9, 12, 15, 17, 20, 23, 26):
                    wait(rwkv_step.sem, rwkv_step.at(l, rw_at(p, k)))
                nxt = p + 1 < HP
                wc = WC[:, (p % 2) * 4:(p % 2) * 4 + 4]
                if k == 0:
                    masked(Qd, A[0], "q_blk")
                    masked(QdT, A[1], "qt_blk")
                    masked(QT32, A[1], "qt_32")
                    masked(QT64, A[1], "qt_64").then_inc(q_masked.sem, 1)
                elif k == 1:
                    masked(Mrb, A[2], "incl")
                    masked(Mak, A[3], "strict_x")
                    masked(Mrk, A[4], "incl_x").then_inc(m_masked.sem, 1)
                elif k == 2:
                    dve.tensor_copy(Vst[0:HD, :, :], quad(A[5])[0:HD, :, HD:P])
                    dve.tensor_copy(Vst[HD:P, :, :], quad(A[5])[HD:P, :, 0:HD]).then_inc(v_ready.sem, 1)
                    if p:
                        group_norm(p - 1)
                elif k == 5:
                    wait(x1_ready.sem, x1_ready.at(l, p + 1))
                    grow(p, 0)
                elif k == 6:
                    tt(view2(R[:, p, :], NCH), view2(A[1][:, 0:S], NCH), VDUP[:, :, 0:CH], ALU.mult
                       ).then_inc(bonus_ready.sem, 1)
                elif k == 7:
                    wait(x_step.sem, x_step.at(l, 4 * p + 1))
                    grow(p, 1)
                    if p:
                        y_end(p - 1)
                elif k == 9:
                    wait(x_step.sem, x_step.at(l, 4 * p + 2))
                    grow(p, 2)
                    if nxt:
                        scan(p + 1)
                elif k == 12:
                    wait(x_step.sem, x_step.at(l, 4 * p + 3))
                    grow(p, 3)
                    if nxt:
                        norm_floor(p + 1)
                elif k == 13 and nxt:
                    values(p + 1)
                elif k == 15:
                    wait(x_step.sem, x_step.at(l, 4 * p + 4))
                    stt(flat(TT), A[4][:, :], -1.0, flat(X), ALU.mult, ALU.subtract).then_inc(t_ready.sem, 1)
                    if nxt:
                        keys(p + 1)
                elif k == 17:
                    chain.settle()
                    ts(Z, A[1][:, 256:256 + CH], wc[:, 0:1], None, ALU.mult).then_inc(z_ready.sem, 1)
                    wait(z_ready.sem, z_ready.at(l, 3 * p + 1))
                    chain.step(ts(Zt, Z, wc[:, 1:2], None, ALU.mult))
                    if nxt:
                        queries(p + 1)
                elif k == 20 or k == 23:
                    c = (k - 17) // 3
                    chain.settle()
                    stt(Z, A[1][:, 256 + c * CH:256 + (c + 1) * CH], wc[:, c:c + 1], Zt, ALU.mult, ALU.add
                        ).then_inc(z_ready.sem, 1)
                    if c == 1:
                        wait(z_ready.sem, z_ready.at(l, 3 * p + 2))
                        chain.step(ts(Zt, Z, wc[:, 2:3], None, ALU.mult))
                elif k == 26:
                    y = view2(A[2][:, 0:S], NCH)
                    op(dve.tensor_reduce(GNS[:, 0:4], y, AX.X, ALU.add))
                    op(ts(GNS[:, 0:4], GNS[:, 0:4], 1.0 / HD, None, ALU.mult))
                    tt(view2(K[:, p, :], NCH), y,
                       GNS[:, 0:4].rearrange("p (c o) -> p c o", o=1).to_broadcast([P, NCH, HD]), ALU.subtract
                       ).then_inc(yc_ready.sem, 1)
                    if not nxt:
                        group_norm(p)

            def rwkv(i):
                if i < HP * RW_STEPS:
                    rwkv_pair(i // RW_STEPS, i % RW_STEPS)

            scan(0)
            norm_floor(0)
            values(0)
            keys(0)
            queries(0)
            for u in range(4):
                for i in range(16):
                    rwkv(16 * u + i)
                silu(4 + u, U_ZA + u, ZA, 2 * u)
            for u in range(8):
                for i in range(16):
                    rwkv(64 + 16 * u + i)
            for u in range(8):
                for i in range(8):
                    rwkv(192 + 8 * u + i)
                wait(*done(l, U_PB + u))
                for v in (U_MGB + u,):
                    wait(*taken(l, v))
                m = flat(MB[:, 2 * u:2 * u + 2, :])
                stt(m, m, 1.0, PB[u % 2][:, :], ALU.add, ALU.mult).then_inc(unit_free[u % 2].sem, 1)
            y_end(HP - 1)
            for j in range(4):
                for i in range(2):
                    u = U_A + 4 * j + 2 + i
                    wait(*done(l, u))
                    wait(*taken(l, U_A + 4 * j + i))
                    g = GAB[:, j % 2, i * 512:(i + 1) * 512]
                    m = flat(MB[:, 4 * j + 2 * i:4 * j + 2 * i + 2, :])
                    stt(g, g, 1.0, PB[u % 2][:, :], ALU.add, ALU.mult).then_inc(unit_free[u % 2].sem, 1)
                    wait(*taken(l, u))
                    tt(m, m, g, ALU.add).then_inc(merged_ready.sem, 1)
            for n in range(4):
                for t in range(2):
                    u = U_WO + 2 * n + t
                    wait(wo_sq.sem, wo_sq.at(l, 2 * n + t + 1))
                    dve.tensor_copy(OUT[:, t, n * 512:(n + 1) * 512], PB[t][:, :]).then_inc(unit_free[t].sem, 1)
            op(dve.tensor_reduce(small[:, 6:8], view2(small[:, 40:48], 2), AX.X, ALU.add))
            ts(small[:, 6:8], small[:, 6:8], 0.25 / D, NORM_EPS, ALU.mult, ALU.add).then_inc(ms2_ready.sem, 1)
            wait(rstd2_ready.sem, rstd2_ready.at(l, 1))
            op(ts(small[:, 10:12], small[:, 8:10], 0.5, None, ALU.mult))
            wait(xr_loaded.sem, xr_loaded.at(l, 32))
            wait(*taken(l, U_WO + 6))
            wait(*taken(l, U_WO + 7))
            for t in range(2):
                chain.step(stt(OUT[:, t, :], OUT[:, t, :], small[:, 10 + t:11 + t], GPOST, ALU.mult, ALU.mult))
            chain.settle()
            for t in range(2):
                ins = tt(XR[:, t, :], XR[:, t, :], OUT[:, t, :], ALU.add)
            ins.then_inc(x_new.sem, 1)

        @block.vector
        def _(dve):
            chain = Chain(dve, dve_chain)
            wait = dve.wait_ge

            def op(ins):
                chain.step(ins)
                chain.settle()

            wait(pos_loaded, 16)
            wait(con_loaded, 16)
            posf, ang, turns = (WORK[:, 8192 + i * S:8192 + (i + 1) * S] for i in range(3))
            op(dve.tensor_copy(posf, WORK[:, 14208:14208 + S].bitcast(I32)))
            op(dve.tensor_scalar(ang, posf, cv("invf"), None, ALU.mult))
            c1 = 6.28125
            c2 = float(np.float32(round((2 * np.pi - c1) * 2 ** 20) / 2 ** 20))
            c3 = float(2 * np.pi - c1 - c2)
            big = 1.5 * 2 ** 23
            for i, shift in enumerate((0.25, 0.0)):
                o = cs[:, i * S:(i + 1) * S]
                op(dve.tensor_scalar(turns, ang, float(1 / (2 * np.pi)), shift, ALU.mult, ALU.add))
                op(dve.tensor_scalar(turns, turns, big, None, ALU.add))
                op(dve.tensor_scalar(turns, turns, big, None, ALU.subtract))
                op(dve.scalar_tensor_tensor(o, turns, -c1, ang, ALU.mult, ALU.add))
                op(dve.scalar_tensor_tensor(o, turns, -c2, o, ALU.mult, ALU.add))
                op(dve.scalar_tensor_tensor(o, turns, -c3, o, ALU.mult, ALU.add))
                if i == 0:
                    op(dve.tensor_scalar(o, o, float(np.pi / 2), None, ALU.add))
                op(dve.tensor_scalar(o, o, 3.1415925, -3.1415925, ALU.min, ALU.max))
            dve.tensor_copy(turns, ang).then_inc(sin_arg, 1)
            wait(table_ready, 1)
            wait(zeroed, 1)
            wait(x_loaded, 16)
            chain.restart()
            with dve.Fori(0, LAYERS) as l:
                dve_layer(dve, l, chain)
                chain.restart()

        def pool_layer(pool, l):
            wait = pool.wait_ge

            def view2(ap, n):
                return ap.rearrange("p (t n) -> p t n", t=n)

            wait(par_loaded.sem, par_loaded.at(l, 16))
            pool.tensor_tensor(ha0, pv("a0"), half8[:, :], ALU.mult)
            pool.tensor_scalar(omu, pv("mu"), -1.0, 1.0, ALU.mult, ALU.add)
            pool.tensor_scalar(nw0, pv("w0"), -1.0, None, ALU.mult)
            pool.tensor_scalar(hv0, pv("v0"), 0.5, None, ALU.mult)
            pool.tensor_copy(view2(w2kd[:, :], 2)[:, :, 0:HD], view2(pv("w2k"), 2))
            pool.tensor_copy(view2(w2kd[:, :], 2)[:, :, HD:P], view2(pv("w2k"), 2)).then_inc(derived_ready.sem, 1)
            wait(ms_ready.sem, ms_ready.at(l, 1))
            pool.tensor_tensor(small[:, 4:6], small[:, 2:4], halves[:, 0:2], ALU.pow).then_inc(rstd_ready.sem, 1)

            for h in range(HEADS):
                b = h % 2
                cf = small[:, 48 + 6 * b:54 + 6 * b]
                wait(cf_ready.sem, cf_ready.at(l, h + 1))
                for n, (s, w) in enumerate(((SC0[:, b, :, :], P), (SC1[:, b, :, :], S), (PC[:, b, :, 0:NCMP], NCMP))):
                    k = cf[:, 2 * n:2 * n + 2].rearrange("p (r o) -> p r o", o=1).to_broadcast([P, 2, w])
                    ins = pool.tensor_tensor(s, s, k, ALU.mult)
                ins.then_inc(probs_ready.sem, 1)

            wait(yb_ready.sem, yb_ready.at(l, HP))
            pool.tensor_tensor(GNS[:, 20:24], halves[:, :], halves[:, :], ALU.subtract)
            for a in (BB, KA, Ybd):
                pool.memset(a, 0.0)
            pool.memset(WORK[:, 0:2048], 0.0)
            pool.memset(GNS[:, 0:20], 0.0).then_inc(pads_zero.sem, 1)
            wait(pads_zero.sem, pads_zero.at(l, 1))

            def before(p):
                wait(scan_done.sem, scan_done.at(l, p + 1))
                pool.tensor_tensor(LPW, LIW, SG, ALU.subtract).then_inc(lp_ready.sem, 1)
                wait(mid_ready.sem, mid_ready.at(l, p + 1))
                wait(decays_ready.sem, decays_ready.at(l, p + 1))
                for h in range(2):
                    a, b = h * HD, (h + 1) * HD
                    pool.tensor_tensor(BB[a:b, :, a:b], view2(BKK[a:b, :], NCH), view2(LIW[a:b, :], NCH), ALU.mult)
                    ins = pool.tensor_tensor(KA[a:b, :, HD - a:P - a], view2(K2[a:b, :], NCH), view2(LIW[a:b, :], NCH),
                                             ALU.mult)
                ins.then_inc(ew_pool.sem, 1)

            def group_rstd(p):
                wait(var_ready.sem, var_ready.at(l, p + 1))
                pool.tensor_tensor(GNS[:, 12:16], GNS[:, 8:12], halves[:, 0:4], ALU.pow).then_inc(grstd_ready.sem, 1)

            before(0)
            for p in range(HP):
                wait(q_masked.sem, q_masked.at(l, p + 1))
                pool.tensor_tensor(X, Qd, spread(cv("ident"), NCH, P), ALU.add).then_inc(x1_ready.sem, 1)
                if p:
                    group_rstd(p - 1)
                if p + 1 < HP:
                    before(p + 1)
            group_rstd(HP - 1)
            wait(ms2_ready.sem, ms2_ready.at(l, 1))
            pool.tensor_tensor(small[:, 8:10], small[:, 6:8], halves[:, 0:2], ALU.pow).then_inc(rstd2_ready.sem, 1)

        @block.gpsimd
        def _(pool):
            pool.memset(VF, 0.0)
            pool.memset(VC, 0.0)
            pool.memset(PC, 0.0)
            pool.memset(small[:, :], 0.0)
            pool.memset(half8[:, :], 0.5)
            pool.memset(halves[:, :], -0.5).then_inc(zeroed, 1)
            pool.wait_ge(zeroed, 1)
            with pool.Fori(0, LAYERS) as l:
                pool_layer(pool, l)


def chunked(w):
    n = w.shape[0] // P
    return np.ascontiguousarray(w.reshape(n, P, -1).transpose(1, 0, 2)).reshape(P, -1)


def weight_stream(w_in, ck_w1, cv_w1, w_a, w_b, w_o):
    shift = 3 * RW + 2 * LORA_W
    za, q = shift, shift + RW
    kv = q + RW
    gate = kv + 6 * NG * HD
    zb = gate + 3 * HEADS
    mg = zb + RW
    col = lambda a, n=256: chunked(w_in[:, a:a + n])
    log = np.zeros((D, 256), np.float32)
    log[:, 0:2 * LORA_W] = w_in[:, 3 * RW:shift]
    log[:, 192:240] = w_in[:, gate:gate + 48]
    vt = np.concatenate([w_in[:, kv + 768:kv + 1024], w_in[:, kv + 1280:kv + 1536]], 1)
    blocks = [chunked(log), col(kv), col(kv + 256), col(kv + 512), col(kv + 1024), chunked(vt[0:1024]),
              chunked(vt[1024:])]
    blocks += [col(q + 256 * i) for i in range(4)]
    blocks += [chunked(ck_w1), chunked(cv_w1)]
    blocks += [col(zb + 256 * i) for i in range(4)]
    for a in (RW, 2 * RW, 0):
        blocks += [col(a + 256 * i) for i in range(4)]
    blocks += [col(za + 256 * i) for i in range(4)]
    blocks += [col(mg + D + 256 * i) for i in range(8)]
    blocks += [chunked(w_b[:, 512 * i:512 * (i + 1)]) for i in range(4)]
    for j in range(4):
        blocks += [col(mg + 512 * j), col(mg + 512 * j + 256), chunked(w_a[:, 512 * j:512 * (j + 1)])]
    blocks += [chunked(w_o[1024 * kh:1024 * (kh + 1), 512 * n:512 * (n + 1)]) for n in range(4) for kh in range(2)]
    assert len(blocks) == NB and all(b.shape == (P, BLK) for b in blocks)
    return np.stack(blocks)


def param_tile(a, l):
    t = np.zeros((P, NPAR), np.float32)

    def put(name, v):
        lo, hi = PAR[name]
        t[0:v.shape[0], lo:hi] = v

    v = max(l - 1, 0)
    cols = lambda w: w.reshape(-1, P).T
    mu = a["rwkv_mu"][l]
    put("w_up", a["rwkv_w_up"][l])
    put("a_up", a["rwkv_a_up"][l])
    put("v_up", a["rwkv_v_up"][v])
    put("v_down", chunked(a["rwkv_v_down"][v]))
    put("w2k", chunked(a["nsa_ck_w2"][l]))
    put("w2v", chunked(a["nsa_cv_w2"][l]))
    m = np.zeros((P, 26), np.float32)
    m[:, 0:24] = np.concatenate([cols(mu[RW:2 * RW]), cols(mu[2 * RW:3 * RW]), cols(mu[0:RW])], 1)
    m[0:LORA_W, 24] = mu[3 * RW:3 * RW + LORA_W]
    m[0:LORA_W, 25] = mu[3 * RW + LORA_W:]
    put("mu", m)
    for name in ("w0", "a0", "k_k", "k_a", "gn_w", "gn_b"):
        put(name, cols(a["rwkv_" + name][l]))
    put("v0", cols(a["rwkv_v0"][v]))
    put("r_k", cols(a["rwkv_r_k"][l].reshape(-1)))
    put("norm_pre", cols(a["norm_pre"][l]))
    put("pe_k", cols(a["nsa_pe_k"][l].reshape(-1)))
    put("pe_v", cols(a["nsa_pe_v"][l].reshape(-1)))
    put("first", np.full((P, 1), 1.0 if l == 0 else 0.0, np.float32))
    return t


def constant_tile():
    t = np.zeros((P, NCON), np.float32)

    def put(name, v):
        lo, hi = CON[name]
        t[0:v.shape[0], lo:hi] = v

    i = np.arange(P)
    put("ident", np.eye(P))
    r, c = i[:, None], i[None, :]
    same = lambda n: r // n == c // n
    put("q_blk", -1.0 * (same(16) & (r < c)))
    put("qt_blk", -1.0 * (same(16) & (r > c)))
    put("qt_32", -1.0 * (same(32) & ~same(16) & (r > c)))
    put("qt_64", -1.0 * (same(64) & ~same(32) & (r > c)))
    rr, cc = r % CH, c % CH
    put("incl", 1.0 * (same(64) & (rr <= cc)))
    put("strict_x", 1.0 * (~same(64) & (rr < cc)))
    put("incl_x", 1.0 * (~same(64) & (rr <= cc)))
    put("ones", 1.0 * same(64))
    put("ident2", 1.0 * (i[:, None] % CH == np.arange(CH)[None, :]))
    rot = np.zeros((P, P))
    half = HD // 8
    for h in range(2):
        for m in range(half):
            rot[h * HD + m + half, h * HD + m] = -1.0
            rot[h * HD + m, h * HD + m + half] = 1.0
    put("rot", rot)
    dup = []
    for gg in range(2):
        d = np.zeros((P, P))
        for m in range(P):
            d[gg * HD + m % HD, m] = 1.0
        dup += [d, d @ rot]
    put("dup", np.concatenate(dup, 1))
    k = np.arange(S)[None, :]
    put("caus0", np.where(k[:, :P] > i[:, None], -1e30, 0.0))
    put("caus1", np.where(k > P + i[:, None], -1e30, 0.0))
    end = np.arange(NCMP)[None, :] * CSTR + CMP - 1
    put("cmpmask", np.concatenate([np.where(end <= t0 + i[:, None], 0.0, -1e30) for t0 in (0, P)], 1))
    put("rowok", 1.0 * (i[:, None] >= CMP - 1))
    inv = np.float32(500000.0) ** (-np.arange(half, dtype=np.float32) * np.float32(2.0 / (HD // 4)))
    f = np.zeros((P, 1), np.float32)
    for h in range(2):
        f[h * HD:h * HD + half, 0] = inv
        f[h * HD + half:h * HD + 2 * half, 0] = inv
    put("invf", f)
    put("inchunk", 1.0 * np.broadcast_to(k % CH != 0, (P, S)))
    return t


def kernel(**inputs):
    import concourse.bacc as bacc
    from concourse.bass_utils import run_bass_kernel_spmd as run

    a = {n: np.asarray(v) for n, v in inputs.items()}
    arrays = {
        "in_x": np.ascontiguousarray(a["x"]),
        "in_positions": np.ascontiguousarray(a["positions"]),
        "in_stream": np.concatenate([weight_stream(a["w_in"][l], a["nsa_ck_w1"][l], a["nsa_cv_w1"][l],
                                                   a["w_proj_a"][l], a["w_proj_b"][l], a["w_out"][l])
                                     for l in range(LAYERS)]),
        "in_params": np.stack([param_tile(a, min(l, LAYERS - 1)) for l in range(LAYERS + 1)]),
        "in_constants": constant_tile(),
        "in_norm_post": np.ascontiguousarray(a["norm_post"]),
    }
    nc = bacc.Bacc("TRN2", target_bir_lowering=False, num_devices=1)
    args = [nc.dram_tensor(n, v.shape, mybir.dt.from_np(v.dtype), kind="ExternalInput").ap()
            for n, v in arrays.items()]
    out = nc.dram_tensor("out_x", (1, S, D), F32, kind="ExternalOutput").ap()
    build(nc, *args, out)
    return run(nc, [arrays], core_ids=[0]).results[0]["out_x"]
```

```python
from contextlib import ExitStack

import numpy as np
import concourse.bass as bass
from concourse import mybir

F32 = mybir.dt.float32
F32R = mybir.dt.float32r
I32 = mybir.dt.int32
ALU = mybir.AluOpType
ACT = mybir.ActivationFunctionType
AX = mybir.AxisListType

P = 128
LAYERS, D, S = 2, 2048, 256
KC = D // P
RW = 1024
HP = RW // P
HEADS = 16
HD = 64
CH = 64
NCH = S // CH
LORA_W = 96
LORA_V = 64
CMP = 32
CSTR = 16
NCMP = (S - CMP) // CSTR + 1
NG = 4
NCG = NCMP * NG
SCALE = HD ** -0.5
DECAY = float(np.exp(-0.5))
GN_EPS, L2_EPS, NORM_EPS = 64e-5, 1e-12, 1e-6

B_LOG, B_KC, B_VC, B_KS, B_KW, B_VT, B_Q, B_CK, B_CV = 0, 1, 2, 3, 4, 5, 7, 11, 12
B_ZB, B_K, B_V, B_R, B_ZA, B_MGB, B_PB, B_A, B_WO = 13, 17, 21, 25, 29, 33, 41, 45, 57
NB = 65
GR = 1024
QG = 4
NGR = NB * QG
SLOTS = 5
assert NGR % SLOTS == 0
LEAD = 2
U_LO, U_GATE, U_KC, U_VC, U_KS, U_KW, U_VT, U_Q, U_ZB = 0, 1, 2, 3, 4, 5, 6, 8, 12
U_K, U_ZA, U_MGB, U_PB, U_A, U_WO, UNITS = 16, 28, 32, 40, 48, 64, 72



def native(g):
    b = g // QG
    return b in (B_CK, B_CV) or B_PB <= b < B_A


def splits(g):
    return sum(not native(i) for i in range(g + 1))


def unit_ended(g):
    b, q = g // QG, g % QG
    if B_PB <= b < B_A:
        return U_PB + 2 * (b - B_PB) + q // 2 if q % 2 else None
    if B_A <= b < B_WO and (b - B_A) % 3 == 2:
        return U_A + 4 * ((b - B_A) // 3) + 2 + q // 2 if q % 2 else None
    if q < QG - 1 or b in (B_VT, B_CK, B_CV):
        return None
    if b == B_LOG:
        return U_GATE
    if b < B_VT:
        return U_KC + b - B_KC
    if b == B_VT + 1:
        return U_VT + 1
    if b < B_CK:
        return U_Q + b - B_Q
    if b < B_PB:
        return U_ZB + b - B_ZB
    if b < B_WO:
        return U_A + 4 * ((b - B_A) // 3) + (b - B_A) % 3
    return U_WO + 2 * ((b - B_WO) // 2) + 1 if (b - B_WO) % 2 else None


def hidden_ended(g):
    return g % QG == QG - 1 and g // QG in (B_CK, B_CV)


def parts(g):
    return sum(unit_ended(i) is None and not hidden_ended(i) for i in range(g + 1))


PAR = {}
_at = 0
for _n, _w in (("v_down", HP * LORA_V), ("w2k", 128), ("w2v", 128),
               ("mu", 26), ("w0", 8), ("a0", 8), ("v0", 8), ("k_k", 8), ("k_a", 8), ("r_k", 8), ("gn_w", 8),
               ("gn_b", 8), ("norm_pre", 16), ("pe_k", 16), ("pe_v", 16)):
    PAR[_n] = (_at, _at + _w)
    _at += _w
NPAR = _at
CON = {}
_at = 0
for _n, _w in (("ident", 128), ("q_blk", 128), ("qt_blk", 128), ("qt_32", 128), ("qt_64", 128), ("incl", 128),
               ("strict_x", 128), ("incl_x", 128), ("ones", 128), ("ident2", 64), ("rowok", 1), ("invf", 1),
               ("inchunk", 256)):
    CON[_n] = (_at, _at + _w)
    _at += _w
NCON = _at
ATT = {}
_at = 0
for _n, _w in (("rot", 128), ("dup", 4 * 128), ("caus0", 128), ("caus1", 256), ("cmpmask", 30)):
    ATT[_n] = (_at, _at + _w)
    _at += _w
NATT = _at

RW_STEPS = 27
PRE_STEPS = 2


def rw_at(p, k):
    return PRE_STEPS + p * RW_STEPS + k + 1


def lora_at(p):
    return 1 if p == 0 else rw_at(p - 1, 9)


def norms_at(p):
    return 2 if p == 0 else rw_at(p - 1, 11)


def rw_granule(i):
    return QG * B_ZA + i // 4


def att_granule(i):
    return QG * B_K + 2 * i + 1


class Signal:

    def __init__(self, sem, per_layer, ahead=0):
        self.sem, self.per_layer, self.ahead = sem, per_layer, ahead

    def at(self, l, n):
        return l * self.per_layer + (n + self.ahead)


class Chain:

    def __init__(self, eng, sem):
        self.eng, self.sem, self.n = eng, sem, 0

    def step(self, ins):
        self.n += 1
        ins.then_inc(self.sem, 1)
        return ins

    def settle(self):
        self.eng.wait_ge(self.sem, self.n)

    def restart(self):
        self.settle()
        self.eng.sem_clear(self.sem)
        self.n = 0


def build(nc, x, pos, stream, params, ups, consts, att_consts, norm_post, v_first, out):
    ctx = ExitStack()
    with ctx:
        used = [-(-nc.sbuf_base // 32) * 32]

        def place(name, cols, at, dt=F32):
            return nc.alloc_sbuf_tensor_at(name, [P, cols], dt, offset=at)

        def sb(name, cols, dt=F32):
            at = used[0]
            used[0] += -(-cols * 4 // 32) * 32
            assert used[0] <= nc.sbuf_usable_end, (name, used[0])
            return place(name, cols, at, dt)

        def sem(name):
            return ctx.enter_context(nc.semaphore(name))

        def signal(name, per_layer, ahead=0):
            return Signal(sem(name), per_layer, ahead)

        def tiles(t, n):
            return t[:, :].rearrange("p (c n) -> p c n", c=n)

        at = used[0]
        hT = [tiles(sb("hT_hi", KC * S, F32R), KC), tiles(sb("hT_lo", KC * S, F32R), KC)]
        OUT = tiles(place("w_out_result", KC * S, at), 2)
        at = used[0]
        w_raw = [sb(f"weights{s}", GR) for s in range(SLOTS)]
        w_lo = [place(f"weights_lo{s}", GR, at + 4 * GR * s, F32R) for s in range(SLOTS)]
        w_hi = [sb(f"weights_hi{s}", GR, F32R) for s in range(SLOTS)]
        at = used[0]
        ZA = tiles(sb("za", HP * S), HP)
        ya_lo = tiles(place("ya_lo", HP * S, at, F32R), HP)
        ZB = tiles(sb("zb", HP * S), HP)
        at = used[0]
        merged = sb("merged", KC * S)
        MB = tiles(merged, KC)
        merged_lo = tiles(place("merged_lo", KC * S, at, F32R), KC)
        at = used[0]
        KVR = [tiles(sb(n, HP * S), HP) for n in ("rk", "rv", "rr")]
        K, V, R = KVR
        ya_hi = tiles(place("ya_hi", HP * S, at, F32R), HP)
        merged_hi = tiles(place("merged_hi", KC * S, at + 4 * HP * S, F32R), KC)
        par = sb("par", NPAR)
        con = sb("con", NCON)
        pair_up = sb("pair_up", 3 * P)
        pair_vf = sb("pair_v_first", S)
        cs = sb("cos_sin", 2 * S)
        derived = sb("derived", 26 + 24)
        w2kd = sb("w2kd", 256)
        gates = sb("gates", HEADS * 6)[:, :].rearrange("p (h i) -> p h i", i=6)
        VC = sb("v_cmp", NG * HD)[:, :].rearrange("p (g d) -> p g d", g=NG)
        PC = sb("p_cmp", 2 * 2 * P)[:, :].rearrange("p (b q k) -> p b q k", b=2, q=2)
        LO = sb("lora_in", 2 * S)
        small = sb("small", 64)
        halves = sb("halves", 4)
        half8 = sb("half8", 8)
        VD = sb("v_down_out", S)
        ZT = sb("z_tanh", 512)
        WORK = sb("work", 13856)

        def pv(name, a=0, b=None):
            lo, hi = PAR[name]
            return par[:, lo + a:(hi if b is None else lo + b)]

        def cv(name, a=0, b=None):
            lo, hi = CON[name]
            return con[:, lo + a:(hi if b is None else lo + b)]

        def av(name, a=0, b=None):
            lo, hi = ATT[name]
            return merged[:, lo + a:(hi if b is None else lo + b)]

        def spread(ap, n, w):
            return ap.rearrange("p (o w) -> p o w", o=1).to_broadcast([P, n, w])

        omu = derived[:, 0:26]
        nw0, ha0, hv0 = (derived[:, 26 + 8 * i:34 + 8 * i] for i in range(3))
        cosT, sinT = cs[:, 0:S], cs[:, S:2 * S]

        def views(*sizes):
            at, res = 0, []
            for w in sizes:
                res.append(WORK[:, at:at + w])
                at += w
            assert at <= 13856, at
            return res

        (QR, KD, KRAW, QRAW, VTM, RT, SC0, SC1, PT, HIDK, HIDV, HT, GS, KCR, KCd) = views(
            2048, 2048, 1024, 1024, 1024, 1024, 512, 1024, 1024, 120, 120, 240, 96, 120, 60)
        QR = QR.rearrange("p (t n) -> p t n", t=HP)
        KD = KD.rearrange("p (t n) -> p t n", t=8)
        X2, XW = merged[:, NATT:NATT + 1024], merged[:, NATT + 1024:NATT + 1024 + 2 * NCG * CMP // 2]
        X2 = X2.rearrange("p (b g n) -> p b g n", b=2, g=NG)
        XW = XW.rearrange("p (b m j) -> p b m j", b=2, m=CMP // 2)
        VTM = VTM.rearrange("p (t n) -> p t n", t=2)
        SC0 = SC0.rearrange("p (b r k) -> p b r k", b=2, r=2)
        SC1 = SC1.rearrange("p (b r k) -> p b r k", b=2, r=2)
        GS = GS.rearrange("p (t n) -> p t n", t=2)

        (KR, BB, KA, Ybd, BBt, KAt, Qd, QdT, QT32, QT64, Mrb, Mak, Mrk, Q2, Q2T, Q4T, X, VDUP, Vst, SG, LPW, LIW,
         Wd, TA, NK, K2, KSQ, TV, VX, WC, Z, Zt, RHS, Uc, GNS) = views(
            2048, 512, 512, 512, 512, 512, 512, 512, 512, 512, 512, 512, 512, 512, 512, 512, 512, 512, 256,
            256, 256, 256, 256, 256, 256, 256, 256, 256, 256, 8, 64, 64, 64, 64, 24)
        KR = KR.rearrange("p (b c n) -> p b c n", b=2, c=NCH)
        BB, KA, Ybd, BBt, KAt, Qd, QdT, QT32, QT64, Mrb, Mak, Mrk, Q2, Q2T, Q4T, X, VDUP = (
            a.rearrange("p (c n) -> p c n", c=NCH)
            for a in (BB, KA, Ybd, BBt, KAt, Qd, QdT, QT32, QT64, Mrb, Mak, Mrk, Q2, Q2T, Q4T, X, VDUP))
        Vst = Vst.rearrange("p (c n) -> p c n", c=NCH)
        TT, XT, WX = Qd, Q2T, Q2
        RKK, BKK = SG, TA
        (XR, XN, GPOST) = views(4096, 4096, 2048)
        XR = XR.rearrange("p (t n) -> p t n", t=2)
        XN = XN.rearrange("p (t n) -> p t n", t=2)
        GAB = WORK[:, 10240:12288].rearrange("p (b n) -> p b n", b=2)
        SQJ = WORK[:, 12288:12800]

        bank = [ctx.enter_context(nc.psum_tensor(f"bank{b}", [P, 512], F32)) for b in range(8)]
        PB, A = bank[0:2], bank[2:8]

        def quad(b):
            return b[:, :].rearrange("p (c n) -> p c n", c=4)

        loaded = [signal(f"granule_loaded{s}", 16 * (NGR // SLOTS)) for s in range(SLOTS)]
        att_loaded = signal("att_constants_loaded", 16)
        v_stored = signal("v_stored", 16)
        pair_loaded = signal("pair_loaded", 32 * HP)
        par_loaded = signal("params_loaded", 16)
        con_loaded = sem("constants_loaded")
        pos_loaded = sem("positions_loaded")
        x_loaded = sem("x_loaded")
        x_copied = sem("x_copied")
        xr_loaded = signal("residual_loaded", 32)
        x_stored = signal("x_stored", 32)
        unit_done = [signal(f"unit_done{b}", UNITS // 2, 1) for b in range(2)]
        part_used = signal("part_used", parts(NGR - 1), SLOTS - 1)
        hT_turned = signal("hT_turned", 8)
        hidden_done = signal("hidden_done", 2)
        cmp_done = signal("cmp_done", 3)
        krope_done = signal("krope_done", 8)
        qrope_done = signal("qrope_done", 4)
        scores_done = signal("scores_done", HEADS)
        probs_turned = signal("probs_turned", HEADS)
        pv_done = signal("pv_done", HEADS)
        vd_done = signal("vd_done", 1)
        rwkv_step = signal("rwkv_step", PRE_STEPS + HP * RW_STEPS + 1)
        unit_free = [signal(f"unit_free{b}", UNITS // 2, 1) for b in range(2)]
        act_chain = sem("act_chain")
        x_squared = signal("x_squared", 1)
        hT_hi_ready = signal("hT_hi_ready", 8)
        hi_ready = signal("weights_hi_ready", splits(NGR - 1))
        ya_hi_ready = signal("ya_hi_ready", 4)
        merged_hi_ready = signal("merged_hi_ready", 8)
        lo_act = signal("lora_inputs_scaled", 1)
        lo_ready = signal("lora_inputs_ready", 1)
        x2_act = signal("x2_act", 2)
        z_tanh = signal("z_tanh", 8)
        kvr_act = signal("kvr_scaled", 12)
        wo_sq = signal("wo_squared", 8)
        hid_sq = signal("hidden_squared", 2)
        hid_tanh = signal("hidden_tanh", 2)
        kcraw_ready = signal("kcraw_ready", 1)
        vc_ready = signal("vc_ready", 1)
        exps_done = signal("exps_done", HEADS)
        pt_act = signal("pt_act", HEADS)
        vd_ready = signal("vd_ready", 1)
        q2_ready = signal("q2_ready", HP)
        tok_ready = signal("bet_kha_tokenmajor", HP)
        q4_ready = signal("q4_ready", HP)
        v1_ready = signal("v1_ready", HP)
        xt_ready = signal("xt_ready", 2 * HP)
        wx_ready = signal("wx_ready", 2 * HP)
        rhs_ready = signal("rhs_ready", NCH * HP)
        u_ready = signal("u_ready", NCH * HP)
        ksq_ready = signal("ksq_ready", HP)
        lora_read = signal("lora_read", HP)
        tv_ready = signal("tv_ready", HP)
        decays_ready = signal("decays_ready", HP)
        sqrt_ready = signal("sqrt_ready", HP)
        ysq_ready = signal("ysq_ready", HP)
        yt_ready = signal("yt_ready", HP)
        dve_chain = sem("dve_chain")
        sin_arg = sem("sin_arg")
        table_ready = sem("table_ready")
        ms_ready = signal("ms_ready", 1)
        xn_ready = signal("xn_ready", 1)
        hT_ready = signal("hT_ready", 8)
        lo_weights = signal("weights_lo_ready", splits(NGR - 1))
        ya_lo_ready = signal("ya_lo_ready", 4)
        merged_lo_ready = signal("merged_lo_ready", 8)
        vf_read = signal("v_first_read", HP)
        xw_ready = signal("xw_ready", 2)
        kd_ready = signal("kd_ready", 8)
        qr_ready = signal("qr_ready", 4)
        hid_arg = signal("hidden_arg", 2)
        hid_ready = signal("hid_ready", 2)
        kc_ready = signal("kc_ready", 1)
        sc_ready = signal("scores_masked", HEADS)
        cf_ready = signal("coef_ready", HEADS)
        pt_dve = signal("pt_dve", HEADS)
        yb_ready = signal("yb_ready", HP)
        q_masked = signal("q_masked", HP)
        m_masked = signal("m_masked", HP)
        v_ready = signal("v_stack_ready", HP)
        x_step = signal("x_step", 4 * HP)
        t_ready = signal("t_ready", HP)
        bonus_ready = signal("bonus_ready", HP)
        z_ready = signal("z_ready", (NCH - 1) * HP)
        scan_done = signal("scan_done", HP)
        n_ready = signal("n_ready", HP)
        mid_ready = signal("mid_ready", HP)
        ew_dve = signal("ew_dve", HP)
        yc_ready = signal("yc_ready", HP)
        var_ready = signal("var_ready", HP)
        ybd_ready = signal("ybd_ready", HP)
        ya_ready = signal("ya_ready", HP)
        merged_ready = signal("merged_ready", 8)
        ms2_ready = signal("ms2_ready", 1)
        x_new = signal("x_new", 1, 1)
        zeroed = sem("zeroed")
        pads_zero = signal("pads_zero", 1)
        derived_ready = signal("derived_ready", 1)
        rstd_ready = signal("rstd_ready", 1)
        probs_ready = signal("probs_ready", HEADS)
        x1_ready = signal("x1_ready", HP)
        lp_ready = signal("lp_ready", HP)
        ew_pool = signal("ew_pool", HP)
        grstd_ready = signal("grstd_ready", HP)
        rstd2_ready = signal("rstd2_ready", 1)

        def taken(l, u):
            return unit_free[u % 2].sem, unit_free[u % 2].at(l, u // 2 + 1)

        def done(l, u):
            return unit_done[u % 2].sem, unit_done[u % 2].at(l, u // 2 + 1)

        block = ctx.enter_context(nc.Block())
        out2 = out.rearrange("a (t p) n -> p (a t) n", p=P)
        x2 = x.rearrange("a (t p) n -> p (a t) n", p=P)

        @block.sync
        def _(sp):
            sp.dma_start(con[:, :], consts).then_inc(con_loaded, 16)
            sp.dma_start(WORK[:, 8192 + 3 * S:8192 + 4 * S].bitcast(I32), pos.to_broadcast([P, S])).then_inc(pos_loaded, 16)
            sp.dma_start(XR, x2).then_inc(x_loaded, 16)
            sp.dma_start(par[:, :], params[0, :, :]).then_inc(par_loaded.sem, 16)
            sp.dma_start(out, x).then_inc(x_copied, 16)


            def used_up(g):
                u = unit_ended(g)
                if u is not None:
                    return unit_done[u % 2], u // 2 + 1
                if hidden_ended(g):
                    return hidden_done, g // QG - B_CK + 1
                return part_used, parts(g)

            with sp.Fori(0, LAYERS) as l:
                def load(g):
                    s = g % SLOTS
                    if g >= SLOTS:
                        before, n = used_up(g - SLOTS)
                    else:
                        before, n = used_up(g - SLOTS + NGR)
                        n -= before.per_layer
                    sp.wait_ge(before.sem, before.at(l, n))
                    sp.dma_start(w_raw[s][:, :], stream[bass.ds(l * NGR + g, 1), :, :].rearrange("a p n -> (a p) n")
                                 ).then_inc(loaded[s].sem, 16)

                def load_pair(p):
                    sp.dma_start(pair_up[:, :], ups[bass.ds(l * HP + p, 1), :, :].rearrange("a p n -> (a p) n")
                                 ).then_inc(pair_loaded.sem, 16)
                    sp.dma_start(pair_vf[:, :], v_first[0, :, p * S:(p + 1) * S]).then_inc(pair_loaded.sem, 16)

                at_pair = {QG * B_ZA + SLOTS: 1}
                for p in range(2, HP):
                    at_pair[rw_granule((p - 2) * RW_STEPS + 13) + SLOTS + 1] = p
                for g in range(NGR):
                    if g == SLOTS:
                        sp.dma_start(merged[:, 0:NATT], att_consts).then_inc(att_loaded.sem, 16)
                    if g == QG * (B_K + 9) + SLOTS:
                        sp.wait_ge(*taken(l, U_K + 6))
                        sp.wait_ge(*taken(l, U_K + 7))
                        sp.dma_start(v_first[bass.ds(l, 1), :, :].rearrange("a p n -> (a p) n"),
                                     V.rearrange("p t n -> p (t n)")).then_inc(v_stored.sem, 16)
                    if g == QG * (B_K + 11) + SLOTS:
                        sp.wait_ge(v_stored.sem, v_stored.at(l, 16))
                        load_pair(0)
                    if g in at_pair:
                        sp.wait_ge(vf_read.sem, vf_read.at(l, at_pair[g]))
                        load_pair(at_pair[g])
                    if g == QG * (B_WO - 2):
                        sp.wait_ge(ya_ready.sem, ya_ready.at(l, HP))
                        sp.wait_ge(x_copied, 16)
                        sp.wait_ge(x_stored.sem, x_stored.at(l, 0) + 1)
                        sp.dma_start(XR, out2).then_inc(xr_loaded.sem, 16)
                        sp.dma_start(GPOST, norm_post[bass.ds(l, 1), :].to_broadcast([P, D])
                                     ).then_inc(xr_loaded.sem, 16)
                        sp.dma_start(par[:, :], params[bass.ds(l + 1, 1), :, :].rearrange("a p n -> (a p) n")
                                     ).then_inc(par_loaded.sem, 16)
                    load(g)
                sp.wait_ge(x_new.sem, x_new.at(l, 1))
                for t in range(2):
                    sp.dma_start(out2[:, t, :], XR[:, t, :]).then_inc(x_stored.sem, 16)
            sp.wait_ge(x_stored.sem, LAYERS * 32 + 1)
            sp.wait_ge(par_loaded.sem, (LAYERS + 1) * 16)

        def pe_layer(pe, l):
            mm = pe.matmul

            def take(g):
                s = g % SLOTS
                if native(g):
                    pe.wait_ge(loaded[s].sem, loaded[s].at(l, 16 * (g // SLOTS + 1)))
                    return [w_raw[s]]
                pe.wait_ge(lo_weights.sem, lo_weights.at(l, splits(g)))
                return [w_hi[s], w_lo[s]]

            def multiply(o, lhs, rhs, start, stop):
                if len(lhs) == 1:
                    return mm(o, lhs[0], rhs[0], start=start, stop=stop)
                mm(o, lhs[0], rhs[0], start=start, stop=False)
                mm(o, lhs[0], rhs[1], start=False, stop=False)
                return mm(o, lhs[1], rhs[0], start=False, stop=stop)

            def part(ins, g):
                if unit_ended(g) is None and not hidden_ended(g):
                    ins.then_inc(part_used.sem, 1)

            def start_unit(u):
                pe.wait_ge(unit_free[u % 2].sem, unit_free[u % 2].at(l, u // 2))
                return PB[u % 2]

            def end_unit(ins, u):
                ins.then_inc(unit_done[u % 2].sem, 1)

            def point(kind, i):
                if kind == "att":
                    attention(i)
                if kind == "rwkv":
                    rwkv(i)

            def product(b, u, rhs, kind=None, first=0, every=16, chunks=KC, tiles=(0, 1)):
                o, n = start_unit(u), 0
                for j, tile in enumerate(tiles):
                    for c in range(chunks):
                        g, i = b * QG + (tile * chunks + c) // 8, c % 8
                        if i == 0:
                            w = take(g)
                        ins = multiply(o[:, j * S:(j + 1) * S], [a[:, i * P:(i + 1) * P] for a in w],
                                       [a[:, c, :] for a in rhs], c == 0, c == chunks - 1)
                        n += 1
                        if n == chunks * len(tiles):
                            end_unit(ins, u)
                        elif i == 7:
                            part(ins, g)
                        if kind and n % every == 0:
                            point(kind, first + n // every - 1)

            pe.wait_ge(xn_ready.sem, xn_ready.at(l, 1))
            for j in range(8):
                if j >= 4:
                    pe.wait_ge(hT_ready.sem, hT_ready.at(l, j - 3))
                for c in (2 * j, 2 * j + 1):
                    for t in range(2):
                        at = (c % 2) * S + t * P
                        ins = pe.transpose(A[j % 4][:, at:at + P], XN[:, t, c * P:(c + 1) * P], cv("ident"))
                ins.then_inc(hT_turned.sem, 1)

            lo_out = start_unit(U_LO), A[4]
            gate_out = start_unit(U_GATE), A[5]
            for q in range(QG):
                pe.wait_ge(hT_ready.sem, hT_ready.at(l, 2 * q + 2))
                w = take(QG * B_LOG + q)
                for j in range(2):
                    for i in range(4):
                        c = 4 * q + i
                        ins = multiply(lo_out[j][0:LORA_W, 0:S],
                                       [a[:, i * 256 + j * LORA_W:i * 256 + (j + 1) * LORA_W] for a in w],
                                       [a[:, c, :] for a in hT], c == 0, c == KC - 1)
                if q == QG - 1:
                    end_unit(ins, U_LO)
                for t in range(2):
                    for i in range(4):
                        c = 4 * q + i
                        ins = multiply(gate_out[t][:, 0:48], [a[:, c, t * P:(t + 1) * P] for a in hT],
                                       [a[:, i * 256 + 192:i * 256 + 240] for a in w], c == 0, c == KC - 1)
                part(ins, QG * B_LOG + q)
            end_unit(ins, U_GATE)

            for b, u in ((B_KC, U_KC), (B_VC, U_VC), (B_KS, U_KS), (B_KW, U_KW)):
                product(b, u, hT)

            def token_major(g0, u0, lhs, ready=None):
                for t in range(2):
                    start_unit(u0 + t)
                for q in range(KC // 2):
                    if ready:
                        pe.wait_ge(ready.sem, ready.at(l, q + 1))
                    w = take(g0 + q)
                    for t in range(2):
                        for i in range(2):
                            c = 2 * q + i
                            ins = multiply(PB[t][:, :], [a[:, c, t * P:(t + 1) * P] for a in lhs],
                                           [a[:, i * 512:(i + 1) * 512] for a in w], c == 0, c == KC - 1)
                        if c == KC - 1:
                            end_unit(ins, u0 + t)
                    part(ins, g0 + q)

            token_major(QG * B_VT, U_VT, hT)

            def k_rope(n):
                src, tile, gg = n // 4, (n % 4) // 2, n % 2
                if n == 0:
                    pe.wait_ge(att_loaded.sem, att_loaded.at(l, 16))
                if n % 4 == 0:
                    pe.wait_ge(*taken(l, U_KS + src))
                if n >= 4:
                    pe.wait_ge(kd_ready.sem, kd_ready.at(l, n - 3))
                raw = KRAW[:, src * 512 + tile * S:src * 512 + (tile + 1) * S]
                for r in range(2):
                    ins = mm(A[n % 4][:, r * S:(r + 1) * S], av("dup", (2 * gg + r) * P, (2 * gg + r + 1) * P), raw,
                             start=True, stop=True)
                ins.then_inc(krope_done.sem, 1)

            def q_rope(j):
                pe.wait_ge(*taken(l, U_Q + j))
                if j >= 2:
                    pe.wait_ge(qr_ready.sem, qr_ready.at(l, j - 1))
                mm(A[4 + j % 2][:, :], av("rot"), QRAW[:, (j % 2) * 512:(j % 2 + 1) * 512], start=True, stop=True
                   ).then_inc(qrope_done.sem, 1)

            for j in range(4):
                product(B_Q + j, U_Q + j, hT)
                k_rope(2 * j)
                k_rope(2 * j + 1)
                if j >= 1:
                    q_rope(j - 1)
            for i in range(2):
                pe.wait_ge(xw_ready.sem, xw_ready.at(l, i + 1))
                if i == 0:
                    pe.wait_ge(kd_ready.sem, kd_ready.at(l, 8))
                for hh in range(2):
                    for m in range(CMP // 2):
                        g = QG * (B_CK + i) + 2 * hh + m // 8
                        if m % 8 == 0:
                            w, = take(g)
                        ins = mm(A[i][:, hh * 64:hh * 64 + NCG], w[:, m % 8 * P:(m % 8 + 1) * P], XW[:, i, m, :],
                                 start=(m == 0), stop=(m == CMP // 2 - 1))
                        if m % 8 == 7:
                            part(ins, g)
                ins.then_inc(hidden_done.sem, 1)
            q_rope(3)
            product(B_ZB, U_ZB, hT)
            pe.wait_ge(hid_ready.sem, hid_ready.at(l, 1))
            pe.wait_ge(derived_ready.sem, derived_ready.at(l, 1))
            for hh in range(2):
                ins = mm(A[2][:, 0:NCG], w2kd[:, hh * P:(hh + 1) * P], HIDK[:, hh * NCG:(hh + 1) * NCG],
                         start=(hh == 0), stop=(hh == 1))
            ins.then_inc(cmp_done.sem, 1)
            product(B_ZB + 1, U_ZB + 1, hT)
            pe.wait_ge(kcraw_ready.sem, kcraw_ready.at(l, 1))
            mm(A[2][:, 64:64 + NCG], av("rot"), KCR[:, 0:NCG], start=True, stop=True).then_inc(cmp_done.sem, 1)
            pe.wait_ge(hid_ready.sem, hid_ready.at(l, 2))
            for g in range(NG):
                for hh in range(2):
                    ins = mm(A[3][0:NCMP, g * HD:(g + 1) * HD],
                             HIDV[:, hh * NCG + g * NCMP:hh * NCG + (g + 1) * NCMP],
                             pv("w2v", hh * HD, (hh + 1) * HD), start=(hh == 0), stop=(hh == 1))
            ins.then_inc(cmp_done.sem, 1)
            product(B_ZB + 2, U_ZB + 2, hT)
            product(B_ZB + 3, U_ZB + 3, hT)
            pe.wait_ge(qr_ready.sem, qr_ready.at(l, 4))
            pe.wait_ge(kc_ready.sem, kc_ready.at(l, 1))
            pe.wait_ge(vc_ready.sem, vc_ready.at(l, 1))
            pe.wait_ge(*taken(l, U_VT))
            pe.wait_ge(*taken(l, U_VT + 1))

            def scores(h):
                g, tile, a = h // 4, h // 2, (h % 2) * HD
                if h >= 1:
                    pe.wait_ge(sc_ready.sem, sc_ready.at(l, h))
                for qt in range(2):
                    q = QR[a:a + HD, tile, qt * P:(qt + 1) * P]
                    n = P * (qt + 1)
                    for r in range(2):
                        mm(A[qt][:, r * n:(r + 1) * n], q, KD[a:a + HD, 4 * r + g, 0:n], start=True, stop=True)
                for qt in range(2):
                    q = QR[a:a + HD, tile, qt * P:(qt + 1) * P]
                    ins = mm(A[0][:, 256 + 16 * qt:256 + 16 * qt + NCMP], q, KCd[a:a + HD, g * NCMP:(g + 1) * NCMP],
                             start=True, stop=True)
                ins.then_inc(scores_done.sem, 1)

            def turn_probs(h):
                pe.wait_ge(probs_ready.sem, probs_ready.at(l, h + 1))
                if h >= 1:
                    pe.wait_ge(pt_act.sem, pt_act.at(l, h))
                    pe.wait_ge(pt_dve.sem, pt_dve.at(l, h))
                b = h % 2
                for r in range(2):
                    pe.transpose(A[2 + r][:, 0:128], SC0[:, b, r, :], cv("ident"))
                    pe.transpose(A[2 + r][:, 128:256], SC1[:, b, r, 0:128], cv("ident"))
                    pe.transpose(A[2 + r][:, 256:384], SC1[:, b, r, 128:256], cv("ident"))
                    ins = pe.transpose(A[2 + r][:, 384:512], PC[:, b, r, :], cv("ident"))
                ins.then_inc(probs_turned.sem, 1)

            def weigh_values(h):
                g, a = h // 4, (h % 2) * HD
                pe.wait_ge(pt_act.sem, pt_act.at(l, h + 1))
                pe.wait_ge(pt_dve.sem, pt_dve.at(l, h + 1))
                if h >= 4 and h % 2 == 0:
                    pe.wait_ge(yb_ready.sem, yb_ready.at(l, h // 2 - 1))
                full, lo, hi = (A[4 + (h // 2) % 2][a:a + HD, s:e] for s, e in ((0, S), (0, P), (P, S)))
                mm(full, VTM[:, 0, g * HD:(g + 1) * HD], PT[:, 0:256], start=True, stop=False)
                mm(hi, VTM[:, 1, g * HD:(g + 1) * HD], PT[:, 256:384], start=False, stop=False)
                mm(lo, VC[:, g, :], PT[:, 384:512], start=False, stop=False)
                mm(full, VTM[:, 0, 256 + g * HD:256 + (g + 1) * HD], PT[:, 512:768], start=False, stop=False)
                mm(hi, VTM[:, 1, 256 + g * HD:256 + (g + 1) * HD], PT[:, 768:896], start=False, stop=False)
                mm(hi, VC[:, g, :], PT[:, 896:1024], start=False, stop=True).then_inc(pv_done.sem, 1)

            def attention(i):
                if 2 <= i < HEADS + 2:
                    weigh_values(i - 2)
                if 1 <= i < HEADS + 1:
                    turn_probs(i - 1)
                if i < HEADS:
                    scores(i)
                if i == 20:
                    pe.wait_ge(yb_ready.sem, yb_ready.at(l, HP))
                    pe.wait_ge(*taken(l, U_K + 6))
                    pe.wait_ge(*taken(l, U_K + 7))
                    for c in range(HP):
                        ins = mm(A[5][0:LORA_V, 0:S], pv("v_down", c * LORA_V, (c + 1) * LORA_V), V[:, c, :],
                                 start=(c == 0), stop=(c == HP - 1))
                    ins.then_inc(vd_done.sem, 1)

            for u in range(12):
                product(B_K + u, U_K + u, hT, "att", 2 * u)

            def lora(p):
                pe.wait_ge(pair_loaded.sem, pair_loaded.at(l, 32 * (p + 1)))
                mm(A[3][:, 0:S], pair_up[0:LORA_W, 0:P], LO[0:LORA_W, 0:S], start=True, stop=True)
                return mm(A[3][:, S:2 * S], pair_up[0:LORA_W, P:2 * P], LO[0:LORA_W, S:2 * S], start=True, stop=True)

            def norms(p):
                mm(A[1][:, 0:S], pair_up[0:LORA_V, 2 * P:3 * P], VD[0:LORA_V, :], start=True, stop=True)
                pe.wait_ge(ksq_ready.sem, ksq_ready.at(l, p + 1))
                return mm(A[1][:, S:2 * S], cv("ones"), KSQ, start=True, stop=True)

            def four(o, lhs, rhs, turn=False):
                for c in range(NCH):
                    if turn:
                        ins = pe.transpose(quad(o)[:, c, :], lhs[:, c, :], cv("ident"))
                    else:
                        ins = mm(quad(o)[:, c, :], lhs[:, c, :], rhs[:, c, :], start=True, stop=True)
                return ins

            def turn_y(p):
                pe.wait_ge(ybd_ready.sem, ybd_ready.at(l, p + 1))
                for c in range(NCH):
                    ins = mm(A[2][:, c * CH:(c + 1) * CH], Ybd[:, c, :], cv("ident2"), start=True, stop=True)
                return ins

            def rwkv_pair(p, k):
                kap, rho = KR[:, p % 2, :, 0:P], KR[:, p % 2, :, P:2 * P]
                wait = pe.wait_ge
                if k == 0:
                    wait(ew_dve.sem, ew_dve.at(l, p + 1))
                    wait(ew_pool.sem, ew_pool.at(l, p + 1))
                    if p:
                        wait(z_ready.sem, z_ready.at(l, 3 * p))
                    four(A[0], BB, kap)
                    ins = four(A[1], kap, BB)
                elif k == 1:
                    if p:
                        wait(yc_ready.sem, yc_ready.at(l, p))
                    four(A[2], BB, rho)
                    four(A[3], KA, kap)
                    ins = four(A[4], KA, rho)
                elif k == 2:
                    ins = four(A[5], VDUP, None, True)
                elif k == 3:
                    wait(q_masked.sem, q_masked.at(l, p + 1))
                    four(A[0], QdT, Qd)
                    ins = four(A[1], Qd, QdT)
                elif k == 4:
                    wait(m_masked.sem, m_masked.at(l, p + 1))
                    four(A[2], BB, None, True)
                    ins = four(A[3], KA, None, True)
                elif k == 5:
                    wait(q2_ready.sem, q2_ready.at(l, p + 1))
                    wait(x1_ready.sem, x1_ready.at(l, p + 1))
                    four(A[4], Q2T, X)
                    ins = four(A[0], Q2, Q2T)
                elif k == 6:
                    ins = mm(A[1][:, 0:S], cv("ones"), RKK, start=True, stop=True)
                elif k == 7:
                    wait(q4_ready.sem, q4_ready.at(l, p + 1))
                    wait(x_step.sem, x_step.at(l, 4 * p + 1))
                    ins = four(A[4], Q4T, X)
                    if p:
                        wait(tok_ready.sem, tok_ready.at(l, p + 1))
                        ins = turn_y(p - 1)
                elif k == 8:
                    wait(x_step.sem, x_step.at(l, 4 * p + 2))
                    wait(v_ready.sem, v_ready.at(l, p + 1))
                    ins = four(A[5], Q4T, X)
                elif k == 9:
                    wait(v1_ready.sem, v1_ready.at(l, p + 1))
                    ins = four(A[4], Q4T, WX)
                    if p + 1 < HP:
                        wait(tok_ready.sem, tok_ready.at(l, p + 1))
                        ins = lora(p + 1)
                elif k == 10 or k == 13:
                    wait(x_step.sem, x_step.at(l, 4 * p + (3 if k == 10 else 4)))
                    ins = four(A[5], X, None, True)
                elif k == 11:
                    ins = four(A[0], QT32, X)
                    if p + 1 < HP:
                        wait(bonus_ready.sem, bonus_ready.at(l, p + 1))
                        ins = norms(p + 1)
                elif k == 12:
                    wait(xt_ready.sem, xt_ready.at(l, 2 * p + 1))
                    wait(wx_ready.sem, wx_ready.at(l, 2 * p + 1))
                    ins = four(A[4], XT, WX)
                elif k == 14:
                    four(A[0], QT64, X)
                    if p + 1 < HP:
                        wait(lora_read.sem, lora_read.at(l, p + 2))
                    else:
                        wait(tok_ready.sem, tok_ready.at(l, p + 1))
                    ins = mm(A[3][:, 0:CH], Mak[:, 0, :], Vst[:, 0, :], start=True, stop=True)
                elif k == 15:
                    wait(xt_ready.sem, xt_ready.at(l, 2 * p + 2))
                    wait(wx_ready.sem, wx_ready.at(l, 2 * p + 2))
                    ins = four(A[4], XT, WX)
                elif k % 3 == 0:
                    c = (k - 15) // 3
                    wait(z_ready.sem, z_ready.at(l, 3 * p + c))
                    mm(A[3][:, c * CH:(c + 1) * CH], kap[:, c, :], Z, start=True, stop=False)
                    ins = mm(A[3][:, c * CH:(c + 1) * CH], Mak[:, c, :], Vst[:, c, :], start=False, stop=True)
                elif k % 3 == 1:
                    c = (k - 16) // 3
                    if c == 0:
                        wait(t_ready.sem, t_ready.at(l, p + 1))
                    wait(rhs_ready.sem, rhs_ready.at(l, NCH * p + c + 1))
                    ins = mm(A[3][:, 256 + c * CH:256 + (c + 1) * CH], TT[:, c, :], RHS, start=True, stop=True)
                else:
                    c = (k - 17) // 3
                    y, z = A[2][:, c * CH:(c + 1) * CH], A[1][:, 256 + c * CH:256 + (c + 1) * CH]
                    wait(u_ready.sem, u_ready.at(l, NCH * p + c + 1))
                    if c == 0:
                        wait(tok_ready.sem, tok_ready.at(l, p + 1))
                        if p:
                            wait(yt_ready.sem, yt_ready.at(l, p))
                        if p + 1 < HP:
                            wait(tv_ready.sem, tv_ready.at(l, p + 2))
                            wait(n_ready.sem, n_ready.at(l, p + 2))
                    else:
                        mm(y, rho[:, c, :], Z, start=True, stop=False)
                    mm(y, Mrb[:, c, :], Uc, start=(c == 0), stop=False)
                    ins = mm(y, Mrk[:, c, :], Vst[:, c, :], start=False, stop=True)
                    if c + 1 < NCH:
                        mm(z, BBt[:, c, :], Uc, start=True, stop=False)
                        ins = mm(z, KAt[:, c, :], Vst[:, c, :], start=False, stop=True)
                ins.then_inc(rwkv_step.sem, 1)

            def rwkv(i):
                if i < HP * RW_STEPS:
                    rwkv_pair(i // RW_STEPS, i % RW_STEPS)

            pe.wait_ge(lo_ready.sem, lo_ready.at(l, 1))
            pe.wait_ge(yb_ready.sem, yb_ready.at(l, HP))
            lora(0).then_inc(rwkv_step.sem, 1)
            pe.wait_ge(vd_ready.sem, vd_ready.at(l, 1))
            norms(0).then_inc(rwkv_step.sem, 1)
            for u in range(4):
                product(B_ZA + u, U_ZA + u, hT, "rwkv", 16 * u, 2)
            for u in range(8):
                product(B_MGB + u, U_MGB + u, hT, "rwkv", 64 + 16 * u, 2)
            for u in range(8):
                product(B_PB + u // 2, U_PB + u, [ZB], "rwkv", 192 + 8 * u, 2, HP, (2 * (u % 2), 2 * (u % 2) + 1))
            turn_y(HP - 1).then_inc(rwkv_step.sem, 1)

            for j in range(4):
                product(B_A + 3 * j, U_A + 4 * j, hT)
                product(B_A + 3 * j + 1, U_A + 4 * j + 1, hT)
                if j == 0:
                    pe.wait_ge(ya_lo_ready.sem, ya_lo_ready.at(l, 4))
                for i in range(2):
                    product(B_A + 3 * j + 2, U_A + 4 * j + 2 + i, [ya_hi, ya_lo], None, 0, 16, HP, (2 * i, 2 * i + 1))
            for n in range(4):
                token_major(QG * (B_WO + 2 * n), U_WO + 2 * n, [merged_hi, merged_lo],
                            merged_lo_ready if n == 0 else None)

        @block.tensor
        def _(pe):
            for s in unit_done + unit_free + [part_used]:
                pe.sem_inc(s.sem, s.ahead)
            pe.sem_inc(x_stored.sem, 1)
            pe.sem_inc(x_new.sem, 1)
            pe.wait_ge(con_loaded, 16)
            pe.wait_ge(zeroed, 1)
            with pe.Fori(0, LAYERS) as l:
                pe_layer(pe, l)

        def act_layer(act, l, chain):
            wait = act.wait_ge

            def copy(o, i, scale=1.0):
                return act.activation(o, i, ACT.Copy, scale=scale)

            def flat(a):
                return a.rearrange("p a b -> p (a b)")

            split_next = [0]

            def split_to(last):
                for g in range(split_next[0], min(last, NGR - 1) + 1):
                    if not native(g):
                        s = g % SLOTS
                        wait(loaded[s].sem, loaded[s].at(l, 16 * (g // SLOTS + 1)))
                        copy(w_hi[s][:, :], w_raw[s][:, :]).then_inc(hi_ready.sem, 1)
                    split_next[0] = g + 1

            def behind(g):
                split_to(g + LEAD)

            wait(x_new.sem, x_new.at(l, 0))
            for t in range(2):
                chain.step(act.activation(XN[:, t, :], XR[:, t, :], ACT.Square, accum_out=small[:, t:t + 1]))
            chain.settle()
            act.activation(small[:, 60:61], small[:, 0:1], ACT.Copy).then_inc(x_squared.sem, 1)
            wait(par_loaded.sem, par_loaded.at(l, 16))
            split_to(2)
            for j in range(8):
                wait(hT_turned.sem, hT_turned.at(l, j + 1))
                for c in range(2):
                    ins = copy(hT[0][:, 2 * j + c, :], A[j % 4][:, c * S:(c + 1) * S],
                               pv("norm_pre", 2 * j + c, 2 * j + c + 1))
                ins.then_inc(hT_hi_ready.sem, 1)
            behind(QG * B_LOG + 3)
            wait(derived_ready.sem, derived_ready.at(l, 1))
            wait(*done(l, U_LO))
            for j in range(2):
                ins = copy(LO[0:LORA_W, j * S:(j + 1) * S], (PB[0], A[4])[j][0:LORA_W, 0:S],
                           omu[0:LORA_W, 24 + j:25 + j])
            ins.then_inc(lo_act.sem, 1)
            wait(*done(l, U_GATE))
            act.activation(GS[:, 1, :], A[5][:, 0:48], ACT.Tanh, scale=0.5)
            act.activation(GS[:, 0, :], PB[1][:, 0:48], ACT.Tanh, scale=0.5).then_inc(unit_free[1].sem, 1)
            wait(*taken(l, U_LO))
            act.activation(LO[0:LORA_W, 0:S], LO[0:LORA_W, 0:S], ACT.Tanh).then_inc(lo_ready.sem, 1)

            for i in range(2):
                u = U_KC + i
                behind(QG * (B_KC + i) + 3)
                wait(*done(l, u))
                src = PB[u % 2][:, :].rearrange("p (t n r) -> p t n r", t=2, r=2)
                for gg in range(2):
                    ins = copy(X2[0:HD, i, gg::2, :], src[gg * HD:(gg + 1) * HD, :, :, 0])
                ins.then_inc(x2_act.sem, 1)
            for i in range(2):
                u = U_KS + i
                behind(QG * (B_KS + i) + 3)
                wait(*done(l, u))
                copy(KRAW[:, i * 512:(i + 1) * 512], PB[u % 2][:, :]).then_inc(unit_free[u % 2].sem, 1)
            for t in range(2):
                u = U_VT + t
                behind(QG * B_VT + 7)
                wait(*done(l, u))
                copy(VTM[:, t, :], PB[u % 2][:, :]).then_inc(unit_free[u % 2].sem, 1)
            for j in range(4):
                u = U_Q + j
                behind(QG * (B_Q + j) + 3)
                wait(*done(l, u))
                if j >= 2:
                    wait(qr_ready.sem, qr_ready.at(l, j - 1))
                copy(QRAW[:, (j % 2) * 512:(j % 2 + 1) * 512], PB[u % 2][:, :]).then_inc(unit_free[u % 2].sem, 1)
            behind(QG * B_CV + 3)
            for i in range(2):
                wait(hidden_done.sem, hidden_done.at(l, i + 1))
                if i:
                    wait(hid_ready.sem, hid_ready.at(l, 1))
                x = A[i][:, 0:128].rearrange("p (h n) -> p h n", h=2)[:, :, 0:NCG]
                act.activation(HT[:, 0:120].rearrange("p (h n) -> p h n", h=2), x, ACT.Square
                               ).then_inc(hid_sq.sem, 1)
                wait(hid_arg.sem, hid_arg.at(l, i + 1))
                act.activation(HT[:, 120:240], HT[:, 0:120], ACT.Tanh, scale=float(np.sqrt(2 / np.pi))
                               ).then_inc(hid_tanh.sem, 1)

            def z_pass(i, u):
                behind(QG * (B_ZB + i if i < 4 else B_ZA + i - 4) + 3)
                wait(*done(l, u))
                if i >= 1:
                    wait(*taken(l, u - 1))
                act.activation(ZT[:, :], PB[u % 2][:, :], ACT.Tanh, scale=0.5).then_inc(z_tanh.sem, 1)

            z_pass(0, U_ZB)
            wait(cmp_done.sem, cmp_done.at(l, 1))
            copy(KCR[:, 0:NCG], A[2][:, 0:NCG], 0.5).then_inc(kcraw_ready.sem, 1)
            z_pass(1, U_ZB + 1)
            wait(cmp_done.sem, cmp_done.at(l, 3))
            wait(zeroed, 1)
            copy(flat(VC)[0:NCMP, :], A[3][0:NCMP, 0:256], 0.5).then_inc(vc_ready.sem, 1)
            z_pass(2, U_ZB + 2)
            z_pass(3, U_ZB + 3)

            def attention(i):
                behind(att_granule(i))
                if 1 <= i < HEADS + 1:
                    wait(probs_turned.sem, probs_turned.at(l, i))
                    copy(PT[:, 0:512], A[2][:, :]).then_inc(pt_act.sem, 1)
                if i < HEADS:
                    b = i % 2
                    wait(sc_ready.sem, sc_ready.at(l, i + 1))
                    for n, s in enumerate((SC0[:, b, 0, :], SC0[:, b, 1, :], SC1[:, b, 0, :], SC1[:, b, 1, :],
                                           PC[:, b, 0, 0:NCMP], PC[:, b, 1, 0:NCMP])):
                        ins = act.activation(s, s, ACT.Exp, bias=small[:, 12 + 6 * b + n:13 + 6 * b + n],
                                             accum_out=small[:, 24 + 6 * b + n:25 + 6 * b + n])
                        chain.step(ins)
                    chain.settle()
                    act.activation(small[:, 61:62], small[:, 24:25], ACT.Copy).then_inc(exps_done.sem, 1)
                if i == 21:
                    wait(vd_done.sem, vd_done.at(l, 1))
                    copy(VD[0:LORA_V, :], A[5][0:LORA_V, 0:S]).then_inc(vd_ready.sem, 1)

            for u in range(12):
                attention(2 * u)
                behind(QG * (B_K + u) + 3)
                wait(*done(l, U_K + u))
                for t in range(2):
                    n = 2 * u + t
                    ins = copy(KVR[n // 8][:, n % 8, :], PB[u % 2][:, t * S:(t + 1) * S], omu[:, n:n + 1])
                ins.then_inc(kvr_act.sem, 1)
                attention(2 * u + 1)

            def kk_square(p):
                act.activation(KSQ, K[:, p, :], ACT.Square, scale=pv("k_k", p, p + 1)).then_inc(ksq_ready.sem, 1)

            def lora_pass(p):
                wait(rwkv_step.sem, rwkv_step.at(l, lora_at(p)))
                act.activation(SG, A[3][:, 0:S], ACT.Exp, bias=nw0[:, p:p + 1], scale=-1.0)
                act.activation(TA, A[3][:, S:2 * S], ACT.Tanh, bias=ha0[:, p:p + 1], scale=0.5
                               ).then_inc(lora_read.sem, 1)

            def tv_pass(p):
                wait(rwkv_step.sem, rwkv_step.at(l, norms_at(p)))
                act.activation(TV, A[1][:, 0:S], ACT.Tanh, bias=hv0[:, p:p + 1], scale=0.5).then_inc(tv_ready.sem, 1)

            def decays(p):
                wait(lp_ready.sem, lp_ready.at(l, p + 1))
                chain.step(act.activation(Wd, LIW, ACT.Exp, scale=-DECAY))
                act.activation(LPW, LPW, ACT.Exp, scale=-DECAY)
                chain.settle()
                act.activation(LIW, LIW, ACT.Exp, scale=DECAY).then_inc(decays_ready.sem, 1)

            def kk_norm(p):
                wait(n_ready.sem, n_ready.at(l, p + 1))
                act.activation(NK, NK, ACT.Sqrt).then_inc(sqrt_ready.sem, 1)

            def y_pass(p):
                act.activation(V[:, p, :], A[2][:, 0:S], ACT.Identity, bias=pv("gn_b", p, p + 1),
                               scale=pv("gn_w", p, p + 1)).then_inc(yt_ready.sem, 1)

            def rwkv_pair(p, k):
                if k in (3, 4, 5, 7, 8, 9, 10, 11, 13, 14) or k >= 16:
                    wait(rwkv_step.sem, rwkv_step.at(l, rw_at(p, k)))
                nxt = p + 1 < HP
                if k == 3:
                    copy(flat(Q2), A[0][:, :])
                    copy(flat(Q2T), A[1][:, :]).then_inc(q2_ready.sem, 1)
                elif k == 4:
                    copy(flat(BBt), A[2][:, :])
                    copy(flat(KAt), A[3][:, :]).then_inc(tok_ready.sem, 1)
                elif k == 5:
                    copy(flat(Q4T), A[0][:, :]).then_inc(q4_ready.sem, 1)
                elif k == 7 and p:
                    y_pass(p - 1)
                elif k == 8:
                    copy(flat(WX), A[5][:, :]).then_inc(v1_ready.sem, 1)
                    if nxt:
                        kk_square(p + 1)
                elif k == 9 and nxt:
                    lora_pass(p + 1)
                elif k == 10 or k == 13:
                    copy(flat(XT), A[5][:, :]).then_inc(xt_ready.sem, 1)
                elif k == 11:
                    copy(flat(WX), A[0][:, :]).then_inc(wx_ready.sem, 1)
                    if nxt:
                        tv_pass(p + 1)
                elif k == 12 and nxt:
                    decays(p + 1)
                elif k == 14:
                    copy(flat(WX), A[0][:, :]).then_inc(wx_ready.sem, 1)
                    copy(RHS, A[3][:, 0:CH]).then_inc(rhs_ready.sem, 1)
                    if nxt:
                        kk_norm(p + 1)
                elif k >= 16 and k % 3 == 1:
                    c = (k - 16) // 3
                    copy(Uc, A[3][:, 256 + c * CH:256 + (c + 1) * CH]).then_inc(u_ready.sem, 1)
                elif k >= 16 and k % 3 == 0:
                    c = (k - 15) // 3
                    copy(RHS, A[3][:, c * CH:(c + 1) * CH]).then_inc(rhs_ready.sem, 1)
                elif k == 26:
                    wait(yc_ready.sem, yc_ready.at(l, p + 1))
                    act.activation(V[:, p, :], K[:, p, :], ACT.Square).then_inc(ysq_ready.sem, 1)

            def rwkv(i):
                behind(rw_granule(i))
                if i < HP * RW_STEPS:
                    rwkv_pair(i // RW_STEPS, i % RW_STEPS)

            wait(yb_ready.sem, yb_ready.at(l, HP))
            wait(*taken(l, U_K + 10))
            wait(*taken(l, U_K + 11))
            split_to(QG * B_ZA + 1)
            kk_square(0)
            lora_pass(0)
            tv_pass(0)
            decays(0)
            kk_norm(0)
            for u in range(4):
                for i in range(16):
                    rwkv(16 * u + i)
                z_pass(4 + u, U_ZA + u)
            for u in range(8):
                for i in range(16):
                    rwkv(64 + 16 * u + i)
                wait(*done(l, U_MGB + u))
                act.activation(flat(MB[:, 2 * u:2 * u + 2, :]), PB[u % 2][:, :], ACT.Tanh, scale=0.5
                               ).then_inc(unit_free[u % 2].sem, 1)
            for i in range(192, 256):
                rwkv(i)
            behind(QG * B_A - 1)
            wait(rwkv_step.sem, rwkv_step.at(l, rw_at(HP, 0)))
            y_pass(HP - 1)

            wait(ya_ready.sem, ya_ready.at(l, HP))
            for n in range(4):
                copy(flat(ya_hi[:, 2 * n:2 * n + 2, :]), flat(ZA[:, 2 * n:2 * n + 2, :])).then_inc(ya_hi_ready.sem, 1)

            def merged_high(j):
                for n in (2 * j, 2 * j + 1):
                    wait(merged_ready.sem, merged_ready.at(l, n + 1))
                    copy(flat(merged_hi[:, 2 * n:2 * n + 2, :]), flat(MB[:, 2 * n:2 * n + 2, :])
                         ).then_inc(merged_hi_ready.sem, 1)

            for j in range(4):
                if j >= 2:
                    wait(merged_ready.sem, merged_ready.at(l, 2 * j - 2))
                for i in range(2):
                    u = U_A + 4 * j + i
                    behind(QG * (B_A + 3 * j + i) + 3)
                    wait(*done(l, u))
                    act.activation(GAB[:, j % 2, i * 512:(i + 1) * 512], PB[u % 2][:, :], ACT.Tanh, scale=0.5
                                   ).then_inc(unit_free[u % 2].sem, 1)
                if j:
                    merged_high(j - 1)
            behind(QG * (B_A + 11) + 3)
            merged_high(3)
            for n in range(4):
                behind(QG * (B_WO + 2 * n) + 7)
                for t in range(2):
                    u = U_WO + 2 * n + t
                    wait(*done(l, u))
                    chain.step(act.activation(SQJ, PB[t][:, :], ACT.Square,
                                              accum_out=small[:, 40 + 4 * t + n:41 + 4 * t + n]))
                    chain.settle()
                    act.activation(small[:, 62:63], small[:, 0:1], ACT.Copy).then_inc(wo_sq.sem, 1)

        @block.scalar
        def _(act):
            chain = Chain(act, act_chain)
            act.wait_ge(sin_arg, 1)
            act.activation(cs[:, :], cs[:, :], ACT.Sin).then_inc(table_ready, 1)
            act.wait_ge(x_loaded, 16)
            act.wait_ge(zeroed, 1)
            with act.Fori(0, LAYERS) as l:
                act_layer(act, l, chain)
                chain.restart()

        def dve_layer(dve, l, chain):
            wait = dve.wait_ge
            stt, tt, ts = dve.scalar_tensor_tensor, dve.tensor_tensor, dve.tensor_scalar

            def op(ins):
                chain.step(ins)
                chain.settle()

            def flat(a):
                return a.rearrange("p a b -> p (a b)")

            def view2(ap, n):
                return ap.rearrange("p (t n) -> p t n", t=n)

            split_next = [0]

            def split_to(last):
                for g in range(split_next[0], min(last, NGR - 1) + 1):
                    if not native(g):
                        s = g % SLOTS
                        wait(hi_ready.sem, hi_ready.at(l, splits(g)))
                        tt(w_lo[s][:, :], w_raw[s][:, :], w_hi[s][:, :].bitcast(F32), ALU.subtract
                           ).then_inc(lo_weights.sem, 1)
                    split_next[0] = g + 1

            def behind(g):
                split_to(g + LEAD)

            def low(o, whole, hi):
                return tt(flat(o), flat(whole), flat(hi).bitcast(F32), ALU.subtract)

            wait(x_squared.sem, x_squared.at(l, 1))
            ts(small[:, 2:4], small[:, 0:2], 1.0 / D, NORM_EPS, ALU.mult, ALU.add).then_inc(ms_ready.sem, 1)
            wait(rstd_ready.sem, rstd_ready.at(l, 1))
            for t in range(2):
                ins = ts(XN[:, t, :], XR[:, t, :], small[:, 4 + t:5 + t], None, ALU.mult)
            ins.then_inc(xn_ready.sem, 1)
            wait(par_loaded.sem, par_loaded.at(l, 16))
            split_to(2)
            for j in range(8):
                wait(hT_hi_ready.sem, hT_hi_ready.at(l, j + 1))
                for c in range(2):
                    ins = stt(hT[1][:, 2 * j + c, :], A[j % 4][:, c * S:(c + 1) * S],
                              pv("norm_pre", 2 * j + c, 2 * j + c + 1), hT[0][:, 2 * j + c, :].bitcast(F32),
                              ALU.mult, ALU.subtract)
                ins.then_inc(hT_ready.sem, 1)
            behind(QG * B_LOG + 3)
            wait(lo_act.sem, lo_act.at(l, 1))
            for j in range(2):
                ins = stt(LO[0:LORA_W, j * S + 1:(j + 1) * S], (PB[0], A[4])[j][0:LORA_W, 0:S - 1],
                          pv("mu", 24 + j, 25 + j)[0:LORA_W, :], LO[0:LORA_W, j * S + 1:(j + 1) * S], ALU.mult, ALU.add)
            ins.then_inc(unit_free[0].sem, 1)
            wait(*taken(l, U_GATE))
            for i, (qt, br) in enumerate(((0, 1), (0, 2), (1, 1), (1, 2), (0, 0), (1, 0))):
                chain.step(ts(gates[:, :, i], GS[:, qt, br * HEADS:(br + 1) * HEADS], 0.5, 0.5, ALU.mult, ALU.add))
            chain.settle()
            chain.step(ts(gates[:, :, 4], gates[:, :, 4], cv("rowok"), None, ALU.mult))

            for i in range(2):
                u = U_KC + i
                behind(QG * (B_KC + i) + 3)
                wait(x2_act.sem, x2_act.at(l, i + 1))
                src = PB[u % 2][:, :].rearrange("p (t n r) -> p t n r", t=2, r=2)
                for gg in range(2):
                    ins = dve.tensor_copy(X2[HD:P, i, gg::2, :], src[gg * HD:(gg + 1) * HD, :, :, 1])
                ins.then_inc(unit_free[u % 2].sem, 1)
                wait(*taken(l, u))
                for m in range(CMP // 2):
                    ins = ts(view2(XW[:, i, m, :], NG), X2[:, i, :, m:m + 8 * (NCMP - 1) + 1:8],
                             pv("pe_k" if i == 0 else "pe_v", m, m + 1), None, ALU.add)
                ins.then_inc(xw_ready.sem, 1)

            wait(x_stored.sem, x_stored.at(l, 0) + 1)
            wait(att_loaded.sem, att_loaded.at(l, 16))
            for j in range(5):
                behind(QG * (B_Q + j) + 3 if j < 4 else QG * B_CV + 3)
                if j < 4:
                    for n in (2 * j, 2 * j + 1):
                        wait(krope_done.sem, krope_done.at(l, n + 1))
                        chain.step(tt(RT[:, 0:S], A[n % 4][:, 0:S], cosT, ALU.mult))
                        chain.step(tt(RT[:, S:2 * S], A[n % 4][:, S:2 * S], sinT, ALU.mult))
                        chain.settle()
                        tt(KD[:, n, :], RT[:, 0:S], RT[:, S:2 * S], ALU.add).then_inc(kd_ready.sem, 1)
                        wait(kd_ready.sem, kd_ready.at(l, n + 1))
                if j >= 1:
                    q = j - 1
                    wait(qrope_done.sem, qrope_done.at(l, q + 1))
                    chain.step(tt(view2(RT[:, 0:512], 2), view2(QRAW[:, (q % 2) * 512:(q % 2 + 1) * 512], 2),
                                  spread(cosT, 2, S), ALU.mult))
                    chain.step(tt(view2(RT[:, 512:1024], 2), view2(A[4 + q % 2][:, :], 2), spread(sinT, 2, S),
                                  ALU.mult))
                    chain.settle()
                    tt(flat(QR[:, 2 * q:2 * q + 2, :]), RT[:, 0:512], RT[:, 512:1024], ALU.add
                       ).then_inc(qr_ready.sem, 1)
                    wait(qr_ready.sem, qr_ready.at(l, q + 1))
            for i in range(2):
                x = A[i][:, 0:128].rearrange("p (h n) -> p h n", h=2)[:, :, 0:NCG]
                poly, th = view2(HT[:, 0:120], 2), view2(HT[:, 120:240], 2)
                wait(hid_sq.sem, hid_sq.at(l, i + 1))
                op(ts(poly, poly, 0.044715, 1.0, ALU.mult, ALU.add))
                tt(poly, poly, x, ALU.mult).then_inc(hid_arg.sem, 1)
                wait(hid_tanh.sem, hid_tanh.at(l, i + 1))
                stt(view2(HIDV if i else HIDK, 2), th, 1.0, x, ALU.add, ALU.mult).then_inc(hid_ready.sem, 1)

            def silu(i, u, z, tile):
                behind(QG * (B_ZB + i if i < 4 else B_ZA + i - 4) + 3)
                wait(z_tanh.sem, z_tanh.at(l, i + 1))
                stt(flat(z[:, tile:tile + 2, :]), ZT[:, :], 1.0, PB[u % 2][:, :], ALU.add, ALU.mult
                    ).then_inc(unit_free[u % 2].sem, 1)

            silu(0, U_ZB, ZB, 0)
            silu(1, U_ZB + 1, ZB, 2)
            wait(cmp_done.sem, cmp_done.at(l, 2))
            wait(kcraw_ready.sem, kcraw_ready.at(l, 1))
            ends = slice(CMP - 1, CMP - 1 + CSTR * (NCMP - 1) + 1, CSTR)
            chain.step(tt(view2(RT[:, 0:NCG], NG), view2(KCR[:, 0:NCG], NG), spread(cosT[:, ends], NG, NCMP), ALU.mult))
            chain.step(tt(view2(RT[:, 64:64 + NCG], NG), view2(A[2][:, 64:64 + NCG], NG),
                          spread(sinT[:, ends], NG, NCMP), ALU.mult))
            chain.settle()
            tt(KCd, RT[:, 0:NCG], RT[:, 64:64 + NCG], ALU.add).then_inc(kc_ready.sem, 1)
            silu(2, U_ZB + 2, ZB, 4)
            silu(3, U_ZB + 3, ZB, 6)

            def attention(i):
                behind(att_granule(i))
                if 3 <= i < HEADS + 2 and i % 2 == 1:
                    tile = (i - 3) // 2
                    wait(pv_done.sem, pv_done.at(l, i - 1))
                    stt(ZB[:, tile, :], A[4 + tile % 2][:, 0:S], 0.5, ZB[:, tile, :],
                        ALU.mult, ALU.mult).then_inc(yb_ready.sem, 1)
                if 1 <= i < HEADS + 1:
                    wait(probs_turned.sem, probs_turned.at(l, i))
                    dve.tensor_copy(PT[:, 512:1024], A[3][:, :]).then_inc(pt_dve.sem, 1)
                if i < HEADS:
                    b = i % 2
                    mx, rs, cf = (small[:, o + 6 * b:o + 6 * b + 6] for o in (12, 24, 48))
                    wait(scores_done.sem, scores_done.at(l, i + 1))
                    chain.step(stt(SC0[:, b, :, :], view2(A[0][:, 0:256], 2), SCALE, spread(av("caus0"), 2, P),
                                   ALU.mult, ALU.add))
                    chain.step(stt(SC1[:, b, :, :], view2(A[1][:, :], 2), SCALE, spread(av("caus1"), 2, S),
                                   ALU.mult, ALU.add))
                    chain.step(stt(PC[:, b, :, 0:NCMP], view2(A[0][:, 256:288], 2)[:, :, 0:NCMP], SCALE,
                                   view2(av("cmpmask"), 2), ALU.mult, ALU.add))
                    chain.settle()
                    for n, s in enumerate((SC0[:, b, :, :], SC1[:, b, :, :], PC[:, b, :, 0:NCMP])):
                        chain.step(dve.tensor_reduce(mx[:, 2 * n:2 * n + 2], s, AX.X, ALU.max))
                    chain.settle()
                    ts(mx, mx, -1.0, None, ALU.mult).then_inc(sc_ready.sem, 1)
                    wait(exps_done.sem, exps_done.at(l, i + 1))
                    op(dve.reciprocal(rs, rs))
                    tt(cf, rs, gates[:, i, :], ALU.mult).then_inc(cf_ready.sem, 1)

            for u in range(12):
                attention(2 * u)
                behind(QG * (B_K + u) + 3)
                wait(kvr_act.sem, kvr_act.at(l, u + 1))
                for t in range(2):
                    n = 2 * u + t
                    o = KVR[n // 8][:, n % 8, 1:S]
                    ins = stt(o, PB[u % 2][:, t * S:(t + 1) * S - 1], pv("mu", n, n + 1), o, ALU.mult, ALU.add)
                ins.then_inc(unit_free[u % 2].sem, 1)
                attention(2 * u + 1)

            def scan(p):
                wait(lora_read.sem, lora_read.at(l, p + 1))
                op(ts(SG, SG, 1.0, None, ALU.add))
                op(dve.reciprocal(SG, SG))
                dve.tensor_tensor_scan(LIW, cv("inchunk"), SG, 0.0, ALU.mult, ALU.add).then_inc(scan_done.sem, 1)

            def norm_floor(p):
                wait(tv_ready.sem, tv_ready.at(l, p + 1))
                ts(NK, A[1][:, S:2 * S], L2_EPS * L2_EPS, None, ALU.max).then_inc(n_ready.sem, 1)

            def values(p):
                wait(pair_loaded.sem, pair_loaded.at(l, 32 * (p + 1)))
                wait(tv_ready.sem, tv_ready.at(l, p + 1))
                tt(VX, pair_vf[:, :], V[:, p, :], ALU.subtract).then_inc(vf_read.sem, 1)
                wait(vf_read.sem, vf_read.at(l, p + 1))
                op(stt(VX, TV, 1.0, VX, ALU.add, ALU.mult))
                for r in range(2):
                    chain.step(stt(VDUP[:, :, r * CH:(r + 1) * CH], view2(VX, NCH), 0.5, view2(V[:, p, :], NCH),
                                   ALU.mult, ALU.add))

            def keys(p):
                wait(sqrt_ready.sem, sqrt_ready.at(l, p + 1))
                chain.step(dve.reciprocal(NK, NK))
                op(ts(TA, TA, 0.5, -0.5, ALU.mult, ALU.add))
                chain.step(stt(NK, K[:, p, :], pv("k_k", p, p + 1), NK, ALU.mult, ALU.mult))
                op(ts(K2, TA, pv("k_a", p, p + 1), None, ALU.mult))
                chain.step(stt(K2, K2, 1.0, K[:, p, :], ALU.add, ALU.mult))
                chain.settle()
                stt(BKK, TA, 1.0, NK, ALU.add, ALU.mult).then_inc(mid_ready.sem, 1)

            def queries(p):
                wait(decays_ready.sem, decays_ready.at(l, p + 1))
                wait(mid_ready.sem, mid_ready.at(l, p + 1))
                if isinstance(p, int) and p == 0:
                    wait(pads_zero.sem, pads_zero.at(l, 1))
                chain.step(stt(RKK, R[:, p, :], pv("r_k", p, p + 1), K2, ALU.mult, ALU.mult))
                chain.step(dve.tensor_copy(WC[:, (p % 2) * 4:(p % 2) * 4 + 4], Wd[:, CH - 1:S:CH]))
                for h in range(2):
                    a, b = h * HD, (h + 1) * HD
                    chain.step(tt(KR[a:b, p % 2, :, a:b], view2(NK[a:b, :], NCH), view2(LPW[a:b, :], NCH), ALU.mult))
                    chain.step(tt(KR[a:b, p % 2, :, P + a:P + b], view2(R[a:b, p, :], NCH), view2(Wd[a:b, :], NCH),
                                  ALU.mult))
                chain.settle()
                dve.tensor_copy(GNS[:, 20:21], GNS[:, 20:21]).then_inc(ew_dve.sem, 1)

            def group_norm(p):
                wait(ysq_ready.sem, ysq_ready.at(l, p + 1))
                op(dve.tensor_reduce(GNS[:, 4:8], view2(V[:, p, :], NCH), AX.X, ALU.add))
                ts(GNS[:, 8:12], GNS[:, 4:8], 1.0 / HD, GN_EPS, ALU.mult, ALU.add).then_inc(var_ready.sem, 1)
                wait(grstd_ready.sem, grstd_ready.at(l, p + 1))
                for h in range(2):
                    a, b = h * HD, (h + 1) * HD
                    ins = tt(Ybd[a:b, :, a:b], view2(K[a:b, p, :], NCH),
                             GNS[a:b, 12:16].rearrange("p (c o) -> p c o", o=1).to_broadcast([HD, NCH, HD]), ALU.mult)
                ins.then_inc(ybd_ready.sem, 1)

            def y_end(p):
                wait(yt_ready.sem, yt_ready.at(l, p + 1))
                op(tt(V[:, p, :], V[:, p, :], R[:, p, :], ALU.add))
                stt(ZA[:, p, :], V[:, p, :], 0.5, ZA[:, p, :], ALU.mult, ALU.mult).then_inc(ya_ready.sem, 1)

            def masked(o, b, mask):
                return tt(o, quad(b), spread(cv(mask), NCH, P), ALU.mult)

            def grow(p, n):
                tt(flat(X), A[4][:, :], flat(X), ALU.add).then_inc(x_step.sem, 1)

            def rwkv_pair(p, k):
                if k in (0, 1, 2, 5, 6, 7, 9, 12, 15, 17, 20, 23, 26):
                    wait(rwkv_step.sem, rwkv_step.at(l, rw_at(p, k)))
                nxt = p + 1 < HP
                wc = WC[:, (p % 2) * 4:(p % 2) * 4 + 4]
                if k == 0:
                    masked(Qd, A[0], "q_blk")
                    masked(QdT, A[1], "qt_blk")
                    masked(QT32, A[1], "qt_32")
                    masked(QT64, A[1], "qt_64").then_inc(q_masked.sem, 1)
                elif k == 1:
                    masked(Mrb, A[2], "incl")
                    masked(Mak, A[3], "strict_x")
                    masked(Mrk, A[4], "incl_x").then_inc(m_masked.sem, 1)
                elif k == 2:
                    dve.tensor_copy(Vst[0:HD, :, :], quad(A[5])[0:HD, :, HD:P])
                    dve.tensor_copy(Vst[HD:P, :, :], quad(A[5])[HD:P, :, 0:HD]).then_inc(v_ready.sem, 1)
                    if p:
                        group_norm(p - 1)
                elif k == 5:
                    wait(x1_ready.sem, x1_ready.at(l, p + 1))
                    grow(p, 0)
                elif k == 6:
                    tt(view2(R[:, p, :], NCH), view2(A[1][:, 0:S], NCH), VDUP[:, :, 0:CH], ALU.mult
                       ).then_inc(bonus_ready.sem, 1)
                elif k == 7:
                    wait(x_step.sem, x_step.at(l, 4 * p + 1))
                    grow(p, 1)
                    if p:
                        y_end(p - 1)
                elif k == 9:
                    wait(x_step.sem, x_step.at(l, 4 * p + 2))
                    grow(p, 2)
                    if nxt:
                        scan(p + 1)
                elif k == 12:
                    wait(x_step.sem, x_step.at(l, 4 * p + 3))
                    grow(p, 3)
                    if nxt:
                        norm_floor(p + 1)
                elif k == 13 and nxt:
                    values(p + 1)
                elif k == 15:
                    wait(x_step.sem, x_step.at(l, 4 * p + 4))
                    stt(flat(TT), A[4][:, :], -1.0, flat(X), ALU.mult, ALU.subtract).then_inc(t_ready.sem, 1)
                    if nxt:
                        keys(p + 1)
                elif k == 17:
                    chain.settle()
                    ts(Z, A[1][:, 256:256 + CH], wc[:, 0:1], None, ALU.mult).then_inc(z_ready.sem, 1)
                    wait(z_ready.sem, z_ready.at(l, 3 * p + 1))
                    chain.step(ts(Zt, Z, wc[:, 1:2], None, ALU.mult))
                    if nxt:
                        queries(p + 1)
                elif k == 20 or k == 23:
                    c = (k - 17) // 3
                    chain.settle()
                    stt(Z, A[1][:, 256 + c * CH:256 + (c + 1) * CH], wc[:, c:c + 1], Zt, ALU.mult, ALU.add
                        ).then_inc(z_ready.sem, 1)
                    if c == 1:
                        wait(z_ready.sem, z_ready.at(l, 3 * p + 2))
                        chain.step(ts(Zt, Z, wc[:, 2:3], None, ALU.mult))
                elif k == 26:
                    y = view2(A[2][:, 0:S], NCH)
                    op(dve.tensor_reduce(GNS[:, 0:4], y, AX.X, ALU.add))
                    op(ts(GNS[:, 0:4], GNS[:, 0:4], 1.0 / HD, None, ALU.mult))
                    tt(view2(K[:, p, :], NCH), y,
                       GNS[:, 0:4].rearrange("p (c o) -> p c o", o=1).to_broadcast([P, NCH, HD]), ALU.subtract
                       ).then_inc(yc_ready.sem, 1)
                    if not nxt:
                        group_norm(p)

            def rwkv(i):
                behind(rw_granule(i))
                if i < HP * RW_STEPS:
                    rwkv_pair(i // RW_STEPS, i % RW_STEPS)

            split_to(QG * B_ZA + 1)
            scan(0)
            norm_floor(0)
            values(0)
            keys(0)
            queries(0)
            for u in range(4):
                for i in range(16):
                    rwkv(16 * u + i)
                silu(4 + u, U_ZA + u, ZA, 2 * u)
            for u in range(8):
                for i in range(16):
                    rwkv(64 + 16 * u + i)
            for u in range(8):
                for i in range(8):
                    rwkv(192 + 8 * u + i)
                wait(*done(l, U_PB + u))
                for v in (U_MGB + u,):
                    wait(*taken(l, v))
                m = flat(MB[:, 2 * u:2 * u + 2, :])
                stt(m, m, 1.0, PB[u % 2][:, :], ALU.add, ALU.mult).then_inc(unit_free[u % 2].sem, 1)
            behind(QG * B_A - 1)
            y_end(HP - 1)
            wait(ya_ready.sem, ya_ready.at(l, HP))
            for n in range(4):
                t = slice(2 * n, 2 * n + 2)
                wait(ya_hi_ready.sem, ya_hi_ready.at(l, n + 1))
                low(ya_lo[:, t, :], ZA[:, t, :], ya_hi[:, t, :]).then_inc(ya_lo_ready.sem, 1)

            def merged_low(j):
                for n in (2 * j, 2 * j + 1):
                    t = slice(2 * n, 2 * n + 2)
                    wait(merged_hi_ready.sem, merged_hi_ready.at(l, n + 1))
                    low(merged_lo[:, t, :], MB[:, t, :], merged_hi[:, t, :]).then_inc(merged_lo_ready.sem, 1)

            for j in range(4):
                if j:
                    behind(QG * (B_A + 3 * j + 1) + 3)
                    merged_low(j - 1)
                for i in range(2):
                    u = U_A + 4 * j + 2 + i
                    behind(QG * (B_A + 3 * j + 2) + 2 * i + 1)
                    wait(*done(l, u))
                    wait(*taken(l, U_A + 4 * j + i))
                    g = GAB[:, j % 2, i * 512:(i + 1) * 512]
                    m = flat(MB[:, 4 * j + 2 * i:4 * j + 2 * i + 2, :])
                    stt(g, g, 1.0, PB[u % 2][:, :], ALU.add, ALU.mult).then_inc(unit_free[u % 2].sem, 1)
                    wait(*taken(l, u))
                    tt(m, m, g, ALU.add).then_inc(merged_ready.sem, 1)
            merged_low(3)
            for n in range(4):
                behind(QG * (B_WO + 2 * n) + 7)
                for t in range(2):
                    u = U_WO + 2 * n + t
                    wait(wo_sq.sem, wo_sq.at(l, 2 * n + t + 1))
                    dve.tensor_copy(OUT[:, t, n * 512:(n + 1) * 512], PB[t][:, :]).then_inc(unit_free[t].sem, 1)
            op(dve.tensor_reduce(small[:, 6:8], view2(small[:, 40:48], 2), AX.X, ALU.add))
            ts(small[:, 6:8], small[:, 6:8], 0.25 / D, NORM_EPS, ALU.mult, ALU.add).then_inc(ms2_ready.sem, 1)
            wait(rstd2_ready.sem, rstd2_ready.at(l, 1))
            op(ts(small[:, 10:12], small[:, 8:10], 0.5, None, ALU.mult))
            wait(xr_loaded.sem, xr_loaded.at(l, 32))
            wait(*taken(l, U_WO + 6))
            wait(*taken(l, U_WO + 7))
            for t in range(2):
                chain.step(stt(OUT[:, t, :], OUT[:, t, :], small[:, 10 + t:11 + t], GPOST, ALU.mult, ALU.mult))
            chain.settle()
            for t in range(2):
                ins = tt(XR[:, t, :], XR[:, t, :], OUT[:, t, :], ALU.add)
            ins.then_inc(x_new.sem, 1)

        @block.vector
        def _(dve):
            chain = Chain(dve, dve_chain)
            wait = dve.wait_ge

            def op(ins):
                chain.step(ins)
                chain.settle()

            wait(pos_loaded, 16)
            wait(con_loaded, 16)
            posf, ang, turns = (WORK[:, 8192 + i * S:8192 + (i + 1) * S] for i in range(3))
            op(dve.tensor_copy(posf, WORK[:, 8192 + 3 * S:8192 + 4 * S].bitcast(I32)))
            op(dve.tensor_scalar(ang, posf, cv("invf"), None, ALU.mult))
            c1 = 6.28125
            c2 = float(np.float32(round((2 * np.pi - c1) * 2 ** 20) / 2 ** 20))
            c3 = float(2 * np.pi - c1 - c2)
            big = 1.5 * 2 ** 23
            for i, shift in enumerate((0.25, 0.0)):
                o = cs[:, i * S:(i + 1) * S]
                op(dve.tensor_scalar(turns, ang, float(1 / (2 * np.pi)), shift, ALU.mult, ALU.add))
                op(dve.tensor_scalar(turns, turns, big, None, ALU.add))
                op(dve.tensor_scalar(turns, turns, big, None, ALU.subtract))
                op(dve.scalar_tensor_tensor(o, turns, -c1, ang, ALU.mult, ALU.add))
                op(dve.scalar_tensor_tensor(o, turns, -c2, o, ALU.mult, ALU.add))
                op(dve.scalar_tensor_tensor(o, turns, -c3, o, ALU.mult, ALU.add))
                if i == 0:
                    op(dve.tensor_scalar(o, o, float(np.pi / 2), None, ALU.add))
                op(dve.tensor_scalar(o, o, 3.1415925, -3.1415925, ALU.min, ALU.max))
            dve.tensor_copy(turns, ang).then_inc(sin_arg, 1)
            wait(table_ready, 1)
            wait(zeroed, 1)
            wait(x_loaded, 16)
            chain.restart()
            with dve.Fori(0, LAYERS) as l:
                dve_layer(dve, l, chain)
                chain.restart()

        def pool_layer(pool, l):
            wait = pool.wait_ge

            def view2(ap, n):
                return ap.rearrange("p (t n) -> p t n", t=n)

            wait(par_loaded.sem, par_loaded.at(l, 16))
            pool.tensor_tensor(ha0, pv("a0"), half8[:, :], ALU.mult)
            pool.tensor_scalar(omu, pv("mu"), -1.0, 1.0, ALU.mult, ALU.add)
            pool.tensor_scalar(nw0, pv("w0"), -1.0, None, ALU.mult)
            pool.tensor_scalar(hv0, pv("v0"), 0.5, None, ALU.mult)
            pool.tensor_copy(view2(w2kd[:, :], 2)[:, :, 0:HD], view2(pv("w2k"), 2))
            pool.tensor_copy(view2(w2kd[:, :], 2)[:, :, HD:P], view2(pv("w2k"), 2)).then_inc(derived_ready.sem, 1)
            wait(ms_ready.sem, ms_ready.at(l, 1))
            pool.tensor_tensor(small[:, 4:6], small[:, 2:4], halves[:, 0:2], ALU.pow).then_inc(rstd_ready.sem, 1)

            for h in range(HEADS):
                b = h % 2
                cf = small[:, 48 + 6 * b:54 + 6 * b]
                wait(cf_ready.sem, cf_ready.at(l, h + 1))
                for n, (s, w) in enumerate(((SC0[:, b, :, :], P), (SC1[:, b, :, :], S), (PC[:, b, :, 0:NCMP], NCMP))):
                    k = cf[:, 2 * n:2 * n + 2].rearrange("p (r o) -> p r o", o=1).to_broadcast([P, 2, w])
                    ins = pool.tensor_tensor(s, s, k, ALU.mult)
                ins.then_inc(probs_ready.sem, 1)

            wait(yb_ready.sem, yb_ready.at(l, HP))
            pool.tensor_tensor(GNS[:, 20:24], halves[:, :], halves[:, :], ALU.subtract)
            for a in (BB, KA, Ybd):
                pool.memset(a, 0.0)
            pool.memset(WORK[:, 0:2048], 0.0)
            pool.memset(GNS[:, 0:20], 0.0).then_inc(pads_zero.sem, 1)
            wait(pads_zero.sem, pads_zero.at(l, 1))

            def before(p):
                wait(scan_done.sem, scan_done.at(l, p + 1))
                pool.tensor_tensor(LPW, LIW, SG, ALU.subtract).then_inc(lp_ready.sem, 1)
                wait(mid_ready.sem, mid_ready.at(l, p + 1))
                wait(decays_ready.sem, decays_ready.at(l, p + 1))
                for h in range(2):
                    a, b = h * HD, (h + 1) * HD
                    pool.tensor_tensor(BB[a:b, :, a:b], view2(BKK[a:b, :], NCH), view2(LIW[a:b, :], NCH), ALU.mult)
                    ins = pool.tensor_tensor(KA[a:b, :, HD - a:P - a], view2(K2[a:b, :], NCH), view2(LIW[a:b, :], NCH),
                                             ALU.mult)
                ins.then_inc(ew_pool.sem, 1)

            def group_rstd(p):
                wait(var_ready.sem, var_ready.at(l, p + 1))
                pool.tensor_tensor(GNS[:, 12:16], GNS[:, 8:12], halves[:, 0:4], ALU.pow).then_inc(grstd_ready.sem, 1)

            before(0)
            for p in range(HP):
                wait(q_masked.sem, q_masked.at(l, p + 1))
                pool.tensor_tensor(X, Qd, spread(cv("ident"), NCH, P), ALU.add).then_inc(x1_ready.sem, 1)
                if p:
                    group_rstd(p - 1)
                if p + 1 < HP:
                    before(p + 1)
            group_rstd(HP - 1)
            wait(ms2_ready.sem, ms2_ready.at(l, 1))
            pool.tensor_tensor(small[:, 8:10], small[:, 6:8], halves[:, 0:2], ALU.pow).then_inc(rstd2_ready.sem, 1)

        @block.gpsimd
        def _(pool):
            pool.memset(VC, 0.0)
            pool.memset(PC, 0.0)
            pool.memset(small[:, :], 0.0)
            pool.memset(half8[:, :], 0.5)
            pool.memset(halves[:, :], -0.5).then_inc(zeroed, 1)
            pool.wait_ge(zeroed, 1)
            with pool.Fori(0, LAYERS) as l:
                pool_layer(pool, l)


def chunked(w):
    n = w.shape[0] // P
    return np.ascontiguousarray(w.reshape(n, P, -1).transpose(1, 0, 2)).reshape(P, -1)


def weight_stream(w_in, ck_w1, cv_w1, w_a, w_b, w_o):
    shift = 3 * RW + 2 * LORA_W
    za, q = shift, shift + RW
    kv = q + RW
    gate = kv + 6 * NG * HD
    zb = gate + 3 * HEADS
    mg = zb + RW
    tiled = lambda w: np.concatenate([chunked(w[:, i:i + P]) for i in range(0, w.shape[1], P)], 1)
    col = lambda a, n=256: tiled(w_in[:, a:a + n])
    log = np.zeros((D, 256), np.float32)
    log[:, 0:2 * LORA_W] = w_in[:, 3 * RW:shift]
    log[:, 192:240] = w_in[:, gate:gate + 48]
    vt = np.concatenate([w_in[:, kv + 768:kv + 1024], w_in[:, kv + 1280:kv + 1536]], 1)
    blocks = [chunked(log), col(kv), col(kv + 256), col(kv + 512), col(kv + 1024), chunked(vt[0:1024]),
              chunked(vt[1024:])]
    blocks += [col(q + 256 * i) for i in range(4)]
    blocks += [tiled(ck_w1), tiled(cv_w1)]
    blocks += [col(zb + 256 * i) for i in range(4)]
    for a in (RW, 2 * RW, 0):
        blocks += [col(a + 256 * i) for i in range(4)]
    blocks += [col(za + 256 * i) for i in range(4)]
    blocks += [col(mg + D + 256 * i) for i in range(8)]
    blocks += [tiled(w_b[:, 512 * i:512 * (i + 1)]) for i in range(4)]
    for j in range(4):
        blocks += [col(mg + 512 * j), col(mg + 512 * j + 256), tiled(w_a[:, 512 * j:512 * (j + 1)])]
    blocks += [chunked(w_o[1024 * kh:1024 * (kh + 1), 512 * n:512 * (n + 1)]) for n in range(4) for kh in range(2)]
    assert len(blocks) == NB and all(b.shape == (P, QG * GR) for b in blocks)
    return np.ascontiguousarray(np.stack(blocks).reshape(NB, P, QG, GR).transpose(0, 2, 1, 3)).reshape(NGR, P, GR)


def pair_ups(a, l):
    t = np.zeros((HP, P, 3, P), np.float32)
    for i, w in enumerate((a["rwkv_w_up"][l], a["rwkv_a_up"][l], a["rwkv_v_up"][max(l - 1, 0)])):
        t[:, 0:w.shape[0], i, :] = w.reshape(-1, HP, P).transpose(1, 0, 2)
    return t.reshape(HP, P, 3 * P)


def param_tile(a, l):
    t = np.zeros((P, NPAR), np.float32)

    def put(name, v):
        lo, hi = PAR[name]
        t[0:v.shape[0], lo:hi] = v

    v = max(l - 1, 0)
    cols = lambda w: w.reshape(-1, P).T
    mu = a["rwkv_mu"][l]
    put("v_down", chunked(a["rwkv_v_down"][v]))
    put("w2k", chunked(a["nsa_ck_w2"][l]))
    put("w2v", chunked(a["nsa_cv_w2"][l]))
    m = np.zeros((P, 26), np.float32)
    m[:, 0:24] = np.concatenate([cols(mu[RW:2 * RW]), cols(mu[2 * RW:3 * RW]), cols(mu[0:RW])], 1)
    m[0:LORA_W, 24] = mu[3 * RW:3 * RW + LORA_W]
    m[0:LORA_W, 25] = mu[3 * RW + LORA_W:]
    put("mu", m)
    for name in ("w0", "a0", "k_k", "k_a", "gn_w", "gn_b"):
        put(name, cols(a["rwkv_" + name][l]))
    put("v0", cols(a["rwkv_v0"][v]))
    put("r_k", cols(a["rwkv_r_k"][l].reshape(-1)))
    put("norm_pre", cols(a["norm_pre"][l]))
    put("pe_k", cols(a["nsa_pe_k"][l].reshape(-1)))
    put("pe_v", cols(a["nsa_pe_v"][l].reshape(-1)))
    return t


def constant_tiles():
    t, att = np.zeros((P, NCON), np.float32), np.zeros((P, NATT), np.float32)

    def put(name, v):
        lo, hi = CON[name] if name in CON else ATT[name]
        (t if name in CON else att)[0:v.shape[0], lo:hi] = v

    i = np.arange(P)
    put("ident", np.eye(P))
    r, c = i[:, None], i[None, :]
    same = lambda n: r // n == c // n
    put("q_blk", -1.0 * (same(16) & (r < c)))
    put("qt_blk", -1.0 * (same(16) & (r > c)))
    put("qt_32", -1.0 * (same(32) & ~same(16) & (r > c)))
    put("qt_64", -1.0 * (same(64) & ~same(32) & (r > c)))
    rr, cc = r % CH, c % CH
    put("incl", 1.0 * (same(64) & (rr <= cc)))
    put("strict_x", 1.0 * (~same(64) & (rr < cc)))
    put("incl_x", 1.0 * (~same(64) & (rr <= cc)))
    put("ones", 1.0 * same(64))
    put("ident2", 1.0 * (i[:, None] % CH == np.arange(CH)[None, :]))
    rot = np.zeros((P, P))
    half = HD // 8
    for h in range(2):
        for m in range(half):
            rot[h * HD + m + half, h * HD + m] = -1.0
            rot[h * HD + m, h * HD + m + half] = 1.0
    put("rot", rot)
    dup = []
    for gg in range(2):
        d = np.zeros((P, P))
        for m in range(P):
            d[gg * HD + m % HD, m] = 1.0
        dup += [d, d @ rot]
    put("dup", np.concatenate(dup, 1))
    k = np.arange(S)[None, :]
    put("caus0", np.where(k[:, :P] > i[:, None], -1e30, 0.0))
    put("caus1", np.where(k > P + i[:, None], -1e30, 0.0))
    end = np.arange(NCMP)[None, :] * CSTR + CMP - 1
    put("cmpmask", np.concatenate([np.where(end <= t0 + i[:, None], 0.0, -1e30) for t0 in (0, P)], 1))
    put("rowok", 1.0 * (i[:, None] >= CMP - 1))
    inv = np.float32(500000.0) ** (-np.arange(half, dtype=np.float32) * np.float32(2.0 / (HD // 4)))
    f = np.zeros((P, 1), np.float32)
    for h in range(2):
        f[h * HD:h * HD + half, 0] = inv
        f[h * HD + half:h * HD + 2 * half, 0] = inv
    put("invf", f)
    put("inchunk", 1.0 * np.broadcast_to(k % CH != 0, (P, S)))
    return t, att


def kernel(**inputs):
    import concourse.bacc as bacc
    from concourse.bass_utils import run_bass_kernel_spmd as run

    a = {n: np.asarray(v) for n, v in inputs.items()}
    con, att = constant_tiles()
    arrays = {
        "in_x": np.ascontiguousarray(a["x"]),
        "in_positions": np.ascontiguousarray(a["positions"]),
        "in_stream": np.concatenate([weight_stream(a["w_in"][l], a["nsa_ck_w1"][l], a["nsa_cv_w1"][l],
                                                   a["w_proj_a"][l], a["w_proj_b"][l], a["w_out"][l])
                                     for l in range(LAYERS)]),
        "in_params": np.stack([param_tile(a, min(l, LAYERS - 1)) for l in range(LAYERS + 1)]),
        "in_pair_ups": np.concatenate([pair_ups(a, l) for l in range(LAYERS)]),
        "in_constants": con,
        "in_attention_constants": att,
        "in_norm_post": np.ascontiguousarray(a["norm_post"]),
    }
    nc = bacc.Bacc("TRN2", target_bir_lowering=False, num_devices=1)
    args = [nc.dram_tensor(n, v.shape, mybir.dt.from_np(v.dtype), kind="ExternalInput").ap()
            for n, v in arrays.items()]
    out = nc.dram_tensor("out_x", (1, S, D), F32, kind="ExternalOutput").ap()
    v_first = nc.dram_tensor("v_by_layer", (LAYERS, P, HP * S), F32, kind="Internal").ap()
    build(nc, *args, v_first, out)
    return run(nc, [arrays], core_ids=[0]).results[0]["out_x"]
```

```python
from contextlib import ExitStack

import numpy as np
import concourse.bass as bass
from concourse import mybir

F32 = mybir.dt.float32
F32R = mybir.dt.float32r
I32 = mybir.dt.int32
ALU = mybir.AluOpType
ACT = mybir.ActivationFunctionType
AX = mybir.AxisListType

P = 128
LAYERS, D, S = 2, 2048, 256
KC = D // P
RW = 1024
HP = RW // P
HEADS = 16
HD = 64
CH = 64
NCH = S // CH
LORA_W = 96
LORA_V = 64
CMP = 32
CSTR = 16
NCMP = (S - CMP) // CSTR + 1
NG = 4
NCG = NCMP * NG
SCALE = HD ** -0.5
DECAY = float(np.exp(-0.5))
GN_EPS, L2_EPS, NORM_EPS = 64e-5, 1e-12, 1e-6

B_LOG, B_KC, B_VC, B_KS, B_KW, B_VT, B_Q, B_CK, B_CV = 0, 1, 2, 3, 4, 5, 7, 11, 12
B_ZB, B_K, B_V, B_R, B_ZA, B_MGB, B_PB, B_A, B_WO = 13, 17, 21, 25, 29, 33, 41, 45, 57
NB = 65
GR = 1024
QG = 4
NGR = NB * QG
SLOTS = 5
assert NGR % SLOTS == 0
LEAD = 2
U_LO, U_GATE, U_KC, U_VC, U_KS, U_KW, U_VT, U_Q, U_ZB = 0, 1, 2, 3, 4, 5, 6, 8, 12
U_K, U_ZA, U_MGB, U_PB, U_A, U_WO, UNITS = 16, 28, 32, 40, 48, 64, 72



def native(g):
    b = g // QG
    return b in (B_CK, B_CV)


def splits(g):
    return sum(not native(i) for i in range(g + 1))


def unit_ended(g):
    b, q = g // QG, g % QG
    if B_PB <= b < B_A:
        return U_PB + 2 * (b - B_PB) + q // 2 if q % 2 else None
    if B_A <= b < B_WO and (b - B_A) % 3 == 2:
        return U_A + 4 * ((b - B_A) // 3) + 2 + q // 2 if q % 2 else None
    if q < QG - 1 or b in (B_VT, B_CK, B_CV):
        return None
    if b == B_LOG:
        return U_GATE
    if b < B_VT:
        return U_KC + b - B_KC
    if b == B_VT + 1:
        return U_VT + 1
    if b < B_CK:
        return U_Q + b - B_Q
    if b < B_PB:
        return U_ZB + b - B_ZB
    if b < B_WO:
        return U_A + 4 * ((b - B_A) // 3) + (b - B_A) % 3
    return U_WO + 2 * ((b - B_WO) // 2) + 1 if (b - B_WO) % 2 else None


def hidden_ended(g):
    return g % QG == QG - 1 and g // QG in (B_CK, B_CV)


def parts(g):
    return sum(unit_ended(i) is None and not hidden_ended(i) for i in range(g + 1))


PAR = {}
_at = 0
for _n, _w in (("v_down", HP * LORA_V), ("w2k", 128), ("w2v", 128),
               ("mu", 26), ("w0", 8), ("a0", 8), ("v0", 8), ("k_k", 8), ("k_a", 8), ("r_k", 8), ("gn_w", 8),
               ("gn_b", 8), ("norm_pre", 16), ("pe_k", 16), ("pe_v", 16)):
    PAR[_n] = (_at, _at + _w)
    _at += _w
NPAR = _at
CON = {}
_at = 0
for _n, _w in (("ident", 128), ("q_blk", 128), ("qt_blk", 128), ("qt_32", 128), ("qt_64", 128), ("incl", 128),
               ("strict_x", 128), ("incl_x", 128), ("ones", 128), ("headcol", 30), ("ident2", 64),
               ("rowok", 1), ("invf", 1), ("inchunk", 256)):
    CON[_n] = (_at, _at + _w)
    _at += _w
NCON = _at
ATT = {}
_at = 0
for _n, _w in (("rot", 128), ("dup", 4 * 128), ("caus0", 128), ("caus1", 256), ("cmpmask", 30)):
    ATT[_n] = (_at, _at + _w)
    _at += _w
NATT = _at

RW_STEPS = 27
PRE_STEPS = 2
PRE_POINT = 19
SCHEDULE = (0, 1, 2, 3, 4, 5, 6, None, 7, 8, 9, None, 10, 11, 12, None, 13, 14, 15, None, 16, 17, None,
            18, 19, 20, 21, 22, 23, 24, 25, 26)
PAIR_POINTS = len(SCHEDULE)
HI_AT = {0: 2, 6: 3, 10: 4, 13: 5, 18: 6, 21: 7, 25: 8, 28: 9}
LO_AT = {3: 2, 7: 3, 11: 4, 15: 5, 22: 6, 26: 7, 29: 8, 30: 9}
YB_PAIR, YB_HI_AT, YB_LO_AT = 5, (1, 2), (12, 27)



def rw_at(p, k):
    return PRE_STEPS + p * RW_STEPS + k + 1


def lora_at(p):
    return 1 if p == 0 else rw_at(p - 1, 9)


def norms_at(p):
    return 2 if p == 0 else rw_at(p - 1, 11)


def rw_granule(i):
    return QG * B_ZA + i // 4


def att_granule(i):
    return QG * B_K + 2 * i + 1


class Signal:

    def __init__(self, sem, per_layer, ahead=0):
        self.sem, self.per_layer, self.ahead = sem, per_layer, ahead

    def at(self, l, n):
        return l * self.per_layer + (n + self.ahead)


class Chain:

    def __init__(self, eng, sem):
        self.eng, self.sem, self.n = eng, sem, 0

    def step(self, ins):
        self.n += 1
        ins.then_inc(self.sem, 1)
        return ins

    def settle(self):
        self.eng.wait_ge(self.sem, self.n)

    def restart(self):
        self.settle()
        self.eng.sem_clear(self.sem)
        self.n = 0


def build(nc, x, pos, stream, params, ups, consts, att_consts, norm_post, v_first, out):
    ctx = ExitStack()
    with ctx:
        used = [-(-nc.sbuf_base // 32) * 32]

        def place(name, cols, at, dt=F32):
            return nc.alloc_sbuf_tensor_at(name, [P, cols], dt, offset=at)

        def sb(name, cols, dt=F32):
            at = used[0]
            used[0] += -(-cols * 4 // 32) * 32
            assert used[0] <= nc.sbuf_usable_end, (name, used[0])
            return place(name, cols, at, dt)

        def sem(name):
            return ctx.enter_context(nc.semaphore(name))

        def signal(name, per_layer, ahead=0):
            return Signal(sem(name), per_layer, ahead)

        def tiles(t, n):
            return t[:, :].rearrange("p (c n) -> p c n", c=n)

        at = used[0]
        hT = [tiles(sb("hT_hi", KC * S, F32R), KC), tiles(sb("hT_lo", KC * S, F32R), KC)]
        OUT = tiles(place("w_out_result", KC * S, at), 2)
        at = used[0]
        w_raw = [sb(f"weights{s}", GR) for s in range(SLOTS)]
        w_lo = [place(f"weights_lo{s}", GR, at + 4 * GR * s, F32R) for s in range(SLOTS)]
        w_hi = [sb(f"weights_hi{s}", GR, F32R) for s in range(SLOTS)]
        at = used[0]
        ZA = tiles(sb("za", HP * S), HP)
        ya_lo = tiles(place("ya_lo", HP * S, at, F32R), HP)
        at_zb = used[0]
        ZB = tiles(sb("zb", HP * S), HP)
        yb_lo = tiles(place("yb_lo", HP * S, at_zb, F32R), HP)
        at = used[0]
        merged = sb("merged", KC * S)
        MB = tiles(merged, KC)
        merged_lo = tiles(place("merged_lo", KC * S, at, F32R), KC)
        at = used[0]
        KVR = [tiles(sb(n, HP * S), HP) for n in ("rk", "rv", "rr")]
        K, V, R = KVR
        yb_hi = tiles(place("yb_hi", 2 * HP * S, at, F32R), 2 * HP)
        yb_hi = [yb_hi[:, c, :] for c in (0, 1, 2, 3, HP, HP + 1, HP + 2, HP + 3)]
        ya_hi = tiles(place("ya_hi", HP * S, at, F32R), HP)
        merged_hi = tiles(place("merged_hi", KC * S, at + 4 * HP * S, F32R), KC)
        par = sb("par", NPAR)
        con = sb("con", NCON)
        pair_up = sb("pair_up", 3 * P)
        pair_vf = sb("pair_v_first", S)
        cs = sb("cos_sin", 2 * S)
        derived = sb("derived", 26 + 24)
        w2kd = sb("w2kd", 256)
        gates = sb("gates", HEADS * 6)[:, :].rearrange("p (h i) -> p h i", i=6)
        v_cmp = sb("v_cmp", 2 * NG * HD)
        VC = v_cmp[:, :].rearrange("p (t g d) -> p t g d", t=2, g=NG)
        PC = sb("p_cmp", 2 * P)[:, :].rearrange("p (b q k) -> p b q k", b=2, q=2)
        LO = sb("lora_in", 2 * S)
        small = sb("small", 64)
        halves = sb("halves", 4)
        half8 = sb("half8", 8)
        VD = sb("v_down_out", S)
        NI = VD[LORA_V:LORA_V + HEADS, :]
        ZT = sb("z_tanh", 512)
        WORK = sb("work", 13600)

        def pv(name, a=0, b=None):
            lo, hi = PAR[name]
            return par[:, lo + a:(hi if b is None else lo + b)]

        def cv(name, a=0, b=None):
            lo, hi = CON[name]
            return con[:, lo + a:(hi if b is None else lo + b)]

        def av(name, a=0, b=None):
            lo, hi = ATT[name]
            return merged[:, lo + a:(hi if b is None else lo + b)]

        def spread(ap, n, w):
            return ap.rearrange("p (o w) -> p o w", o=1).to_broadcast([P, n, w])

        omu = derived[:, 0:26]
        hw0, ha0, hv0 = (derived[:, 26 + 8 * i:34 + 8 * i] for i in range(3))
        cosT, sinT = cs[:, 0:S], cs[:, S:2 * S]

        def views(*sizes):
            at, res = 0, []
            for w in sizes:
                res.append(WORK[:, at:at + w])
                at += w
            assert at <= 13600, at
            return res

        (QR, KD, KRAW, QRAW, VTM, RT, SC0, SC1, PT, HIDK, HIDV, GS, KCR, KCd, HT, HR) = views(
            2048, 2048, 1024, 1024, 1024, 1024, 512, 1024, 1024, 120, 120, 96, 120, 60, 512, 512)
        QR = QR.rearrange("p (t n) -> p t n", t=HP)
        KD = KD.rearrange("p (t n) -> p t n", t=8)
        X2, XW = merged[:, NATT:NATT + 1024], merged[:, NATT + 1024:NATT + 1024 + 2 * NCG * CMP // 2]
        X2 = X2.rearrange("p (b g n) -> p b g n", b=2, g=NG)
        XW = XW.rearrange("p (b m j) -> p b m j", b=2, m=CMP // 2)
        VTM = VTM.rearrange("p (t n) -> p t n", t=2)
        SC0 = SC0.rearrange("p (b r k) -> p b r k", b=2, r=2)
        SC1 = SC1.rearrange("p (b r k) -> p b r k", b=2, r=2)
        GS = GS.rearrange("p (t n) -> p t n", t=2)
        KSQ = WORK[:, 11520:11520 + HP * S].rearrange("p (t n) -> p t n", t=HP)

        (KR, BB, KA, Ybd, BBt, KAt, Qd, QdT, QT32, QT64, Mrb, Mak, Mrk, Q2, Q2T, Q4T, X, VDUP, Vst, SG, LPW, LIW,
         Wd, TA, NK, K2, TV, VX, WC, Z, Zt, RHS, Uc, GNS) = views(
            2048, 512, 512, 512, 512, 512, 512, 512, 512, 512, 512, 512, 512, 512, 512, 512, 512, 512, 256,
            256, 256, 256, 256, 256, 256, 256, 256, 256, 8, 64, 64, 64, 64, 24)
        KR = KR.rearrange("p (b c n) -> p b c n", b=2, c=NCH)
        BB, KA, Ybd, BBt, KAt, Qd, QdT, QT32, QT64, Mrb, Mak, Mrk, Q2, Q2T, Q4T, X, VDUP = (
            a.rearrange("p (c n) -> p c n", c=NCH)
            for a in (BB, KA, Ybd, BBt, KAt, Qd, QdT, QT32, QT64, Mrb, Mak, Mrk, Q2, Q2T, Q4T, X, VDUP))
        Vst = Vst.rearrange("p (c n) -> p c n", c=NCH)
        TT, XT, WX = Qd, Q2T, Q2
        RKK, BKK = SG, TA
        (XR, SQX, GPOST) = views(4096, 4096, 2048)
        XR = XR.rearrange("p (t n) -> p t n", t=2)
        SQX = SQX.rearrange("p (t n) -> p t n", t=2)
        GAB = WORK[:, 10240:12288].rearrange("p (b n) -> p b n", b=2)
        SQJ = WORK[:, 12288:12800]
        RDIAG = WORK[:, 12800:12800 + 2 * P].rearrange("p (t n) -> p t n", t=2)

        bank = [ctx.enter_context(nc.psum_tensor(f"bank{b}", [P, 512], F32)) for b in range(8)]
        PB, A = bank[0:2], bank[2:8]

        def out_banks(n):
            return A[0:2] if n % 2 else PB

        def quad(b):
            return b[:, :].rearrange("p (c n) -> p c n", c=4)

        loaded = [signal(f"granule_loaded{s}", 16 * (NGR // SLOTS)) for s in range(SLOTS)]
        att_loaded = signal("att_constants_loaded", 16)
        v_stored = signal("v_stored", 16)
        pair_loaded = signal("pair_loaded", 32 * HP)
        par_loaded = signal("params_loaded", 16)
        con_loaded = sem("constants_loaded")
        pos_loaded = sem("positions_loaded")
        x_loaded = sem("x_loaded")
        xr_loaded = signal("residual_loaded", 48)
        x_stored = signal("x_stored", 32)
        unit_done = [signal(f"unit_done{b}", UNITS // 2, 1) for b in range(2)]
        part_used = signal("part_used", parts(NGR - 1), SLOTS - 1)
        hT_turned = signal("hT_turned", 8)
        hidden_done = signal("hidden_done", 2)
        hidden_turned = signal("hidden_turned", 1)
        cmp_done = signal("cmp_done", 3)
        krope_done = signal("krope_done", 8)
        qrope_done = signal("qrope_done", 4)
        scores_done = signal("scores_done", HEADS)
        probs_turned = signal("probs_turned", HEADS)
        pv_done = signal("pv_done", HEADS)
        vd_done = signal("vd_done", 1)
        rwkv_step = signal("rwkv_step", PRE_STEPS + HP * RW_STEPS + 1)
        unit_free = [signal(f"unit_free{b}", UNITS // 2, 1) for b in range(2)]
        act_chain = sem("act_chain")
        x_squared = signal("x_squared", 2)
        hT_hi_ready = signal("hT_hi_ready", 8)
        hi_ready = signal("weights_hi_ready", splits(NGR - 1))
        yb_hi_ready = signal("yb_hi_ready", 2)
        ya_hi_ready = signal("ya_hi_ready", 4)
        merged_hi_ready = signal("merged_hi_ready", 8)
        lo_act = signal("lora_inputs_scaled", 1)
        lo_ready = signal("lora_inputs_ready", 1)
        x2_act = signal("x2_act", 2)
        z_tanh = signal("z_tanh", 8)
        kvr_act = signal("kvr_scaled", 12)
        wo_sq = signal("wo_squared", 8)
        hid_sq = signal("hidden_squared", 2)
        hid_tanh = signal("hidden_tanh", 2)
        hidT_ready = signal("hidden_channelmajor", 1)
        kcraw_ready = signal("kcraw_ready", 1)
        vc_ready = signal("vc_ready", 1)
        exps_done = signal("exps_done", HEADS)
        pt_act = signal("pt_act", HEADS)
        vd_ready = signal("vd_ready", 1)
        q2_ready = signal("q2_ready", HP)
        tok_ready = signal("bet_kha_tokenmajor", HP)
        q4_ready = signal("q4_ready", HP)
        v1_ready = signal("v1_ready", HP)
        xt_ready = signal("xt_ready", 2 * HP)
        wx_ready = signal("wx_ready", 2 * HP)
        rhs_ready = signal("rhs_ready", NCH * HP)
        u_ready = signal("u_ready", NCH * HP)
        ksq_ready = signal("ksq_ready", 1)
        lora_read = signal("lora_read", HP)
        tv_ready = signal("tv_ready", HP)
        decays_ready = signal("decays_ready", HP)
        norms_ready = signal("kk_norms_ready", 1)
        ysq_ready = signal("ysq_ready", HP)
        yt_ready = signal("yt_ready", HP)
        dve_chain = sem("dve_chain")
        sin_arg = sem("sin_arg")
        table_ready = sem("table_ready")
        ms_ready = signal("ms_ready", 2)
        diag_ready = signal("diag_ready", 2)
        hT_ready = signal("hT_ready", 8)
        lo_weights = signal("weights_lo_ready", splits(NGR - 1))
        yb_lo_ready = signal("yb_lo_ready", 2)
        ya_lo_ready = signal("ya_lo_ready", 4)
        merged_lo_ready = signal("merged_lo_ready", 8)
        vf_read = signal("v_first_read", HP)
        xw_ready = signal("xw_ready", 2)
        kd_ready = signal("kd_ready", 8)
        qr_ready = signal("qr_ready", 4)
        hid_arg = signal("hidden_arg", 2)
        hid_ready = signal("hid_ready", 2)
        kc_ready = signal("kc_ready", 1)
        sc_ready = signal("scores_masked", HEADS)
        cf_ready = signal("coef_ready", HEADS)
        pt_dve = signal("pt_dve", HEADS)
        yb_ready = signal("yb_ready", HP)
        q_masked = signal("q_masked", HP)
        m_masked = signal("m_masked", HP)
        v_ready = signal("v_stack_ready", HP)
        x_step = signal("x_step", 4 * HP)
        t_ready = signal("t_ready", HP)
        bonus_ready = signal("bonus_ready", HP)
        z_ready = signal("z_ready", (NCH - 1) * HP)
        scan_done = signal("scan_done", HP)
        inverse_ready = signal("kk_inverse_norms_ready", 1)
        nk_ready = signal("unit_kk_ready", HP)
        mid_ready = signal("mid_ready", HP)
        ew_dve = signal("ew_dve", HP)
        yc_ready = signal("yc_ready", HP)
        var_ready = signal("var_ready", HP)
        ybd_ready = signal("ybd_ready", HP)
        ya_ready = signal("ya_ready", HP)
        merged_ready = signal("merged_ready", 8)
        ms2_ready = signal("ms2_ready", 1)
        x_new = signal("x_new", 2, 2)
        zeroed = sem("zeroed")
        pads_zero = signal("pads_zero", 1)
        derived_ready = signal("derived_ready", 1)
        rstd_ready = signal("rstd_ready", 2)
        probs_ready = signal("probs_ready", HEADS)
        x1_ready = signal("x1_ready", HP)
        lp_ready = signal("lp_ready", HP)
        ew_pool = signal("ew_pool", HP)
        grstd_ready = signal("grstd_ready", HP)
        rstd2_ready = signal("rstd2_ready", 1)

        def taken(l, u):
            return unit_free[u % 2].sem, unit_free[u % 2].at(l, u // 2 + 1)

        def done(l, u):
            return unit_done[u % 2].sem, unit_done[u % 2].at(l, u // 2 + 1)

        block = ctx.enter_context(nc.Block())
        out2 = out.rearrange("a (t p) n -> p (a t) n", p=P)
        x2 = x.rearrange("a (t p) n -> p (a t) n", p=P)

        @block.sync
        def _(sp):
            sp.dma_start(con[:, :], consts).then_inc(con_loaded, 16)
            sp.dma_start(WORK[:, 8192 + 3 * S:8192 + 4 * S].bitcast(I32), pos.to_broadcast([P, S])
                         ).then_inc(pos_loaded, 16)
            sp.dma_start(XR, x2).then_inc(x_loaded, 16)
            sp.dma_start(par[:, :], params[0, :, :]).then_inc(par_loaded.sem, 16)

            def used_up(g):
                u = unit_ended(g)
                if u is not None:
                    return unit_done[u % 2], u // 2 + 1
                if hidden_ended(g):
                    return hidden_done, g // QG - B_CK + 1
                return part_used, parts(g)

            with sp.Fori(0, LAYERS) as l:
                def load(g):
                    s = g % SLOTS
                    if g >= SLOTS:
                        before, n = used_up(g - SLOTS)
                    else:
                        before, n = used_up(g - SLOTS + NGR)
                        n -= before.per_layer
                    sp.wait_ge(before.sem, before.at(l, n))
                    sp.dma_start(w_raw[s][:, :], stream[bass.ds(l * NGR + g, 1), :, :].rearrange("a p n -> (a p) n")
                                 ).then_inc(loaded[s].sem, 16)

                def load_pair(p):
                    sp.dma_start(pair_up[:, :], ups[bass.ds(l * HP + p, 1), :, :].rearrange("a p n -> (a p) n")
                                 ).then_inc(pair_loaded.sem, 16)
                    sp.dma_start(pair_vf[:, :], v_first[0, :, p * S:(p + 1) * S]).then_inc(pair_loaded.sem, 16)

                at_pair = {QG * B_ZA + SLOTS: 1}
                for p in range(2, HP):
                    at_pair[rw_granule((p - 2) * PAIR_POINTS + SCHEDULE.index(13)) + SLOTS + 1] = p
                for g in range(NGR):
                    if g == SLOTS:
                        sp.dma_start(merged[:, 0:NATT], att_consts).then_inc(att_loaded.sem, 16)
                        sp.wait_ge(x_loaded, 16)
                        sp.wait_ge(x_new.sem, x_new.at(l, 0))
                        for t in range(2):
                            sp.dma_start(out2[:, t, :], XR[:, t, :]).then_inc(x_stored.sem, 16)
                    if g == QG * (B_K + 8) + SLOTS:
                        sp.wait_ge(*taken(l, U_K + 6))
                        sp.wait_ge(*taken(l, U_K + 7))
                        sp.dma_start(v_first[bass.ds(l, 1), :, :].rearrange("a p n -> (a p) n"),
                                     V.rearrange("p t n -> p (t n)")).then_inc(v_stored.sem, 16)
                    if g == QG * (B_K + 9) + SLOTS:
                        sp.wait_ge(v_stored.sem, v_stored.at(l, 16))
                        load_pair(0)
                    if g in at_pair:
                        sp.wait_ge(vf_read.sem, vf_read.at(l, at_pair[g]))
                        load_pair(at_pair[g])
                    if g == QG * (B_A + 2):
                        sp.wait_ge(ya_ready.sem, ya_ready.at(l, HP))
                        sp.wait_ge(x_stored.sem, x_stored.at(l, 32))
                    if g in (QG * (B_A + 2), QG * (B_A + 4)):
                        t = (g - QG * (B_A + 2)) // (2 * QG)
                        sp.dma_start(XR[:, t, :], out2[:, t, :]).then_inc(xr_loaded.sem, 16)
                    if g == QG * (B_A + 6):
                        sp.dma_start(GPOST, norm_post[bass.ds(l, 1), :].to_broadcast([P, D])
                                     ).then_inc(xr_loaded.sem, 16)
                    if g == QG * (B_A + 8):
                        sp.dma_start(par[:, :], params[bass.ds(l + 1, 1), :, :].rearrange("a p n -> (a p) n")
                                     ).then_inc(par_loaded.sem, 16)
                    load(g)
            for t in range(2):
                sp.wait_ge(x_new.sem, x_new.at(LAYERS, t - 1))
                sp.dma_start(out2[:, t, :], XR[:, t, :]).then_inc(x_stored.sem, 16)
            sp.wait_ge(x_stored.sem, (LAYERS + 1) * 32)
            sp.wait_ge(par_loaded.sem, (LAYERS + 1) * 16)

        def pe_layer(pe, l):
            mm = pe.matmul

            def take(g):
                s = g % SLOTS
                if native(g):
                    pe.wait_ge(loaded[s].sem, loaded[s].at(l, 16 * (g // SLOTS + 1)))
                    return [w_raw[s]]
                pe.wait_ge(lo_weights.sem, lo_weights.at(l, splits(g)))
                return [w_hi[s], w_lo[s]]

            def multiply(o, lhs, rhs, start, stop):
                if len(lhs) == 1:
                    return mm(o, lhs[0], rhs[0], start=start, stop=stop)
                mm(o, lhs[0], rhs[0], start=start, stop=False)
                mm(o, lhs[0], rhs[1], start=False, stop=False)
                return mm(o, lhs[1], rhs[0], start=False, stop=stop)

            def part(ins, g):
                if unit_ended(g) is None and not hidden_ended(g):
                    ins.then_inc(part_used.sem, 1)

            def start_unit(u):
                pe.wait_ge(unit_free[u % 2].sem, unit_free[u % 2].at(l, u // 2))
                return PB[u % 2]

            def start_out(n, t):
                u = U_WO + 2 * n + t
                if n != 1:
                    before = u // 2 - (n >= 2)
                    pe.wait_ge(unit_free[t].sem, unit_free[t].at(l, before))

            def end_unit(ins, u):
                ins.then_inc(unit_done[u % 2].sem, 1)

            def point(kind, i):
                if kind == "att":
                    attention(i)
                if kind == "rwkv":
                    rwkv(i)

            def product(b, u, rhs, kind=None, first=0, every=16, chunks=KC, tiles=(0, 1)):
                o, n = start_unit(u), 0
                for j, tile in enumerate(tiles):
                    for c in range(chunks):
                        g, i = b * QG + (tile * chunks + c) // 8, c % 8
                        if i == 0:
                            w = take(g)
                        ins = multiply(o[:, j * S:(j + 1) * S], [a[:, i * P:(i + 1) * P] for a in w],
                                       [a[c] if isinstance(a, list) else a[:, c, :] for a in rhs],
                                       c == 0, c == chunks - 1)
                        n += 1
                        if n == chunks * len(tiles):
                            end_unit(ins, u)
                        elif i == 7:
                            part(ins, g)
                        if kind and n % every == 0:
                            point(kind, first + n // every - 1)

            for half in range(2):
                for t in range(2):
                    if half == 0:
                        pe.wait_ge(diag_ready.sem, diag_ready.at(l, t + 1))
                    for j in range(4 * half, 4 * half + 4):
                        if half and t == 0:
                            pe.wait_ge(hT_ready.sem, hT_ready.at(l, j - 3))
                        for c in range(2):
                            at = c * S + t * P
                            ins = mm(A[j % 4][:, at:at + P], XR[:, t, (2 * j + c) * P:(2 * j + c + 1) * P],
                                     RDIAG[:, t, :], start=True, stop=True)
                        if t == 1:
                            ins.then_inc(hT_turned.sem, 1)

            lo_out = start_unit(U_LO), A[4]
            gate_out = start_unit(U_GATE), A[5]
            for q in range(QG):
                pe.wait_ge(hT_ready.sem, hT_ready.at(l, 2 * q + 2))
                w = take(QG * B_LOG + q)
                for j in range(2):
                    for i in range(4):
                        c = 4 * q + i
                        ins = multiply(lo_out[j][0:LORA_W, 0:S],
                                       [a[:, i * 256 + j * LORA_W:i * 256 + (j + 1) * LORA_W] for a in w],
                                       [a[:, c, :] for a in hT], c == 0, c == KC - 1)
                if q == QG - 1:
                    end_unit(ins, U_LO)
                for t in range(2):
                    for i in range(4):
                        c = 4 * q + i
                        ins = multiply(gate_out[t][:, 0:48], [a[:, c, t * P:(t + 1) * P] for a in hT],
                                       [a[:, i * 256 + 192:i * 256 + 240] for a in w], c == 0, c == KC - 1)
                part(ins, QG * B_LOG + q)
            end_unit(ins, U_GATE)

            for b, u in ((B_KC, U_KC), (B_VC, U_VC), (B_KS, U_KS), (B_KW, U_KW)):
                product(b, u, hT)

            def token_major(g0, u0, lhs, banks, ready=None):
                for q in range(KC // 2):
                    if ready:
                        pe.wait_ge(ready.sem, ready.at(l, q + 1))
                    w = take(g0 + q)
                    for t in range(2):
                        for i in range(2):
                            c = 2 * q + i
                            ins = multiply(banks[t][:, :], [a[:, c, t * P:(t + 1) * P] for a in lhs],
                                           [a[:, i * 512:(i + 1) * 512] for a in w], c == 0, c == KC - 1)
                        if c == KC - 1:
                            end_unit(ins, u0 + t)
                    part(ins, g0 + q)

            token_major(QG * B_VT, U_VT, hT, (start_unit(U_VT), start_unit(U_VT + 1)))

            def k_rope(n):
                src, tile, gg = n // 4, (n % 4) // 2, n % 2
                if n == 0:
                    pe.wait_ge(att_loaded.sem, att_loaded.at(l, 16))
                if n % 4 == 0:
                    pe.wait_ge(*taken(l, U_KS + src))
                if n >= 4:
                    pe.wait_ge(kd_ready.sem, kd_ready.at(l, n - 3))
                raw = KRAW[:, src * 512 + tile * S:src * 512 + (tile + 1) * S]
                for r in range(2):
                    ins = mm(A[n % 4][:, r * S:(r + 1) * S], av("dup", (2 * gg + r) * P, (2 * gg + r + 1) * P), raw,
                             start=True, stop=True)
                ins.then_inc(krope_done.sem, 1)

            def q_rope(j):
                pe.wait_ge(*taken(l, U_Q + j))
                if j >= 2:
                    pe.wait_ge(qr_ready.sem, qr_ready.at(l, j - 1))
                mm(A[4 + j % 2][:, :], av("rot"), QRAW[:, (j % 2) * 512:(j % 2 + 1) * 512], start=True, stop=True
                   ).then_inc(qrope_done.sem, 1)

            for j in range(4):
                product(B_Q + j, U_Q + j, hT)
                k_rope(2 * j)
                k_rope(2 * j + 1)
                if j >= 1:
                    q_rope(j - 1)
            for i in range(2):
                pe.wait_ge(xw_ready.sem, xw_ready.at(l, i + 1))
                if i == 0:
                    pe.wait_ge(kd_ready.sem, kd_ready.at(l, 8))
                for m in range(CMP // 2):
                    g = QG * (B_CK + i) + m // 4
                    if m % 4 == 0:
                        w, = take(g)
                    ins = mm(A[i][0:NCG, 0:S], XW[:, i, m, :], w[:, m % 4 * 256:(m % 4 + 1) * 256],
                             start=(m == 0), stop=(m == CMP // 2 - 1))
                    if m % 4 == 3:
                        part(ins, g)
                ins.then_inc(hidden_done.sem, 1)
            q_rope(3)
            product(B_ZB, U_ZB, hT)
            pe.wait_ge(hid_ready.sem, hid_ready.at(l, 2))
            for i in range(2):
                for hh in range(2):
                    at = (2 * i + hh) * 64
                    ins = mm(A[2][:, at:at + NCG], HR[0:NCG, i * 256 + hh * P:i * 256 + (hh + 1) * P],
                             cv("ident")[0:NCG, 0:NCG], start=True, stop=True)
            ins.then_inc(hidden_turned.sem, 1)
            product(B_ZB + 1, U_ZB + 1, hT)
            pe.wait_ge(hidT_ready.sem, hidT_ready.at(l, 1))
            pe.wait_ge(derived_ready.sem, derived_ready.at(l, 1))
            for hh in range(2):
                ins = mm(A[2][:, 0:NCG], w2kd[:, hh * P:(hh + 1) * P], HIDK[:, hh * NCG:(hh + 1) * NCG],
                         start=(hh == 0), stop=(hh == 1))
            ins.then_inc(cmp_done.sem, 1)
            product(B_ZB + 2, U_ZB + 2, hT)
            pe.wait_ge(kcraw_ready.sem, kcraw_ready.at(l, 1))
            mm(A[2][:, 64:64 + NCG], av("rot"), KCR[:, 0:NCG], start=True, stop=True).then_inc(cmp_done.sem, 1)
            for g in range(NG):
                for hh in range(2):
                    ins = mm(A[3][0:NCMP, g * HD:(g + 1) * HD],
                             HIDV[:, hh * NCG + g * NCMP:hh * NCG + (g + 1) * NCMP],
                             pv("w2v", hh * HD, (hh + 1) * HD), start=(hh == 0), stop=(hh == 1))
            ins.then_inc(cmp_done.sem, 1)
            product(B_ZB + 3, U_ZB + 3, hT)
            pe.wait_ge(qr_ready.sem, qr_ready.at(l, 4))
            pe.wait_ge(kc_ready.sem, kc_ready.at(l, 1))
            pe.wait_ge(vc_ready.sem, vc_ready.at(l, 1))
            pe.wait_ge(*taken(l, U_VT))
            pe.wait_ge(*taken(l, U_VT + 1))

            def scores(h):
                g, tile, a = h // 4, h // 2, (h % 2) * HD
                if h >= 1:
                    pe.wait_ge(sc_ready.sem, sc_ready.at(l, h))
                for qt in range(2):
                    q = QR[a:a + HD, tile, qt * P:(qt + 1) * P]
                    n = P * (qt + 1)
                    for r in range(2):
                        mm(A[qt][:, r * n:(r + 1) * n], q, KD[a:a + HD, 4 * r + g, 0:n], start=True, stop=True)
                for qt in range(2):
                    q = QR[a:a + HD, tile, qt * P:(qt + 1) * P]
                    ins = mm(A[0][:, 256 + 16 * qt:256 + 16 * qt + NCMP], q, KCd[a:a + HD, g * NCMP:(g + 1) * NCMP],
                             start=True, stop=True)
                ins.then_inc(scores_done.sem, 1)

            def turn_probs(h):
                pe.wait_ge(probs_ready.sem, probs_ready.at(l, h + 1))
                if h >= 1:
                    pe.wait_ge(pt_act.sem, pt_act.at(l, h))
                    pe.wait_ge(pt_dve.sem, pt_dve.at(l, h))
                b = h % 2
                pe.transpose(A[2][:, 384:512], PC[:, b, :, :], cv("ident"))
                for r in range(2):
                    pe.transpose(A[2 + r][:, 0:128], SC0[:, b, r, :], cv("ident"))
                    pe.transpose(A[2 + r][:, 128:256], SC1[:, b, r, 0:128], cv("ident"))
                    ins = pe.transpose(A[2 + r][:, 256:384], SC1[:, b, r, 128:256], cv("ident"))
                ins.then_inc(probs_turned.sem, 1)

            def weigh_values(h):
                g, a = h // 4, (h % 2) * HD
                pe.wait_ge(pt_act.sem, pt_act.at(l, h + 1))
                pe.wait_ge(pt_dve.sem, pt_dve.at(l, h + 1))
                if h >= 4 and h % 2 == 0:
                    pe.wait_ge(yb_ready.sem, yb_ready.at(l, h // 2 - 1))
                full, lo, hi = (A[4 + (h // 2) % 2][a:a + HD, s:e] for s, e in ((0, S), (0, P), (P, S)))
                mm(full, VTM[:, 0, g * HD:(g + 1) * HD], PT[:, 0:256], start=True, stop=False)
                mm(hi, VTM[:, 1, g * HD:(g + 1) * HD], PT[:, 256:384], start=False, stop=False)
                mm(lo, VC[:, 0, g, :], PT[:, 384:512], start=False, stop=False)
                mm(hi, VC[:, 1, g, :], PT[:, 384:512], start=False, stop=False)
                mm(full, VTM[:, 0, 256 + g * HD:256 + (g + 1) * HD], PT[:, 512:768], start=False, stop=False)
                mm(hi, VTM[:, 1, 256 + g * HD:256 + (g + 1) * HD], PT[:, 768:896], start=False, stop=True
                   ).then_inc(pv_done.sem, 1)

            def lora(p):
                pe.wait_ge(pair_loaded.sem, pair_loaded.at(l, 32 * (p + 1)))
                mm(A[3][:, 0:S], pair_up[0:LORA_W, 0:P], LO[0:LORA_W, 0:S], start=True, stop=True)
                return mm(A[3][:, S:2 * S], pair_up[0:LORA_W, P:2 * P], LO[0:LORA_W, S:2 * S], start=True, stop=True)

            def norms(p):
                mm(A[1][:, 0:S], pair_up[0:LORA_V, 2 * P:3 * P], VD[0:LORA_V, :], start=True, stop=True)
                return mm(A[1][:, S:2 * S], pair_up[LORA_V:LORA_V + HEADS, 2 * P:3 * P], NI, start=True, stop=True)

            def attention(i):
                if 3 <= i < HEADS + 3:
                    weigh_values(i - 3)
                if 2 <= i < HEADS + 2:
                    turn_probs(i - 2)
                if i < HEADS:
                    scores(i)
                if i == PRE_POINT:
                    pe.wait_ge(yb_ready.sem, yb_ready.at(l, HP))
                    pe.wait_ge(*taken(l, U_K + 6))
                    pe.wait_ge(*taken(l, U_K + 7))
                    pe.wait_ge(ksq_ready.sem, ksq_ready.at(l, 1))
                    for p in range(HP):
                        lo = CON["headcol"][0] + 14 - 2 * p
                        mm(A[5][LORA_V:LORA_V + HEADS, S:2 * S], con[:, lo:lo + HEADS], KSQ[:, p, :],
                           start=(p == 0), stop=(p == HP - 1))
                    for c in range(HP):
                        ins = mm(A[5][0:LORA_V, 0:S], pv("v_down", c * LORA_V, (c + 1) * LORA_V), V[:, c, :],
                                 start=(c == 0), stop=(c == HP - 1))
                    ins.then_inc(vd_done.sem, 1)
                    pe.wait_ge(lo_ready.sem, lo_ready.at(l, 1))
                    lora(0).then_inc(rwkv_step.sem, 1)
                if i == PRE_POINT + 1:
                    pe.wait_ge(vd_ready.sem, vd_ready.at(l, 1))
                    pe.wait_ge(inverse_ready.sem, inverse_ready.at(l, 1))
                    norms(0).then_inc(rwkv_step.sem, 1)

            for u in range(12):
                product(B_K + u, U_K + u, hT, "att", 2 * u)

            def four(o, lhs, rhs, turn=False):
                for c in range(NCH):
                    if turn:
                        ins = pe.transpose(quad(o)[:, c, :], lhs[:, c, :], cv("ident"))
                    else:
                        ins = mm(quad(o)[:, c, :], lhs[:, c, :], rhs[:, c, :], start=True, stop=True)
                return ins

            def turn_y(p):
                pe.wait_ge(ybd_ready.sem, ybd_ready.at(l, p + 1))
                for c in range(NCH):
                    ins = mm(A[2][:, c * CH:(c + 1) * CH], Ybd[:, c, :], cv("ident2"), start=True, stop=True)
                return ins

            def rwkv_pair(p, k):
                kap, rho = KR[:, p % 2, :, 0:P], KR[:, p % 2, :, P:2 * P]
                wait = pe.wait_ge
                if k == 0:
                    wait(ew_dve.sem, ew_dve.at(l, p + 1))
                    wait(ew_pool.sem, ew_pool.at(l, p + 1))
                    if p:
                        wait(z_ready.sem, z_ready.at(l, 3 * p))
                    four(A[0], BB, kap)
                    ins = four(A[1], kap, BB)
                elif k == 1:
                    if p:
                        wait(yc_ready.sem, yc_ready.at(l, p))
                    four(A[2], BB, rho)
                    four(A[3], KA, kap)
                    ins = four(A[4], KA, rho)
                elif k == 2:
                    ins = four(A[5], VDUP, None, True)
                elif k == 3:
                    wait(q_masked.sem, q_masked.at(l, p + 1))
                    four(A[0], QdT, Qd)
                    ins = four(A[1], Qd, QdT)
                elif k == 4:
                    wait(m_masked.sem, m_masked.at(l, p + 1))
                    four(A[2], BB, None, True)
                    ins = four(A[3], KA, None, True)
                elif k == 5:
                    wait(q2_ready.sem, q2_ready.at(l, p + 1))
                    wait(x1_ready.sem, x1_ready.at(l, p + 1))
                    four(A[4], Q2T, X)
                    ins = four(A[0], Q2, Q2T)
                elif k == 6:
                    ins = mm(A[1][:, 0:S], cv("ones"), RKK, start=True, stop=True)
                elif k == 7:
                    wait(q4_ready.sem, q4_ready.at(l, p + 1))
                    if p:
                        wait(tok_ready.sem, tok_ready.at(l, p + 1))
                        turn_y(p - 1)
                    wait(x_step.sem, x_step.at(l, 4 * p + 1))
                    ins = four(A[4], Q4T, X)
                elif k == 8:
                    wait(x_step.sem, x_step.at(l, 4 * p + 2))
                    wait(v_ready.sem, v_ready.at(l, p + 1))
                    ins = four(A[5], Q4T, X)
                elif k == 9:
                    if p + 1 < HP:
                        wait(tok_ready.sem, tok_ready.at(l, p + 1))
                        lora(p + 1)
                    wait(v1_ready.sem, v1_ready.at(l, p + 1))
                    ins = four(A[4], Q4T, WX)
                elif k == 10 or k == 13:
                    wait(x_step.sem, x_step.at(l, 4 * p + (3 if k == 10 else 4)))
                    ins = four(A[5], X, None, True)
                elif k == 11:
                    if p + 1 < HP:
                        wait(bonus_ready.sem, bonus_ready.at(l, p + 1))
                        norms(p + 1)
                    ins = four(A[0], QT32, X)
                elif k == 12:
                    wait(xt_ready.sem, xt_ready.at(l, 2 * p + 1))
                    wait(wx_ready.sem, wx_ready.at(l, 2 * p + 1))
                    ins = four(A[4], XT, WX)
                elif k == 14:
                    four(A[0], QT64, X)
                    if p + 1 < HP:
                        wait(lora_read.sem, lora_read.at(l, p + 2))
                    else:
                        wait(tok_ready.sem, tok_ready.at(l, p + 1))
                    ins = mm(A[3][:, 0:CH], Mak[:, 0, :], Vst[:, 0, :], start=True, stop=True)
                elif k == 15:
                    wait(xt_ready.sem, xt_ready.at(l, 2 * p + 2))
                    wait(wx_ready.sem, wx_ready.at(l, 2 * p + 2))
                    ins = four(A[4], XT, WX)
                elif k % 3 == 0:
                    c = (k - 15) // 3
                    wait(z_ready.sem, z_ready.at(l, 3 * p + c))
                    mm(A[3][:, c * CH:(c + 1) * CH], kap[:, c, :], Z, start=True, stop=False)
                    ins = mm(A[3][:, c * CH:(c + 1) * CH], Mak[:, c, :], Vst[:, c, :], start=False, stop=True)
                elif k % 3 == 1:
                    c = (k - 16) // 3
                    if c == 0:
                        wait(t_ready.sem, t_ready.at(l, p + 1))
                    wait(rhs_ready.sem, rhs_ready.at(l, NCH * p + c + 1))
                    ins = mm(A[3][:, 256 + c * CH:256 + (c + 1) * CH], TT[:, c, :], RHS, start=True, stop=True)
                else:
                    c = (k - 17) // 3
                    y, z = A[2][:, c * CH:(c + 1) * CH], A[1][:, 256 + c * CH:256 + (c + 1) * CH]
                    wait(u_ready.sem, u_ready.at(l, NCH * p + c + 1))
                    if c == 0:
                        wait(tok_ready.sem, tok_ready.at(l, p + 1))
                        if p:
                            wait(yt_ready.sem, yt_ready.at(l, p))
                        if p + 1 < HP:
                            wait(tv_ready.sem, tv_ready.at(l, p + 2))
                            wait(nk_ready.sem, nk_ready.at(l, p + 2))
                    else:
                        mm(y, rho[:, c, :], Z, start=True, stop=False)
                    mm(y, Mrb[:, c, :], Uc, start=(c == 0), stop=False)
                    ins = mm(y, Mrk[:, c, :], Vst[:, c, :], start=False, stop=True)
                    if c + 1 < NCH:
                        mm(z, BBt[:, c, :], Uc, start=True, stop=False)
                        ins = mm(z, KAt[:, c, :], Vst[:, c, :], start=False, stop=True)
                ins.then_inc(rwkv_step.sem, 1)

            def rwkv(i):
                p, k = i // PAIR_POINTS, SCHEDULE[i % PAIR_POINTS]
                if k is not None:
                    rwkv_pair(p, k)

            for u in range(4):
                product(B_ZA + u, U_ZA + u, hT, "rwkv", 16 * u, 2)
            for u in range(8):
                product(B_MGB + u, U_MGB + u, hT, "rwkv", 64 + 16 * u, 2)
            pe.wait_ge(yb_lo_ready.sem, yb_lo_ready.at(l, 2))
            for u in range(8):
                product(B_PB + u // 2, U_PB + u, [yb_hi, yb_lo], "rwkv", 192 + 8 * u, 2, HP,
                        (2 * (u % 2), 2 * (u % 2) + 1))
            for j in range(4):
                product(B_A + 3 * j, U_A + 4 * j, hT)
                if j == 0:
                    turn_y(HP - 1).then_inc(rwkv_step.sem, 1)
                product(B_A + 3 * j + 1, U_A + 4 * j + 1, hT)
                if j == 0:
                    pe.wait_ge(ya_lo_ready.sem, ya_lo_ready.at(l, 4))
                for i in range(2):
                    product(B_A + 3 * j + 2, U_A + 4 * j + 2 + i, [ya_hi, ya_lo], None, 0, 16, HP, (2 * i, 2 * i + 1))
            for n in range(4):
                start_out(n, 0)
                start_out(n, 1)
                token_major(QG * (B_WO + 2 * n), U_WO + 2 * n, [merged_hi, merged_lo], out_banks(n),
                            merged_lo_ready if n == 0 else None)

        @block.tensor
        def _(pe):
            for s in unit_done + unit_free + [part_used]:
                pe.sem_inc(s.sem, s.ahead)
            pe.sem_inc(x_new.sem, x_new.ahead)
            pe.wait_ge(con_loaded, 16)
            pe.wait_ge(zeroed, 1)
            with pe.Fori(0, LAYERS) as l:
                pe_layer(pe, l)

        def act_layer(act, l, chain):
            wait = act.wait_ge

            def copy(o, i, scale=1.0):
                return act.activation(o, i, ACT.Copy, scale=scale)

            def flat(a):
                return a.rearrange("p a b -> p (a b)")

            split_next = [0]

            def split_to(last):
                for g in range(split_next[0], min(last, NGR - 1) + 1):
                    if not native(g):
                        s = g % SLOTS
                        wait(loaded[s].sem, loaded[s].at(l, 16 * (g // SLOTS + 1)))
                        copy(w_hi[s][:, :], w_raw[s][:, :]).then_inc(hi_ready.sem, 1)
                    split_next[0] = g + 1

            def behind(g):
                split_to(g + LEAD)

            for t in range(2):
                wait(x_new.sem, x_new.at(l, t - 1))
                act.activation(SQX[:, t, :], XR[:, t, :], ACT.Square, accum_out=small[:, t:t + 1]
                               ).then_inc(x_squared.sem, 1)
            wait(par_loaded.sem, par_loaded.at(l, 16))
            for j in range(8):
                if j % 2 == 0:
                    split_to(min(j // 2, 2))
                wait(hT_turned.sem, hT_turned.at(l, j + 1))
                for c in range(2):
                    ins = copy(hT[0][:, 2 * j + c, :], A[j % 4][:, c * S:(c + 1) * S],
                               pv("norm_pre", 2 * j + c, 2 * j + c + 1))
                ins.then_inc(hT_hi_ready.sem, 1)
            behind(QG * B_LOG + 3)
            wait(derived_ready.sem, derived_ready.at(l, 1))
            wait(*done(l, U_LO))
            for j in range(2):
                ins = copy(LO[0:LORA_W, j * S:(j + 1) * S], (PB[0], A[4])[j][0:LORA_W, 0:S],
                           omu[0:LORA_W, 24 + j:25 + j])
            ins.then_inc(lo_act.sem, 1)
            wait(*done(l, U_GATE))
            act.activation(GS[:, 1, :], A[5][:, 0:48], ACT.Tanh, scale=0.5)
            act.activation(GS[:, 0, :], PB[1][:, 0:48], ACT.Tanh, scale=0.5).then_inc(unit_free[1].sem, 1)
            wait(*taken(l, U_LO))
            act.activation(LO[0:LORA_W, 0:S], LO[0:LORA_W, 0:S], ACT.Tanh).then_inc(lo_ready.sem, 1)

            for i in range(2):
                u = U_KC + i
                behind(QG * (B_KC + i) + 3)
                wait(*done(l, u))
                src = PB[u % 2][:, :].rearrange("p (t n r) -> p t n r", t=2, r=2)
                for gg in range(2):
                    ins = copy(X2[0:HD, i, gg::2, :], src[gg * HD:(gg + 1) * HD, :, :, 0])
                ins.then_inc(x2_act.sem, 1)
            for i in range(2):
                u = U_KS + i
                behind(QG * (B_KS + i) + 3)
                wait(*done(l, u))
                copy(KRAW[:, i * 512:(i + 1) * 512], PB[u % 2][:, :]).then_inc(unit_free[u % 2].sem, 1)
            for t in range(2):
                u = U_VT + t
                behind(QG * B_VT + 7)
                wait(*done(l, u))
                copy(VTM[:, t, :], PB[u % 2][:, :]).then_inc(unit_free[u % 2].sem, 1)
            for j in range(4):
                u = U_Q + j
                behind(QG * (B_Q + j) + 3)
                wait(*done(l, u))
                if j >= 2:
                    wait(qr_ready.sem, qr_ready.at(l, j - 1))
                copy(QRAW[:, (j % 2) * 512:(j % 2 + 1) * 512], PB[u % 2][:, :]).then_inc(unit_free[u % 2].sem, 1)
            behind(QG * B_CV + 3)
            for i in range(2):
                wait(hidden_done.sem, hidden_done.at(l, i + 1))
                if i:
                    wait(hid_ready.sem, hid_ready.at(l, 1))
                act.activation(HT[0:NCG, 0:256], A[i][0:NCG, 0:256], ACT.Square).then_inc(hid_sq.sem, 1)
                wait(hid_arg.sem, hid_arg.at(l, i + 1))
                act.activation(HT[0:NCG, 256:512], HT[0:NCG, 0:256], ACT.Tanh, scale=float(np.sqrt(2 / np.pi))
                               ).then_inc(hid_tanh.sem, 1)
                split_to(QG * B_ZB + 2 + i)

            def z_pass(i, u):
                behind(QG * (B_ZB + i if i < 4 else B_ZA + i - 4) + 3)
                wait(*done(l, u))
                if i >= 1:
                    wait(*taken(l, u - 1))
                act.activation(ZT[:, :], PB[u % 2][:, :], ACT.Tanh, scale=0.5).then_inc(z_tanh.sem, 1)

            z_pass(0, U_ZB)
            wait(hidden_turned.sem, hidden_turned.at(l, 1))
            for i, hid in enumerate((HIDK, HIDV)):
                src = A[2][:, i * P:(i + 1) * P].rearrange("p (h n) -> p h n", h=2)[:, :, 0:NCG]
                ins = copy(hid.rearrange("p (h n) -> p h n", h=2), src)
            ins.then_inc(hidT_ready.sem, 1)
            z_pass(1, U_ZB + 1)
            wait(cmp_done.sem, cmp_done.at(l, 1))
            copy(KCR[:, 0:NCG], A[2][:, 0:NCG], 0.5).then_inc(kcraw_ready.sem, 1)
            z_pass(2, U_ZB + 2)
            wait(cmp_done.sem, cmp_done.at(l, 3))
            wait(zeroed, 1)
            copy(flat(VC[0:NCMP, 0, :, :]), A[3][0:NCMP, 0:256], 0.5)
            copy(flat(VC[HD:HD + NCMP, 1, :, :]), A[3][0:NCMP, 0:256], 0.5).then_inc(vc_ready.sem, 1)
            z_pass(3, U_ZB + 3)

            def lora_pass(p):
                wait(rwkv_step.sem, rwkv_step.at(l, lora_at(p)))
                act.activation(SG, A[3][:, 0:S], ACT.Tanh, bias=hw0[:, p:p + 1], scale=0.5)
                act.activation(TA, A[3][:, S:2 * S], ACT.Tanh, bias=ha0[:, p:p + 1], scale=0.5
                               ).then_inc(lora_read.sem, 1)

            def tv_pass(p):
                wait(rwkv_step.sem, rwkv_step.at(l, norms_at(p)))
                act.activation(TV, A[1][:, 0:S], ACT.Tanh, bias=hv0[:, p:p + 1], scale=0.5).then_inc(tv_ready.sem, 1)

            def decays(p):
                wait(lp_ready.sem, lp_ready.at(l, p + 1))
                chain.step(act.activation(Wd, LIW, ACT.Exp, scale=-DECAY))
                act.activation(LPW, LPW, ACT.Exp, scale=-DECAY)
                chain.settle()
                act.activation(LIW, LIW, ACT.Exp, scale=DECAY).then_inc(decays_ready.sem, 1)

            def attention(i):
                behind(att_granule(i))
                if 2 <= i < HEADS + 2:
                    wait(probs_turned.sem, probs_turned.at(l, i - 1))
                    copy(PT[:, 0:512], A[2][:, :]).then_inc(pt_act.sem, 1)
                split_to(att_granule(i) + LEAD + 1)
                if i < HEADS:
                    b = i % 2
                    wait(sc_ready.sem, sc_ready.at(l, i + 1))
                    for n, s in enumerate((SC0[:, b, 0, :], SC0[:, b, 1, :], SC1[:, b, 0, :], SC1[:, b, 1, :],
                                           PC[:, b, 0, 0:NCMP], PC[:, b, 1, 0:NCMP])):
                        ins = act.activation(s, s, ACT.Exp, bias=small[:, 12 + 6 * b + n:13 + 6 * b + n],
                                             accum_out=small[:, 24 + 6 * b + n:25 + 6 * b + n])
                        chain.step(ins)
                    chain.settle()
                    act.activation(small[:, 61:62], small[:, 24:25], ACT.Copy).then_inc(exps_done.sem, 1)
                if 9 <= i < 13:
                    wait(*taken(l, U_K + 2))
                    wait(*taken(l, U_K + 3))
                    for p in (2 * i - 18, 2 * i - 17):
                        ins = act.activation(KSQ[:, p, :], K[:, p, :], ACT.Square, scale=pv("k_k", p, p + 1))
                    if i == 12:
                        ins.then_inc(ksq_ready.sem, 1)
                if i == PRE_POINT:
                    wait(yb_ready.sem, yb_ready.at(l, HP))
                    wait(vd_done.sem, vd_done.at(l, 1))
                    act.activation(NI, A[5][LORA_V:LORA_V + HEADS, S:2 * S], ACT.Sqrt).then_inc(norms_ready.sem, 1)
                    copy(VD[0:LORA_V, :], A[5][0:LORA_V, 0:S]).then_inc(vd_ready.sem, 1)
                    lora_pass(0)
                if i == PRE_POINT + 1:
                    tv_pass(0)
                    decays(0)

            for u in range(12):
                attention(2 * u)
                behind(QG * (B_K + u) + 3)
                wait(*done(l, U_K + u))
                for t in range(2):
                    n = 2 * u + t
                    ins = copy(KVR[n // 8][:, n % 8, :], PB[u % 2][:, t * S:(t + 1) * S], omu[:, n:n + 1])
                ins.then_inc(kvr_act.sem, 1)
                attention(2 * u + 1)

            def y_pass(p):
                act.activation(V[:, p, :], A[2][:, 0:S], ACT.Identity, bias=pv("gn_b", p, p + 1),
                               scale=pv("gn_w", p, p + 1)).then_inc(yt_ready.sem, 1)

            def rwkv_pair(p, k):
                if k in (3, 4, 5, 7, 8, 9, 10, 11, 13, 14) or k >= 16:
                    wait(rwkv_step.sem, rwkv_step.at(l, rw_at(p, k)))
                nxt = p + 1 < HP
                if k == 3:
                    copy(flat(Q2), A[0][:, :])
                    copy(flat(Q2T), A[1][:, :]).then_inc(q2_ready.sem, 1)
                elif k == 4:
                    copy(flat(BBt), A[2][:, :])
                    copy(flat(KAt), A[3][:, :]).then_inc(tok_ready.sem, 1)
                elif k == 5:
                    copy(flat(Q4T), A[0][:, :]).then_inc(q4_ready.sem, 1)
                elif k == 7 and p:
                    y_pass(p - 1)
                elif k == 8:
                    copy(flat(WX), A[5][:, :]).then_inc(v1_ready.sem, 1)
                elif k == 9 and nxt:
                    lora_pass(p + 1)
                elif k == 10 or k == 13:
                    copy(flat(XT), A[5][:, :]).then_inc(xt_ready.sem, 1)
                elif k == 11:
                    copy(flat(WX), A[0][:, :]).then_inc(wx_ready.sem, 1)
                    if nxt:
                        tv_pass(p + 1)
                elif k == 12 and nxt:
                    decays(p + 1)
                elif k == 14:
                    copy(flat(WX), A[0][:, :]).then_inc(wx_ready.sem, 1)
                    copy(RHS, A[3][:, 0:CH]).then_inc(rhs_ready.sem, 1)
                elif k >= 16 and k % 3 == 1:
                    c = (k - 16) // 3
                    copy(Uc, A[3][:, 256 + c * CH:256 + (c + 1) * CH]).then_inc(u_ready.sem, 1)
                elif k >= 16 and k % 3 == 0:
                    c = (k - 15) // 3
                    copy(RHS, A[3][:, c * CH:(c + 1) * CH]).then_inc(rhs_ready.sem, 1)
                elif k == 26:
                    wait(yc_ready.sem, yc_ready.at(l, p + 1))
                    act.activation(V[:, p, :], K[:, p, :], ACT.Square).then_inc(ysq_ready.sem, 1)
                    if not nxt:
                        split_to(QG * B_A + 2)

            def rwkv(i):
                p, at = divmod(i, PAIR_POINTS)
                if SCHEDULE[at] is not None:
                    rwkv_pair(p, SCHEDULE[at])
                if p == YB_PAIR and at in YB_HI_AT:
                    half = YB_HI_AT.index(at)
                    wait(ybd_ready.sem, ybd_ready.at(l, 4))
                    wait(ya_ready.sem, ya_ready.at(l, 4))
                    for c in range(4 * half, 4 * half + 4):
                        ins = copy(yb_hi[c], ZB[:, c, :])
                    ins.then_inc(yb_hi_ready.sem, 1)
                if at in HI_AT:
                    split_to(rw_granule(p * PAIR_POINTS) + HI_AT[at])

            wait(*taken(l, U_K + 10))
            wait(*taken(l, U_K + 11))
            for u in range(4):
                for i in range(16):
                    rwkv(16 * u + i)
                z_pass(4 + u, U_ZA + u)
            for u in range(8):
                for i in range(16):
                    rwkv(64 + 16 * u + i)
                wait(*done(l, U_MGB + u))
                act.activation(flat(MB[:, 2 * u:2 * u + 2, :]), PB[u % 2][:, :], ACT.Tanh, scale=0.5
                               ).then_inc(unit_free[u % 2].sem, 1)
            for i in range(192, 256):
                rwkv(i)
            behind(QG * B_A + 3)
            wait(rwkv_step.sem, rwkv_step.at(l, rw_at(HP, 0)))
            y_pass(HP - 1)

            wait(ya_ready.sem, ya_ready.at(l, HP))
            for n in range(4):
                copy(flat(ya_hi[:, 2 * n:2 * n + 2, :]), flat(ZA[:, 2 * n:2 * n + 2, :])).then_inc(ya_hi_ready.sem, 1)

            def merged_high(j):
                for n in (2 * j, 2 * j + 1):
                    wait(merged_ready.sem, merged_ready.at(l, n + 1))
                    copy(flat(merged_hi[:, 2 * n:2 * n + 2, :]), flat(MB[:, 2 * n:2 * n + 2, :])
                         ).then_inc(merged_hi_ready.sem, 1)

            for j in range(4):
                if j >= 2:
                    wait(merged_ready.sem, merged_ready.at(l, 2 * j - 2))
                for i in range(2):
                    u = U_A + 4 * j + i
                    behind(QG * (B_A + 3 * j + i) + 3)
                    wait(*done(l, u))
                    act.activation(GAB[:, j % 2, i * 512:(i + 1) * 512], PB[u % 2][:, :], ACT.Tanh, scale=0.5
                                   ).then_inc(unit_free[u % 2].sem, 1)
                if j:
                    merged_high(j - 1)
            behind(QG * (B_A + 11) + 4)
            merged_high(3)
            for n in range(4):
                behind(QG * (B_WO + 2 * n) + 7)
                for t in range(2):
                    u = U_WO + 2 * n + t
                    wait(*done(l, u))
                    if n or t:
                        wait(wo_sq.sem, wo_sq.at(l, 2 * n + t))
                    act.activation(SQJ, out_banks(n)[t][:, :], ACT.Square,
                                   accum_out=small[:, 40 + 4 * t + n:41 + 4 * t + n]).then_inc(wo_sq.sem, 1)

        @block.scalar
        def _(act):
            chain = Chain(act, act_chain)
            act.wait_ge(sin_arg, 1)
            act.activation(cs[:, :], cs[:, :], ACT.Sin).then_inc(table_ready, 1)
            act.wait_ge(x_loaded, 16)
            act.wait_ge(zeroed, 1)
            with act.Fori(0, LAYERS) as l:
                act_layer(act, l, chain)
                chain.restart()

        def dve_layer(dve, l, chain):
            wait = dve.wait_ge
            stt, tt, ts = dve.scalar_tensor_tensor, dve.tensor_tensor, dve.tensor_scalar

            def op(ins):
                chain.step(ins)
                chain.settle()

            def flat(a):
                return a.rearrange("p a b -> p (a b)")

            def view2(ap, n):
                return ap.rearrange("p (t n) -> p t n", t=n)

            split_next = [0]

            def split_to(last):
                for g in range(split_next[0], min(last, NGR - 1) + 1):
                    if not native(g):
                        s = g % SLOTS
                        wait(hi_ready.sem, hi_ready.at(l, splits(g)))
                        tt(w_lo[s][:, :], w_raw[s][:, :], w_hi[s][:, :].bitcast(F32), ALU.subtract
                           ).then_inc(lo_weights.sem, 1)
                    split_next[0] = g + 1

            def behind(g):
                split_to(g + LEAD)

            def low(o, whole, hi):
                return tt(flat(o), flat(whole), flat(hi).bitcast(F32), ALU.subtract)

            for t in range(2):
                wait(x_squared.sem, x_squared.at(l, t + 1))
                ts(small[:, 2 + t:3 + t], small[:, t:t + 1], 1.0 / D, NORM_EPS, ALU.mult, ALU.add
                   ).then_inc(ms_ready.sem, 1)
                wait(rstd_ready.sem, rstd_ready.at(l, t + 1))
                ts(RDIAG[:, t, :], cv("ident"), small[:, 4 + t:5 + t], None, ALU.mult).then_inc(diag_ready.sem, 1)
            wait(par_loaded.sem, par_loaded.at(l, 16))
            for j in range(8):
                if j % 2 == 0:
                    split_to(min(j // 2, 2))
                wait(hT_hi_ready.sem, hT_hi_ready.at(l, j + 1))
                for c in range(2):
                    ins = stt(hT[1][:, 2 * j + c, :], A[j % 4][:, c * S:(c + 1) * S],
                              pv("norm_pre", 2 * j + c, 2 * j + c + 1), hT[0][:, 2 * j + c, :].bitcast(F32),
                              ALU.mult, ALU.subtract)
                ins.then_inc(hT_ready.sem, 1)
            behind(QG * B_LOG + 3)
            wait(lo_act.sem, lo_act.at(l, 1))
            for j in range(2):
                ins = stt(LO[0:LORA_W, j * S + 1:(j + 1) * S], (PB[0], A[4])[j][0:LORA_W, 0:S - 1],
                          pv("mu", 24 + j, 25 + j)[0:LORA_W, :], LO[0:LORA_W, j * S + 1:(j + 1) * S], ALU.mult, ALU.add)
            ins.then_inc(unit_free[0].sem, 1)
            wait(*taken(l, U_GATE))
            for i, (qt, br) in enumerate(((0, 1), (0, 2), (1, 1), (1, 2), (0, 0), (1, 0))):
                chain.step(ts(gates[:, :, i], GS[:, qt, br * HEADS:(br + 1) * HEADS], 0.5, 0.5, ALU.mult, ALU.add))
            chain.settle()
            chain.step(ts(gates[:, :, 4], gates[:, :, 4], cv("rowok"), None, ALU.mult))

            for i in range(2):
                u = U_KC + i
                behind(QG * (B_KC + i) + 3)
                wait(x2_act.sem, x2_act.at(l, i + 1))
                src = PB[u % 2][:, :].rearrange("p (t n r) -> p t n r", t=2, r=2)
                for gg in range(2):
                    ins = dve.tensor_copy(X2[HD:P, i, gg::2, :], src[gg * HD:(gg + 1) * HD, :, :, 1])
                ins.then_inc(unit_free[u % 2].sem, 1)
                wait(*taken(l, u))
                for m in range(CMP // 2):
                    ins = ts(view2(XW[:, i, m, :], NG), X2[:, i, :, m:m + 8 * (NCMP - 1) + 1:8],
                             pv("pe_k" if i == 0 else "pe_v", m, m + 1), None, ALU.add)
                    if m == 7:
                        split_to(QG * (B_KC + i) + 3 + LEAD + 1)
                ins.then_inc(xw_ready.sem, 1)

            wait(x_stored.sem, x_stored.at(l, 32))
            wait(att_loaded.sem, att_loaded.at(l, 16))
            for j in range(5):
                behind(QG * (B_Q + j) + 3 if j < 4 else QG * B_CV + 3)
                if j < 4:
                    for n in (2 * j, 2 * j + 1):
                        wait(krope_done.sem, krope_done.at(l, n + 1))
                        chain.step(tt(RT[:, 0:S], A[n % 4][:, 0:S], cosT, ALU.mult))
                        chain.step(tt(RT[:, S:2 * S], A[n % 4][:, S:2 * S], sinT, ALU.mult))
                        chain.settle()
                        tt(KD[:, n, :], RT[:, 0:S], RT[:, S:2 * S], ALU.add).then_inc(kd_ready.sem, 1)
                        wait(kd_ready.sem, kd_ready.at(l, n + 1))
                if j >= 1:
                    q = j - 1
                    wait(qrope_done.sem, qrope_done.at(l, q + 1))
                    chain.step(tt(view2(RT[:, 0:512], 2), view2(QRAW[:, (q % 2) * 512:(q % 2 + 1) * 512], 2),
                                  spread(cosT, 2, S), ALU.mult))
                    chain.step(tt(view2(RT[:, 512:1024], 2), view2(A[4 + q % 2][:, :], 2), spread(sinT, 2, S),
                                  ALU.mult))
                    chain.settle()
                    tt(flat(QR[:, 2 * q:2 * q + 2, :]), RT[:, 0:512], RT[:, 512:1024], ALU.add
                       ).then_inc(qr_ready.sem, 1)
                    wait(qr_ready.sem, qr_ready.at(l, q + 1))
            for i in range(2):
                x, poly, th = A[i][0:NCG, 0:256], HT[0:NCG, 0:256], HT[0:NCG, 256:512]
                wait(hid_sq.sem, hid_sq.at(l, i + 1))
                op(ts(poly, poly, 0.044715, 1.0, ALU.mult, ALU.add))
                tt(poly, poly, x, ALU.mult).then_inc(hid_arg.sem, 1)
                wait(hid_tanh.sem, hid_tanh.at(l, i + 1))
                stt(HR[0:NCG, i * 256:(i + 1) * 256], th, 1.0, x, ALU.add, ALU.mult).then_inc(hid_ready.sem, 1)
                split_to(QG * B_ZB + 2 + i)

            def silu(i, u, z, tile):
                behind(QG * (B_ZB + i if i < 4 else B_ZA + i - 4) + 3)
                wait(z_tanh.sem, z_tanh.at(l, i + 1))
                stt(flat(z[:, tile:tile + 2, :]), ZT[:, :], 1.0, PB[u % 2][:, :], ALU.add, ALU.mult
                    ).then_inc(unit_free[u % 2].sem, 1)

            silu(0, U_ZB, ZB, 0)
            silu(1, U_ZB + 1, ZB, 2)
            silu(2, U_ZB + 2, ZB, 4)
            wait(cmp_done.sem, cmp_done.at(l, 2))
            wait(kcraw_ready.sem, kcraw_ready.at(l, 1))
            ends = slice(CMP - 1, CMP - 1 + CSTR * (NCMP - 1) + 1, CSTR)
            chain.step(tt(view2(RT[:, 0:NCG], NG), view2(KCR[:, 0:NCG], NG), spread(cosT[:, ends], NG, NCMP), ALU.mult))
            chain.step(tt(view2(RT[:, 64:64 + NCG], NG), view2(A[2][:, 64:64 + NCG], NG),
                          spread(sinT[:, ends], NG, NCMP), ALU.mult))
            chain.settle()
            tt(KCd, RT[:, 0:NCG], RT[:, 64:64 + NCG], ALU.add).then_inc(kc_ready.sem, 1)
            silu(3, U_ZB + 3, ZB, 6)

            def scan(p):
                wait(lora_read.sem, lora_read.at(l, p + 1))
                op(ts(SG, SG, 0.5, 0.5, ALU.mult, ALU.add))
                dve.tensor_tensor_scan(LIW, cv("inchunk"), SG, 0.0, ALU.mult, ALU.add).then_inc(scan_done.sem, 1)

            def unit_kk(p):
                wait(tv_ready.sem, tv_ready.at(l, p + 1))
                stt(NK, K[:, p, :], pv("k_k", p, p + 1), A[1][:, S:2 * S], ALU.mult, ALU.mult).then_inc(nk_ready.sem, 1)

            def values(p):
                wait(pair_loaded.sem, pair_loaded.at(l, 32 * (p + 1)))
                wait(tv_ready.sem, tv_ready.at(l, p + 1))
                tt(VX, pair_vf[:, :], V[:, p, :], ALU.subtract).then_inc(vf_read.sem, 1)
                wait(vf_read.sem, vf_read.at(l, p + 1))
                op(stt(VX, TV, 1.0, VX, ALU.add, ALU.mult))
                for r in range(2):
                    chain.step(stt(VDUP[:, :, r * CH:(r + 1) * CH], view2(VX, NCH), 0.5, view2(V[:, p, :], NCH),
                                   ALU.mult, ALU.add))

            def keys(p):
                wait(nk_ready.sem, nk_ready.at(l, p + 1))
                op(ts(TA, TA, 0.5, -0.5, ALU.mult, ALU.add))
                op(ts(K2, TA, pv("k_a", p, p + 1), None, ALU.mult))
                chain.step(stt(K2, K2, 1.0, K[:, p, :], ALU.add, ALU.mult))
                chain.settle()
                stt(BKK, TA, 1.0, NK, ALU.add, ALU.mult).then_inc(mid_ready.sem, 1)

            def queries(p):
                wait(decays_ready.sem, decays_ready.at(l, p + 1))
                wait(mid_ready.sem, mid_ready.at(l, p + 1))
                if isinstance(p, int) and p == 0:
                    wait(pads_zero.sem, pads_zero.at(l, 1))
                chain.step(stt(RKK, R[:, p, :], pv("r_k", p, p + 1), K2, ALU.mult, ALU.mult))
                chain.step(dve.tensor_copy(WC[:, (p % 2) * 4:(p % 2) * 4 + 4], Wd[:, CH - 1:S:CH]))
                for h in range(2):
                    a, b = h * HD, (h + 1) * HD
                    chain.step(tt(KR[a:b, p % 2, :, a:b], view2(NK[a:b, :], NCH), view2(LPW[a:b, :], NCH), ALU.mult))
                    chain.step(tt(KR[a:b, p % 2, :, P + a:P + b], view2(R[a:b, p, :], NCH), view2(Wd[a:b, :], NCH),
                                  ALU.mult))
                chain.settle()
                dve.tensor_copy(GNS[:, 20:21], GNS[:, 20:21]).then_inc(ew_dve.sem, 1)

            def attention(i):
                behind(att_granule(i))
                if 4 <= i < HEADS + 3 and i % 2 == 0:
                    tile = (i - 4) // 2
                    wait(pv_done.sem, pv_done.at(l, i - 2))
                    stt(ZB[:, tile, :], A[4 + tile % 2][:, 0:S], 0.5, ZB[:, tile, :],
                        ALU.mult, ALU.mult).then_inc(yb_ready.sem, 1)
                if 2 <= i < HEADS + 2:
                    wait(probs_turned.sem, probs_turned.at(l, i - 1))
                    dve.tensor_copy(PT[:, 512:896], A[3][:, 0:384]).then_inc(pt_dve.sem, 1)
                if i < HEADS:
                    b = i % 2
                    mx, rs, cf = (small[:, o + 6 * b:o + 6 * b + 6] for o in (12, 24, 48))
                    wait(scores_done.sem, scores_done.at(l, i + 1))
                    chain.step(stt(SC0[:, b, :, :], view2(A[0][:, 0:256], 2), SCALE, spread(av("caus0"), 2, P),
                                   ALU.mult, ALU.add))
                    chain.step(stt(SC1[:, b, :, :], view2(A[1][:, :], 2), SCALE, spread(av("caus1"), 2, S),
                                   ALU.mult, ALU.add))
                    chain.step(stt(PC[:, b, :, 0:NCMP], view2(A[0][:, 256:288], 2)[:, :, 0:NCMP], SCALE,
                                   view2(av("cmpmask"), 2), ALU.mult, ALU.add))
                    chain.settle()
                    for n, s in enumerate((SC0[:, b, :, :], SC1[:, b, :, :], PC[:, b, :, 0:NCMP])):
                        chain.step(dve.tensor_reduce(mx[:, 2 * n:2 * n + 2], s, AX.X, ALU.max))
                    chain.settle()
                    ts(mx, mx, -1.0, None, ALU.mult).then_inc(sc_ready.sem, 1)
                split_to(att_granule(i) + LEAD + 1)
                if i < HEADS:
                    wait(exps_done.sem, exps_done.at(l, i + 1))
                    op(dve.reciprocal(rs, rs))
                    tt(cf, rs, gates[:, i, :], ALU.mult).then_inc(cf_ready.sem, 1)
                if i == PRE_POINT:
                    wait(norms_ready.sem, norms_ready.at(l, 1))
                    op(ts(NI, NI, L2_EPS, None, ALU.max))
                    dve.reciprocal(NI, NI).then_inc(inverse_ready.sem, 1)
                    scan(0)
                if i == PRE_POINT + 1:
                    wait(*taken(l, U_K + 8))
                    unit_kk(0)
                    values(0)
                    keys(0)
                    queries(0)

            for u in range(12):
                attention(2 * u)
                behind(QG * (B_K + u) + 3)
                wait(kvr_act.sem, kvr_act.at(l, u + 1))
                for t in range(2):
                    n = 2 * u + t
                    o = KVR[n // 8][:, n % 8, 1:S]
                    ins = stt(o, PB[u % 2][:, t * S:(t + 1) * S - 1], pv("mu", n, n + 1), o, ALU.mult, ALU.add)
                ins.then_inc(unit_free[u % 2].sem, 1)
                attention(2 * u + 1)

            def group_norm(p):
                wait(ysq_ready.sem, ysq_ready.at(l, p + 1))
                op(dve.tensor_reduce(GNS[:, 4:8], view2(V[:, p, :], NCH), AX.X, ALU.add))
                ts(GNS[:, 8:12], GNS[:, 4:8], 1.0 / HD, GN_EPS, ALU.mult, ALU.add).then_inc(var_ready.sem, 1)
                wait(grstd_ready.sem, grstd_ready.at(l, p + 1))
                for h in range(2):
                    a, b = h * HD, (h + 1) * HD
                    ins = tt(Ybd[a:b, :, a:b], view2(K[a:b, p, :], NCH),
                             GNS[a:b, 12:16].rearrange("p (c o) -> p c o", o=1).to_broadcast([HD, NCH, HD]), ALU.mult)
                ins.then_inc(ybd_ready.sem, 1)

            def y_end(p):
                wait(yt_ready.sem, yt_ready.at(l, p + 1))
                op(tt(V[:, p, :], V[:, p, :], R[:, p, :], ALU.add))
                stt(ZA[:, p, :], V[:, p, :], 0.5, ZA[:, p, :], ALU.mult, ALU.mult).then_inc(ya_ready.sem, 1)

            def masked(o, b, mask):
                return tt(o, quad(b), spread(cv(mask), NCH, P), ALU.mult)

            def grow(p, n):
                tt(flat(X), A[4][:, :], flat(X), ALU.add).then_inc(x_step.sem, 1)

            def rwkv_pair(p, k):
                if k in (0, 1, 2, 5, 6, 7, 9, 12, 15, 17, 20, 23, 26):
                    wait(rwkv_step.sem, rwkv_step.at(l, rw_at(p, k)))
                nxt = p + 1 < HP
                wc = WC[:, (p % 2) * 4:(p % 2) * 4 + 4]
                if k == 0:
                    masked(Qd, A[0], "q_blk")
                    masked(QdT, A[1], "qt_blk")
                    masked(QT32, A[1], "qt_32")
                    masked(QT64, A[1], "qt_64").then_inc(q_masked.sem, 1)
                elif k == 1:
                    masked(Mrb, A[2], "incl")
                    masked(Mak, A[3], "strict_x")
                    masked(Mrk, A[4], "incl_x").then_inc(m_masked.sem, 1)
                elif k == 2:
                    dve.tensor_copy(Vst[0:HD, :, :], quad(A[5])[0:HD, :, HD:P])
                    dve.tensor_copy(Vst[HD:P, :, :], quad(A[5])[HD:P, :, 0:HD]).then_inc(v_ready.sem, 1)
                    if p:
                        group_norm(p - 1)
                elif k == 5:
                    wait(x1_ready.sem, x1_ready.at(l, p + 1))
                    grow(p, 0)
                elif k == 6:
                    tt(view2(R[:, p, :], NCH), view2(A[1][:, 0:S], NCH), VDUP[:, :, 0:CH], ALU.mult
                       ).then_inc(bonus_ready.sem, 1)
                elif k == 7:
                    wait(x_step.sem, x_step.at(l, 4 * p + 1))
                    grow(p, 1)
                    if p:
                        y_end(p - 1)
                elif k == 9:
                    wait(x_step.sem, x_step.at(l, 4 * p + 2))
                    grow(p, 2)
                    if nxt:
                        scan(p + 1)
                elif k == 12:
                    wait(x_step.sem, x_step.at(l, 4 * p + 3))
                    grow(p, 3)
                    if nxt:
                        unit_kk(p + 1)
                elif k == 13 and nxt:
                    values(p + 1)
                elif k == 15:
                    wait(x_step.sem, x_step.at(l, 4 * p + 4))
                    stt(flat(TT), A[4][:, :], -1.0, flat(X), ALU.mult, ALU.subtract).then_inc(t_ready.sem, 1)
                    if nxt:
                        keys(p + 1)
                elif k == 17:
                    chain.settle()
                    ts(Z, A[1][:, 256:256 + CH], wc[:, 0:1], None, ALU.mult).then_inc(z_ready.sem, 1)
                    wait(z_ready.sem, z_ready.at(l, 3 * p + 1))
                    chain.step(ts(Zt, Z, wc[:, 1:2], None, ALU.mult))
                elif k == 18 and nxt:
                    queries(p + 1)
                elif k == 20 or k == 23:
                    c = (k - 17) // 3
                    chain.settle()
                    stt(Z, A[1][:, 256 + c * CH:256 + (c + 1) * CH], wc[:, c:c + 1], Zt, ALU.mult, ALU.add
                        ).then_inc(z_ready.sem, 1)
                    if c == 1:
                        wait(z_ready.sem, z_ready.at(l, 3 * p + 2))
                        chain.step(ts(Zt, Z, wc[:, 2:3], None, ALU.mult))
                elif k == 26:
                    y = view2(A[2][:, 0:S], NCH)
                    op(dve.tensor_reduce(GNS[:, 0:4], y, AX.X, ALU.add))
                    op(ts(GNS[:, 0:4], GNS[:, 0:4], 1.0 / HD, None, ALU.mult))
                    tt(view2(K[:, p, :], NCH), y,
                       GNS[:, 0:4].rearrange("p (c o) -> p c o", o=1).to_broadcast([P, NCH, HD]), ALU.subtract
                       ).then_inc(yc_ready.sem, 1)
                    if not nxt:
                        split_to(QG * B_A + 2)
                        group_norm(p)

            def rwkv(i):
                p, at = divmod(i, PAIR_POINTS)
                if SCHEDULE[at] is not None:
                    rwkv_pair(p, SCHEDULE[at])
                if p == YB_PAIR and at in YB_LO_AT:
                    half = YB_LO_AT.index(at)
                    wait(yb_hi_ready.sem, yb_hi_ready.at(l, half + 1))
                    for c in range(4 * half, 4 * half + 4):
                        ins = tt(yb_lo[:, c, :], ZB[:, c, :], yb_hi[c].bitcast(F32), ALU.subtract)
                    ins.then_inc(yb_lo_ready.sem, 1)
                if at in LO_AT:
                    split_to(rw_granule(p * PAIR_POINTS) + LO_AT[at])

            for u in range(4):
                for i in range(16):
                    rwkv(16 * u + i)
                silu(4 + u, U_ZA + u, ZA, 2 * u)
            for u in range(8):
                for i in range(16):
                    rwkv(64 + 16 * u + i)
            for u in range(8):
                for i in range(8):
                    rwkv(192 + 8 * u + i)
                wait(*done(l, U_PB + u))
                for v in (U_MGB + u,):
                    wait(*taken(l, v))
                m = flat(MB[:, 2 * u:2 * u + 2, :])
                stt(m, m, 1.0, PB[u % 2][:, :], ALU.add, ALU.mult).then_inc(unit_free[u % 2].sem, 1)
            behind(QG * B_A + 3)
            y_end(HP - 1)
            wait(ya_ready.sem, ya_ready.at(l, HP))
            for n in range(4):
                t = slice(2 * n, 2 * n + 2)
                wait(ya_hi_ready.sem, ya_hi_ready.at(l, n + 1))
                low(ya_lo[:, t, :], ZA[:, t, :], ya_hi[:, t, :]).then_inc(ya_lo_ready.sem, 1)

            def merged_low(j):
                for n in (2 * j, 2 * j + 1):
                    t = slice(2 * n, 2 * n + 2)
                    wait(merged_hi_ready.sem, merged_hi_ready.at(l, n + 1))
                    low(merged_lo[:, t, :], MB[:, t, :], merged_hi[:, t, :]).then_inc(merged_lo_ready.sem, 1)

            for j in range(4):
                if j:
                    behind(QG * (B_A + 3 * j + 1) + 3)
                    merged_low(j - 1)
                for i in range(2):
                    u = U_A + 4 * j + 2 + i
                    behind(QG * (B_A + 3 * j + 2) + 2 * i + 1)
                    wait(*done(l, u))
                    wait(*taken(l, U_A + 4 * j + i))
                    g = GAB[:, j % 2, i * 512:(i + 1) * 512]
                    m = flat(MB[:, 4 * j + 2 * i:4 * j + 2 * i + 2, :])
                    stt(g, g, 1.0, PB[u % 2][:, :], ALU.add, ALU.mult).then_inc(unit_free[u % 2].sem, 1)
                    wait(*taken(l, u))
                    tt(m, m, g, ALU.add).then_inc(merged_ready.sem, 1)
            behind(QG * (B_A + 11) + 4)
            merged_low(3)
            wait(xr_loaded.sem, xr_loaded.at(l, 48))
            for n in range(4):
                behind(QG * (B_WO + 2 * n) + 7)
                for t in range(2):
                    cols = slice(n * 512, (n + 1) * 512)
                    wait(wo_sq.sem, wo_sq.at(l, 2 * n + t + 1))
                    tt(OUT[:, t, cols], out_banks(n)[t][:, :], GPOST[:, cols], ALU.mult).then_inc(unit_free[t].sem, 1)
            op(dve.tensor_reduce(small[:, 6:8], view2(small[:, 40:48], 2), AX.X, ALU.add))
            ts(small[:, 6:8], small[:, 6:8], 1.0 / D, 4 * NORM_EPS, ALU.mult, ALU.add).then_inc(ms2_ready.sem, 1)
            wait(rstd2_ready.sem, rstd2_ready.at(l, 1))
            wait(*taken(l, U_WO + 6))
            wait(*taken(l, U_WO + 7))
            for t in range(2):
                stt(XR[:, t, :], OUT[:, t, :], small[:, 8 + t:9 + t], XR[:, t, :], ALU.mult, ALU.add
                    ).then_inc(x_new.sem, 1)

        @block.vector
        def _(dve):
            chain = Chain(dve, dve_chain)
            wait = dve.wait_ge

            def op(ins):
                chain.step(ins)
                chain.settle()

            wait(pos_loaded, 16)
            wait(con_loaded, 16)
            posf, ang = (WORK[:, 8192 + i * S:8192 + (i + 1) * S] for i in range(2))
            turns = WORK[:, 8192 + 4 * S:8192 + 6 * S]
            op(dve.tensor_copy(posf, WORK[:, 8192 + 3 * S:8192 + 4 * S].bitcast(I32)))
            op(dve.tensor_scalar(ang, posf, cv("invf"), None, ALU.mult))
            c1 = 6.28125
            c2 = float(np.float32(round((2 * np.pi - c1) * 2 ** 20) / 2 ** 20))
            c3 = float(2 * np.pi - c1 - c2)
            big = 1.5 * 2 ** 23
            both = cs[:, :].rearrange("p (i n) -> p i n", i=2)
            angles = ang.rearrange("p (o n) -> p o n", o=1).to_broadcast([P, 2, S])
            turns2 = turns.rearrange("p (i n) -> p i n", i=2)
            for i, shift in enumerate((0.25, 0.0)):
                chain.step(dve.tensor_scalar(turns[:, i * S:(i + 1) * S], ang, float(1 / (2 * np.pi)), shift,
                                             ALU.mult, ALU.add))
            chain.settle()
            op(dve.tensor_scalar(turns, turns, big, None, ALU.add))
            op(dve.tensor_scalar(turns, turns, big, None, ALU.subtract))
            op(dve.scalar_tensor_tensor(both, turns2, -c1, angles, ALU.mult, ALU.add))
            op(dve.scalar_tensor_tensor(both, turns2, -c2, both, ALU.mult, ALU.add))
            op(dve.scalar_tensor_tensor(both, turns2, -c3, both, ALU.mult, ALU.add))
            op(dve.tensor_scalar(cs[:, 0:S], cs[:, 0:S], float(np.pi / 2), None, ALU.add))
            op(dve.tensor_scalar(both, both, 3.1415925, -3.1415925, ALU.min, ALU.max))
            dve.tensor_copy(turns[:, 0:S], ang).then_inc(sin_arg, 1)
            wait(table_ready, 1)
            wait(zeroed, 1)
            wait(x_loaded, 16)
            chain.restart()
            with dve.Fori(0, LAYERS) as l:
                dve_layer(dve, l, chain)
                chain.restart()

        def pool_layer(pool, l):
            wait = pool.wait_ge

            def view2(ap, n):
                return ap.rearrange("p (t n) -> p t n", t=n)

            wait(par_loaded.sem, par_loaded.at(l, 16))
            pool.tensor_tensor(ha0, pv("a0"), half8[:, :], ALU.mult)
            pool.tensor_scalar(omu, pv("mu"), -1.0, 1.0, ALU.mult, ALU.add)
            pool.tensor_scalar(hw0, pv("w0"), 0.5, None, ALU.mult)
            pool.tensor_scalar(hv0, pv("v0"), 0.5, None, ALU.mult)
            pool.tensor_copy(view2(w2kd[:, :], 2)[:, :, 0:HD], view2(pv("w2k"), 2))
            pool.tensor_copy(view2(w2kd[:, :], 2)[:, :, HD:P], view2(pv("w2k"), 2)).then_inc(derived_ready.sem, 1)
            for t in range(2):
                wait(ms_ready.sem, ms_ready.at(l, t + 1))
                pool.tensor_tensor(small[:, 4 + t:5 + t], small[:, 2 + t:3 + t], halves[:, 0:1], ALU.pow
                                   ).then_inc(rstd_ready.sem, 1)

            for h in range(HEADS):
                b = h % 2
                cf = small[:, 48 + 6 * b:54 + 6 * b]
                wait(cf_ready.sem, cf_ready.at(l, h + 1))
                for n, (s, w) in enumerate(((SC0[:, b, :, :], P), (SC1[:, b, :, :], S), (PC[:, b, :, 0:NCMP], NCMP))):
                    k = cf[:, 2 * n:2 * n + 2].rearrange("p (r o) -> p r o", o=1).to_broadcast([P, 2, w])
                    ins = pool.tensor_tensor(s, s, k, ALU.mult)
                ins.then_inc(probs_ready.sem, 1)

            wait(yb_ready.sem, yb_ready.at(l, HP))
            pool.tensor_tensor(GNS[:, 20:24], halves[:, :], halves[:, :], ALU.subtract)
            for a in (BB, KA, Ybd):
                pool.memset(a, 0.0)
            pool.memset(WORK[:, 0:2048], 0.0)
            pool.memset(GNS[:, 0:20], 0.0).then_inc(pads_zero.sem, 1)
            wait(pads_zero.sem, pads_zero.at(l, 1))

            def before(p):
                wait(scan_done.sem, scan_done.at(l, p + 1))
                pool.tensor_tensor(LPW, LIW, SG, ALU.subtract).then_inc(lp_ready.sem, 1)
                wait(mid_ready.sem, mid_ready.at(l, p + 1))
                wait(decays_ready.sem, decays_ready.at(l, p + 1))
                for h in range(2):
                    a, b = h * HD, (h + 1) * HD
                    pool.tensor_tensor(BB[a:b, :, a:b], view2(BKK[a:b, :], NCH), view2(LIW[a:b, :], NCH), ALU.mult)
                    ins = pool.tensor_tensor(KA[a:b, :, HD - a:P - a], view2(K2[a:b, :], NCH), view2(LIW[a:b, :], NCH),
                                             ALU.mult)
                ins.then_inc(ew_pool.sem, 1)

            def group_rstd(p):
                wait(var_ready.sem, var_ready.at(l, p + 1))
                pool.tensor_tensor(GNS[:, 12:16], GNS[:, 8:12], halves[:, 0:4], ALU.pow).then_inc(grstd_ready.sem, 1)

            before(0)
            for p in range(HP):
                wait(q_masked.sem, q_masked.at(l, p + 1))
                pool.tensor_tensor(X, Qd, spread(cv("ident"), NCH, P), ALU.add).then_inc(x1_ready.sem, 1)
                if p:
                    group_rstd(p - 1)
                if p + 1 < HP:
                    before(p + 1)
            group_rstd(HP - 1)
            wait(ms2_ready.sem, ms2_ready.at(l, 1))
            pool.tensor_tensor(small[:, 8:10], small[:, 6:8], halves[:, 0:2], ALU.pow).then_inc(rstd2_ready.sem, 1)

        @block.gpsimd
        def _(pool):
            pool.memset(v_cmp[:, :], 0.0)
            pool.memset(PC, 0.0)
            pool.memset(small[:, :], 0.0)
            pool.memset(half8[:, :], 0.5)
            pool.memset(halves[:, :], -0.5).then_inc(zeroed, 1)
            pool.wait_ge(zeroed, 1)
            with pool.Fori(0, LAYERS) as l:
                pool_layer(pool, l)


def chunked(w):
    n = w.shape[0] // P
    return np.ascontiguousarray(w.reshape(n, P, -1).transpose(1, 0, 2)).reshape(P, -1)


def weight_stream(w_in, ck_w1, cv_w1, w_a, w_b, w_o):
    shift = 3 * RW + 2 * LORA_W
    za, q = shift, shift + RW
    kv = q + RW
    gate = kv + 6 * NG * HD
    zb = gate + 3 * HEADS
    mg = zb + RW
    tiled = lambda w: np.concatenate([chunked(w[:, i:i + P]) for i in range(0, w.shape[1], P)], 1)
    col = lambda a, n=256: tiled(w_in[:, a:a + n])
    log = np.zeros((D, 256), np.float32)
    log[:, 0:2 * LORA_W] = w_in[:, 3 * RW:shift]
    log[:, 192:240] = w_in[:, gate:gate + 48]
    vt = np.concatenate([w_in[:, kv + 768:kv + 1024], w_in[:, kv + 1280:kv + 1536]], 1)
    blocks = [chunked(log), col(kv), col(kv + 256), col(kv + 512), col(kv + 1024), chunked(vt[0:1024]),
              chunked(vt[1024:])]
    blocks += [col(q + 256 * i) for i in range(4)]
    blocks += [chunked(ck_w1), chunked(cv_w1)]
    blocks += [col(zb + 256 * i) for i in range(4)]
    for a in (RW, 2 * RW, 0):
        blocks += [col(a + 256 * i) for i in range(4)]
    blocks += [col(za + 256 * i) for i in range(4)]
    blocks += [col(mg + D + 256 * i) for i in range(8)]
    blocks += [tiled(w_b[:, 512 * i:512 * (i + 1)]) for i in range(4)]
    for j in range(4):
        blocks += [col(mg + 512 * j), col(mg + 512 * j + 256), tiled(w_a[:, 512 * j:512 * (j + 1)])]
    blocks += [chunked(w_o[1024 * kh:1024 * (kh + 1), 512 * n:512 * (n + 1)]) for n in range(4) for kh in range(2)]
    assert len(blocks) == NB and all(b.shape == (P, QG * GR) for b in blocks)
    return np.ascontiguousarray(np.stack(blocks).reshape(NB, P, QG, GR).transpose(0, 2, 1, 3)).reshape(NGR, P, GR)


def pair_ups(a, l):
    t = np.zeros((HP, P, 3, P), np.float32)
    for i, w in enumerate((a["rwkv_w_up"][l], a["rwkv_a_up"][l], a["rwkv_v_up"][max(l - 1, 0)])):
        t[:, 0:w.shape[0], i, :] = w.reshape(-1, HP, P).transpose(1, 0, 2)
    for h in range(HEADS):
        t[h // 2, LORA_V + h, 2, h % 2 * HD:(h % 2 + 1) * HD] = 1.0
    return t.reshape(HP, P, 3 * P)


def param_tile(a, l):
    t = np.zeros((P, NPAR), np.float32)

    def put(name, v):
        lo, hi = PAR[name]
        t[0:v.shape[0], lo:hi] = v

    v = max(l - 1, 0)
    cols = lambda w: w.reshape(-1, P).T
    mu = a["rwkv_mu"][l]
    put("v_down", chunked(a["rwkv_v_down"][v]))
    put("w2k", chunked(a["nsa_ck_w2"][l]))
    put("w2v", chunked(a["nsa_cv_w2"][l]))
    m = np.zeros((P, 26), np.float32)
    m[:, 0:24] = np.concatenate([cols(mu[RW:2 * RW]), cols(mu[2 * RW:3 * RW]), cols(mu[0:RW])], 1)
    m[0:LORA_W, 24] = mu[3 * RW:3 * RW + LORA_W]
    m[0:LORA_W, 25] = mu[3 * RW + LORA_W:]
    put("mu", m)
    for name in ("w0", "a0", "k_k", "k_a", "gn_w", "gn_b"):
        put(name, cols(a["rwkv_" + name][l]))
    put("v0", cols(a["rwkv_v0"][v]))
    put("r_k", cols(a["rwkv_r_k"][l].reshape(-1)))
    put("norm_pre", cols(a["norm_pre"][l]))
    put("pe_k", cols(a["nsa_pe_k"][l].reshape(-1)))
    put("pe_v", cols(a["nsa_pe_v"][l].reshape(-1)))
    return t


def constant_tiles():
    t, att = np.zeros((P, NCON), np.float32), np.zeros((P, NATT), np.float32)

    def put(name, v):
        lo, hi = CON[name] if name in CON else ATT[name]
        (t if name in CON else att)[0:v.shape[0], lo:hi] = v

    i = np.arange(P)
    put("ident", np.eye(P))
    r, c = i[:, None], i[None, :]
    same = lambda n: r // n == c // n
    put("q_blk", -1.0 * (same(16) & (r < c)))
    put("qt_blk", -1.0 * (same(16) & (r > c)))
    put("qt_32", -1.0 * (same(32) & ~same(16) & (r > c)))
    put("qt_64", -1.0 * (same(64) & ~same(32) & (r > c)))
    rr, cc = r % CH, c % CH
    put("incl", 1.0 * (same(64) & (rr <= cc)))
    put("strict_x", 1.0 * (~same(64) & (rr < cc)))
    put("incl_x", 1.0 * (~same(64) & (rr <= cc)))
    put("ones", 1.0 * same(64))
    for h in range(2):
        t[h * HD:(h + 1) * HD, CON["headcol"][0] + 14 + h] = 1.0
    put("ident2", 1.0 * (i[:, None] % CH == np.arange(CH)[None, :]))
    rot = np.zeros((P, P))
    half = HD // 8
    for h in range(2):
        for m in range(half):
            rot[h * HD + m + half, h * HD + m] = -1.0
            rot[h * HD + m, h * HD + m + half] = 1.0
    put("rot", rot)
    dup = []
    for gg in range(2):
        d = np.zeros((P, P))
        for m in range(P):
            d[gg * HD + m % HD, m] = 1.0
        dup += [d, d @ rot]
    put("dup", np.concatenate(dup, 1))
    k = np.arange(S)[None, :]
    put("caus0", np.where(k[:, :P] > i[:, None], -1e30, 0.0))
    put("caus1", np.where(k > P + i[:, None], -1e30, 0.0))
    end = np.arange(NCMP)[None, :] * CSTR + CMP - 1
    put("cmpmask", np.concatenate([np.where(end <= t0 + i[:, None], 0.0, -1e30) for t0 in (0, P)], 1))
    put("rowok", 1.0 * (i[:, None] >= CMP - 1))
    inv = np.float32(500000.0) ** (-np.arange(half, dtype=np.float32) * np.float32(2.0 / (HD // 4)))
    f = np.zeros((P, 1), np.float32)
    for h in range(2):
        f[h * HD:h * HD + half, 0] = inv
        f[h * HD + half:h * HD + 2 * half, 0] = inv
    put("invf", f)
    put("inchunk", 1.0 * np.broadcast_to(k % CH != 0, (P, S)))
    return t, att


def kernel(**inputs):
    import concourse.bacc as bacc
    from concourse.bass_utils import run_bass_kernel_spmd as run

    a = {n: np.asarray(v) for n, v in inputs.items()}
    con, att = constant_tiles()
    arrays = {
        "in_x": np.ascontiguousarray(a["x"]),
        "in_positions": np.ascontiguousarray(a["positions"]),
        "in_stream": np.concatenate([weight_stream(a["w_in"][l], a["nsa_ck_w1"][l], a["nsa_cv_w1"][l],
                                                   a["w_proj_a"][l], a["w_proj_b"][l], a["w_out"][l])
                                     for l in range(LAYERS)]),
        "in_params": np.stack([param_tile(a, min(l, LAYERS - 1)) for l in range(LAYERS + 1)]),
        "in_pair_ups": np.concatenate([pair_ups(a, l) for l in range(LAYERS)]),
        "in_constants": con,
        "in_attention_constants": att,
        "in_norm_post": np.ascontiguousarray(a["norm_post"]),
    }
    nc = bacc.Bacc("TRN2", target_bir_lowering=False, num_devices=1)
    args = [nc.dram_tensor(n, v.shape, mybir.dt.from_np(v.dtype), kind="ExternalInput").ap()
            for n, v in arrays.items()]
    out = nc.dram_tensor("out_x", (1, S, D), F32, kind="ExternalOutput").ap()
    v_first = nc.dram_tensor("v_by_layer", (LAYERS, P, HP * S), F32, kind="Internal").ap()
    build(nc, *args, v_first, out)
    return run(nc, [arrays], core_ids=[0]).results[0]["out_x"]
```
